# Optimizing a Trainium2 kernel written in Bass

```python
import jax, jax.numpy as jnp
from jax import lax
import numpy as np

D_MODEL = 1024
BATCH = 1
SEQ = 512
DEPTH = 1

D_MIX = D_MODEL
D_ATTN = D_MIX // 2
D_LRU = D_MIX - D_ATTN
HEAD_DIM = 64
N_ATTN_HEADS = D_ATTN // HEAD_DIM
N_LRU_BLOCKS = 8
LRU_BLOCK = D_LRU // N_LRU_BLOCKS
CONV_WIDTH = 4
LRU_C = 8.0
Q_BLOCK = 128
N_GROUPS = 4
EXPERTS_PER_GROUP = 4
N_EXPERTS = N_GROUPS * EXPERTS_PER_GROUP
TOP_K_IN_GROUP = 2
D_EXPERT = D_MODEL // 2
LN_EPS = 1e-5
RMS_EPS = 1e-6
NEG_INF = -1e30
DEEPNORM_ALPHA = (2.0 * DEPTH) ** 0.25
DEEPNORM_BETA = (8.0 * DEPTH) ** -0.25
D_IN = 3 * D_ATTN + N_ATTN_HEADS + 2 * D_LRU


def layer_norm(x, gain=None, bias=None):
    xf = x.astype(jnp.float32)
    mu = jnp.mean(xf, axis=-1, keepdims=True)
    var = jnp.mean(jnp.square(xf - mu), axis=-1, keepdims=True)
    y = (xf - mu) * lax.rsqrt(var + LN_EPS)
    if gain is not None:
        y = y * gain.astype(jnp.float32) + bias.astype(jnp.float32)
    return y.astype(x.dtype)

def rms_norm(x, gain):
    xf = x.astype(jnp.float32)
    y = xf * lax.rsqrt(jnp.mean(jnp.square(xf), axis=-1, keepdims=True) + RMS_EPS)
    return (y * gain.astype(jnp.float32)).astype(x.dtype)

def forgetting_attention(q, k, v, f_logit):
    b, s, h, dh = q.shape
    cum = jnp.cumsum(jax.nn.log_sigmoid(f_logit.astype(jnp.float32)), axis=1)
    cum = jnp.transpose(cum, (0, 2, 1))
    q = jnp.transpose(q, (0, 2, 1, 3)) * (dh ** -0.5)
    k = jnp.transpose(k, (0, 2, 1, 3))
    v = jnp.transpose(v, (0, 2, 1, 3))
    outs = []
    for i in range(s // Q_BLOCK):
        q0 = i * Q_BLOCK
        kend = q0 + Q_BLOCK
        qb = q[:, :, q0:kend]
        kb = k[:, :, :kend]
        vb = v[:, :, :kend]
        logits = jnp.einsum('bhqd,bhkd->bhqk', qb, kb).astype(jnp.float32)
        logits = logits + (cum[:, :, q0:kend, None] - cum[:, :, None, :kend])
        causal = jnp.arange(kend)[None, :] <= (q0 + jnp.arange(Q_BLOCK))[:, None]
        logits = jnp.where(causal, logits, NEG_INF)
        p = jax.nn.softmax(logits, axis=-1).astype(v.dtype)
        outs.append(jnp.einsum('bhqk,bhkd->bhqd', p, vb))
    o = jnp.concatenate(outs, axis=2)
    return jnp.transpose(o, (0, 2, 1, 3)).reshape(b, s, h * dh)

def rg_lru_branch(xb, gb, conv_w, conv_b, w_rg, b_rg, w_ig, b_ig, lru_lambda):
    b, s, _ = xb.shape
    xc = lax.conv_general_dilated(
        xb, conv_w[:, None, :].astype(xb.dtype), window_strides=(1,),
        padding=((CONV_WIDTH - 1, 0),), dimension_numbers=('NWC', 'WIO', 'NWC'),
        feature_group_count=D_LRU) + conv_b
    xr = xc.reshape(b, s, N_LRU_BLOCKS, LRU_BLOCK)
    r = jax.nn.sigmoid(jnp.einsum('bsni,nij->bsnj', xr, w_rg).reshape(b, s, D_LRU) + b_rg)
    ig = jax.nn.sigmoid(jnp.einsum('bsni,nij->bsnj', xr, w_ig).reshape(b, s, D_LRU) + b_ig)
    log_a = -LRU_C * r.astype(jnp.float32) * jax.nn.softplus(-lru_lambda.astype(jnp.float32))
    a = jnp.exp(log_a)
    u = jnp.sqrt(-jnp.expm1(2.0 * log_a)) * (ig * xc).astype(jnp.float32)

    def combine(e1, e2):
        a1, b1 = e1
        a2, b2 = e2
        return a1 * a2, a2 * b1 + b2

    _, hs = lax.associative_scan(combine, (a, u), axis=1)
    return hs.astype(xb.dtype) * jax.nn.gelu(gb)

def hybrid_mixer(u, w_in, b_f, conv_w, conv_b, w_rg, b_rg, w_ig, b_ig, lru_lambda,
                 g_attn, g_lru, w_out):
    b, s, _ = u.shape
    proj = jnp.einsum('bsd,de->bse', u, w_in)
    q, k, v, f_logit, xb, gb = jnp.split(
        proj, [D_ATTN, 2 * D_ATTN, 3 * D_ATTN, 3 * D_ATTN + N_ATTN_HEADS,
               3 * D_ATTN + N_ATTN_HEADS + D_LRU], axis=-1)
    hs = (b, s, N_ATTN_HEADS, HEAD_DIM)
    attn = forgetting_attention(q.reshape(hs), k.reshape(hs), v.reshape(hs), f_logit + b_f)
    lru = rg_lru_branch(xb, gb, conv_w, conv_b, w_rg, b_rg, w_ig, b_ig, lru_lambda)
    mixed = jnp.concatenate([rms_norm(attn, g_attn), rms_norm(lru, g_lru)], axis=-1)
    return jnp.einsum('bse,ed->bsd', mixed, w_out)

def hierarchical_moe(u, w_grp, b_grp, w_exp, b_exp, w_e_gate, w_e_up, w_e_down):
    b, s, d = u.shape
    t = u.reshape(b * s, d)
    grp_prob = jax.nn.softmax((t @ w_grp + b_grp).astype(jnp.float32), axis=-1)
    grp_w, grp_idx = lax.top_k(grp_prob, 1)
    exp_logits = (t @ w_exp + b_exp).astype(jnp.float32).reshape(-1, N_GROUPS, EXPERTS_PER_GROUP)
    sel_logits = jnp.take_along_axis(exp_logits, grp_idx[:, :, None], axis=1)[:, 0]
    top_w, top_idx = lax.top_k(jax.nn.softmax(sel_logits, axis=-1), TOP_K_IN_GROUP)
    top_w = top_w / jnp.sum(top_w, axis=-1, keepdims=True) * grp_w
    expert_id = grp_idx * EXPERTS_PER_GROUP + top_idx
    comb = jnp.sum(jax.nn.one_hot(expert_id, N_EXPERTS, dtype=jnp.float32)
                   * top_w[..., None], axis=1).astype(t.dtype)
    y = jnp.zeros_like(t)
    for e in range(N_EXPERTS):
        h = jax.nn.silu(t @ w_e_gate[e]) * (t @ w_e_up[e])
        y = y + comb[:, e:e + 1] * (h @ w_e_down[e])
    return y.reshape(b, s, d)

def first_inputs(seed: int = 0) -> dict:
    key = jax.random.key(seed)
    ks = jax.random.split(key, 28)
    nrm = jax.random.normal
    L = DEPTH
    x = nrm(ks[0], (BATCH, SEQ, D_MODEL), jnp.float32)
    c = nrm(ks[1], (BATCH, D_MODEL), jnp.float32)
    w_ada = nrm(ks[2], (L, D_MODEL, 6 * D_MODEL)) * (0.1 * D_MODEL ** -0.5)
    b_ada = nrm(ks[3], (L, 6 * D_MODEL)) * 0.01
    w_in = nrm(ks[4], (L, D_MODEL, D_IN)) * D_MODEL ** -0.5
    w_in = w_in.at[..., 2 * D_ATTN:3 * D_ATTN].multiply(DEEPNORM_BETA)
    b_f = jax.random.uniform(ks[5], (L, N_ATTN_HEADS), minval=1.0, maxval=6.0)
    conv_w = nrm(ks[6], (L, CONV_WIDTH, D_LRU)) * CONV_WIDTH ** -0.5
    conv_b = nrm(ks[7], (L, D_LRU)) * 0.01
    w_rg = nrm(ks[8], (L, N_LRU_BLOCKS, LRU_BLOCK, LRU_BLOCK)) * LRU_BLOCK ** -0.5
    b_rg = nrm(ks[9], (L, D_LRU)) * 0.01
    w_ig = nrm(ks[10], (L, N_LRU_BLOCKS, LRU_BLOCK, LRU_BLOCK)) * LRU_BLOCK ** -0.5
    b_ig = nrm(ks[11], (L, D_LRU)) * 0.01
    a_c = jax.random.uniform(ks[12], (L, D_LRU), minval=0.9, maxval=0.999)
    a0 = a_c ** (1.0 / LRU_C)
    lru_lambda = jnp.log(a0) - jnp.log1p(-a0)
    g_attn = 1.0 + 0.02 * nrm(ks[13], (L, D_ATTN))
    g_lru = 1.0 + 0.02 * nrm(ks[14], (L, D_LRU))
    w_out = nrm(ks[15], (L, D_MIX, D_MODEL)) * (D_MIX ** -0.5 * DEEPNORM_BETA)
    ln1_g = 1.0 + 0.02 * nrm(ks[16], (L, D_MODEL))
    ln1_b = 0.01 * nrm(ks[17], (L, D_MODEL))
    w_grp = nrm(ks[18], (L, D_MODEL, N_GROUPS)) * D_MODEL ** -0.5
    b_grp = 0.01 * nrm(ks[19], (L, N_GROUPS))
    w_exp = nrm(ks[20], (L, D_MODEL, N_EXPERTS)) * D_MODEL ** -0.5
    b_exp = 0.01 * nrm(ks[21], (L, N_EXPERTS))
    w_e_gate = nrm(ks[22], (L, N_EXPERTS, D_MODEL, D_EXPERT)) * D_MODEL ** -0.5
    w_e_up = nrm(ks[23], (L, N_EXPERTS, D_MODEL, D_EXPERT)) * D_MODEL ** -0.5
    w_e_down = nrm(ks[24], (L, N_EXPERTS, D_EXPERT, D_MODEL)) * (D_EXPERT ** -0.5 * DEEPNORM_BETA)
    ln2_g = 1.0 + 0.02 * nrm(ks[25], (L, D_MODEL))
    ln2_b = 0.01 * nrm(ks[26], (L, D_MODEL))
    return {"x": x, "c": c, "w_ada": w_ada, "b_ada": b_ada, "w_in": w_in, "b_f": b_f,
            "conv_w": conv_w, "conv_b": conv_b, "w_rg": w_rg, "b_rg": b_rg,
            "w_ig": w_ig, "b_ig": b_ig, "lru_lambda": lru_lambda, "g_attn": g_attn,
            "g_lru": g_lru, "w_out": w_out, "ln1_g": ln1_g, "ln1_b": ln1_b,
            "w_grp": w_grp, "b_grp": b_grp, "w_exp": w_exp, "b_exp": b_exp,
            "w_e_gate": w_e_gate, "w_e_up": w_e_up, "w_e_down": w_e_down,
            "ln2_g": ln2_g, "ln2_b": ln2_b}

def first_block(x, c, w_ada, b_ada, w_in, b_f, conv_w, conv_b, w_rg, b_rg, w_ig, b_ig,
              lru_lambda, g_attn, g_lru, w_out, ln1_g, ln1_b, w_grp, b_grp, w_exp, b_exp,
              w_e_gate, w_e_up, w_e_down, ln2_g, ln2_b):
    for l in range(DEPTH):
        mod = jnp.einsum('bd,de->be', jax.nn.silu(c), w_ada[l]) + b_ada[l]
        sh_m, sc_m, gt_m, sh_f, sc_f, gt_f = jnp.split(mod[:, None, :], 6, axis=-1)
        u = layer_norm(x) * (1.0 + sc_m) + sh_m
        mix = hybrid_mixer(u, w_in[l], b_f[l], conv_w[l], conv_b[l], w_rg[l], b_rg[l],
                           w_ig[l], b_ig[l], lru_lambda[l], g_attn[l], g_lru[l], w_out[l])
        x = layer_norm(DEEPNORM_ALPHA * x + (1.0 + gt_m) * mix, ln1_g[l], ln1_b[l])
        u = layer_norm(x) * (1.0 + sc_f) + sh_f
        ffn = hierarchical_moe(u, w_grp[l], b_grp[l], w_exp[l], b_exp[l],
                               w_e_gate[l], w_e_up[l], w_e_down[l])
        x = layer_norm(DEEPNORM_ALPHA * x + (1.0 + gt_f) * ffn, ln2_g[l], ln2_b[l])
    return x


_first_inputs = first_inputs


def first_inputs(seed=0):
    import zlib

    import numpy as np

    out = dict(_first_inputs(seed))
    spreads = {}
    factors = {'b_rg': 27.36,
     'b_ig': 21.893,
     'g_attn': 17.81,
     'g_lru': 18.723,
     'ln1_b': 4.183,
     'b_grp': 28.587,
     'b_exp': 27.455,
     'ln2_g': 7.778,
     'ln2_b': 15.654}
    for name, (base, spread) in spreads.items():
        noise = np.random.default_rng([zlib.crc32(name.encode()), seed]).standard_normal(out[name].shape)
        drawn = base * np.exp(spread * noise) if base else spread * noise
        out[name] = __import__('jax').numpy.asarray(drawn.astype(out[name].dtype))
    for name, factor in factors.items():
        out[name] = (out[name] * factor).astype(out[name].dtype)
    return out


_narrow_inputs = first_inputs


def first_inputs(seed=0):
    out = dict(_narrow_inputs(seed))
    wider = {'g_attn': 4.17, 'g_lru': 4.14, 'ln2_g': 3.13, 'ln2_b': 3.13}
    for name, times in wider.items():
        mean = out[name].mean()
        out[name] = (mean + times * (out[name] - mean)).astype(out[name].dtype)
    return out


GRID_W = 64
CTX_LEN = 256
NA_HEADS = 8
NA_WIN_R = 8
NA_WIN_C = 16
GQA_HEADS = 8
GQA_KV_HEADS = 2
ROPE_THETA = 10000.0
N_EXPERTS_2 = 32
TOP_K = 4
D_FF = D_MODEL
SWIGLU_LIMIT = 7.0
SWIGLU_ALPHA = 1.702
EXPERT_BLOCK = 128
NORM_EPS = 1e-6

NA_WIDTH = NA_HEADS * HEAD_DIM
GQA_WIDTH = GQA_HEADS * HEAD_DIM
GQA_KV_WIDTH = GQA_KV_HEADS * HEAD_DIM
IN_SPLITS = (NA_WIDTH, NA_WIDTH, GQA_KV_WIDTH, GQA_KV_WIDTH, NA_WIDTH, GQA_WIDTH, D_MODEL, D_MODEL)
KV_COLS = 2 * NA_WIDTH + 2 * GQA_KV_WIDTH
IN_COLS = sum(IN_SPLITS)


def rmsnorm(x, g):
    xf = x.astype(jnp.float32)
    y = xf * lax.rsqrt(jnp.mean(xf * xf, axis=-1, keepdims=True) + NORM_EPS)
    return (y * g.astype(jnp.float32)).astype(x.dtype)

def split_cols(p, sizes):
    return jnp.split(p, np.cumsum(sizes)[:-1].tolist(), axis=-1)

def to_heads(t, n):
    return t.reshape(t.shape[0], t.shape[1], n, HEAD_DIM)

def axial_rope(x, row, col):
    half = HEAD_DIM // 2
    nf = half // 2
    freqs = ROPE_THETA ** (-jnp.arange(nf, dtype=jnp.float32) / nf)

    def rot(xp, pos):
        ang = pos.astype(jnp.float32)[:, None] * freqs
        cos = jnp.cos(ang)[None, :, None, :]
        sin = jnp.sin(ang)[None, :, None, :]
        x1 = xp[..., :nf].astype(jnp.float32)
        x2 = xp[..., nf:].astype(jnp.float32)
        return jnp.concatenate([x1 * cos - x2 * sin, x2 * cos + x1 * sin], axis=-1)

    return jnp.concatenate([rot(x[..., :half], row), rot(x[..., half:], col)], axis=-1).astype(x.dtype)

def gqa_attend(q, k, v):
    s = jnp.einsum('btkgd,bskd->bkgts', q, k)
    p = jax.nn.softmax(s.astype(jnp.float32), axis=-1).astype(q.dtype)
    return jnp.einsum('bkgts,bskd->btkgd', p, v)

def blocked_gqa(q, k, v):
    B, S = q.shape[0], q.shape[1]
    nb = S // Q_BLOCK
    qb = q.reshape(B, nb, Q_BLOCK, *q.shape[2:]).swapaxes(0, 1)
    out = lax.map(lambda blk: gqa_attend(blk, k, v), qb)
    return out.swapaxes(0, 1).reshape(B, S, -1)

def neighbourhood_attention(q, k, v, k_ctx, v_ctx, rpb):
    B, S, H, Dh = q.shape
    rows = S // GRID_W
    kr = min(NA_WIN_R, rows)
    kc = min(NA_WIN_C, GRID_W)
    qg = q.reshape(B, rows, GRID_W, H, Dh)
    kg = k.reshape(B, rows, GRID_W, H, Dh)
    vg = v.reshape(B, rows, GRID_W, H, Dh)
    cols = np.arange(GRID_W)
    c0 = np.clip(cols - kc // 2, 0, GRID_W - kc)
    col_idx = (c0[:, None] + np.arange(kc)[None, :]).astype(np.int32)
    col_off = (col_idx - cols[:, None] + (NA_WIN_C - 1)).astype(np.int32)

    def row_block(r):
        r0 = jnp.clip(r - kr // 2, 0, rows - kr)
        q_r = lax.dynamic_index_in_dim(qg, r, axis=1, keepdims=False)
        k_nb = lax.dynamic_slice_in_dim(kg, r0, kr, axis=1)[:, :, col_idx]
        v_nb = lax.dynamic_slice_in_dim(vg, r0, kr, axis=1)[:, :, col_idx]
        row_off = r0 + jnp.arange(kr, dtype=jnp.int32) - r + (NA_WIN_R - 1)
        bias = rpb[:, row_off[:, None, None], col_off[None, :, :]].transpose(0, 2, 1, 3)
        s_loc = jnp.einsum('bwhd,brwchd->bhwrc', q_r, k_nb) + bias.astype(q.dtype)
        s_ctx = jnp.einsum('bwhd,bnhd->bhwn', q_r, k_ctx)
        s = jnp.concatenate([s_loc.reshape(B, H, GRID_W, kr * kc), s_ctx], axis=-1)
        p = jax.nn.softmax(s.astype(jnp.float32), axis=-1).astype(q.dtype)
        p_loc = p[..., :kr * kc].reshape(B, H, GRID_W, kr, kc)
        p_ctx = p[..., kr * kc:]
        return (jnp.einsum('bhwrc,brwchd->bwhd', p_loc, v_nb)
                + jnp.einsum('bhwn,bnhd->bwhd', p_ctx, v_ctx))

    out = lax.map(row_block, jnp.arange(rows, dtype=jnp.int32))
    return out.transpose(1, 0, 2, 3, 4).reshape(B, S, H * Dh)

def merge_branches(o_a, o_b, g_a, g_b, w_out_a, w_out_b, w_o):
    return (jax.nn.sigmoid(g_a) * (o_a @ w_out_a) + jax.nn.sigmoid(g_b) * (o_b @ w_out_b)) @ w_o

def hybrid_mixer_2(h, h_ctx, w_in, rpb, g_qn, g_kn, w_out_a, w_out_b, w_o, row, col, update_ctx):
    B, S, _ = h.shape
    C = h_ctx.shape[1]
    scale = HEAD_DIM ** -0.5
    G = GQA_HEADS // GQA_KV_HEADS
    k_a, v_a, k_b, v_b, q_a, q_b, g_a, g_b = split_cols(h @ w_in, IN_SPLITS)
    if update_ctx:
        parts = split_cols(h_ctx @ w_in, IN_SPLITS)
    else:
        parts = split_cols(h_ctx @ w_in[:, :KV_COLS], IN_SPLITS[:4])
    k_ca = to_heads(parts[0], NA_HEADS)
    v_ca = to_heads(parts[1], NA_HEADS)
    k_cb = rmsnorm(to_heads(parts[2], GQA_KV_HEADS), g_kn)
    v_cb = to_heads(parts[3], GQA_KV_HEADS)

    o_a = neighbourhood_attention(to_heads(q_a, NA_HEADS) * scale, to_heads(k_a, NA_HEADS),
                                  to_heads(v_a, NA_HEADS), k_ca, v_ca, rpb)
    qb = axial_rope(rmsnorm(to_heads(q_b, GQA_HEADS), g_qn), row, col) * scale
    kb = axial_rope(rmsnorm(to_heads(k_b, GQA_KV_HEADS), g_kn), row, col)
    k_all = jnp.concatenate([kb, k_cb], axis=1)
    v_all = jnp.concatenate([to_heads(v_b, GQA_KV_HEADS), v_cb], axis=1)
    o_b = blocked_gqa(qb.reshape(B, S, GQA_KV_HEADS, G, HEAD_DIM), k_all, v_all)
    y = merge_branches(o_a, o_b, g_a, g_b, w_out_a, w_out_b, w_o)

    y_ctx = None
    if update_ctx:
        q_ca, q_cb, g_ca, g_cb = parts[4:]
        o_ca = gqa_attend(to_heads(q_ca, NA_HEADS)[:, :, :, None, :] * scale, k_ca, v_ca).reshape(B, C, -1)
        qcb = rmsnorm(to_heads(q_cb, GQA_HEADS), g_qn) * scale
        o_cb = gqa_attend(qcb.reshape(B, C, GQA_KV_HEADS, G, HEAD_DIM), k_cb, v_cb).reshape(B, C, -1)
        y_ctx = merge_branches(o_ca, o_cb, g_ca, g_cb, w_out_a, w_out_b, w_o)
    return y, y_ctx

def moe_ffn(h, w_router, b_router, w_gu, b_gu, w_dn, b_dn):
    T, D = h.shape
    logits = (h @ w_router + b_router).astype(jnp.float32)
    top_logits, top_e = lax.top_k(logits, TOP_K)
    top_w = jax.nn.softmax(top_logits, axis=-1).astype(h.dtype)
    n_assign = T * TOP_K
    flat_e = top_e.reshape(-1)
    flat_tok = jnp.arange(n_assign, dtype=jnp.int32) // TOP_K
    order = jnp.argsort(flat_e)
    e_sorted = flat_e[order]
    counts = jnp.bincount(flat_e, length=N_EXPERTS_2)
    padded = (counts + EXPERT_BLOCK - 1) // EXPERT_BLOCK * EXPERT_BLOCK
    pad_end = jnp.cumsum(padded)
    pad_start = pad_end - padded
    start = jnp.cumsum(counts) - counts
    dest = pad_start[e_sorted] + jnp.arange(n_assign, dtype=jnp.int32) - start[e_sorted]
    n_blocks = -(-n_assign // EXPERT_BLOCK) + N_EXPERTS_2
    n_slots = n_blocks * EXPERT_BLOCK
    slot_tok = jnp.full((n_slots,), T, dtype=jnp.int32).at[dest].set(flat_tok[order])
    slot_w = jnp.zeros((n_slots,), h.dtype).at[dest].set(top_w.reshape(-1)[order])
    block_e = jnp.minimum(jnp.searchsorted(pad_end, jnp.arange(n_blocks, dtype=jnp.int32) * EXPERT_BLOCK,
                                           side='right'), N_EXPERTS_2 - 1)
    h_pad = jnp.concatenate([h, jnp.zeros((1, D), h.dtype)], axis=0)
    xb = h_pad[slot_tok].reshape(n_blocks, EXPERT_BLOCK, D)

    def expert_block(args):
        xe, e = args
        gu = xe @ w_gu[e] + b_gu[e]
        x_glu = jnp.minimum(gu[:, :D_FF], SWIGLU_LIMIT)
        x_lin = jnp.clip(gu[:, D_FF:], -SWIGLU_LIMIT, SWIGLU_LIMIT)
        act = (x_lin + 1) * (x_glu * jax.nn.sigmoid(SWIGLU_ALPHA * x_glu))
        return act @ w_dn[e] + b_dn[e]

    yb = lax.map(expert_block, (xb, block_e))
    y = jnp.zeros((T + 1, D), h.dtype).at[slot_tok].add(yb.reshape(n_slots, D) * slot_w[:, None])
    return y[:T]

def second_inputs(seed: int = 0) -> dict:
    key = jax.random.key(seed)
    ks = jax.random.split(key, 23)
    f32 = jnp.float32
    L = DEPTH

    def nrm(k, shape, s):
        return jax.random.normal(k, shape, f32) * s

    def gain(k, shape):
        return 1.0 + 0.05 * jax.random.normal(k, shape, f32)

    return {
        'x': nrm(ks[0], (BATCH, SEQ, D_MODEL), 1.0),
        'c': nrm(ks[1], (BATCH, D_MODEL), 1.0),
        'ctx': nrm(ks[2], (BATCH, CTX_LEN, D_MODEL), 1.0),
        'c_ctx': nrm(ks[3], (D_MODEL,), 1.0),
        'w_mod': nrm(ks[4], (L, D_MODEL, 6 * D_MODEL), 0.5 * D_MODEL ** -0.5),
        'b_mod': nrm(ks[5], (L, 6 * D_MODEL), 0.02),
        'g_pre_mix': gain(ks[6], (L, D_MODEL)),
        'g_post_mix': gain(ks[7], (L, D_MODEL)),
        'g_pre_ffn': gain(ks[8], (L, D_MODEL)),
        'g_post_ffn': gain(ks[9], (L, D_MODEL)),
        'w_in': nrm(ks[10], (L, D_MODEL, IN_COLS), D_MODEL ** -0.5),
        'rpb': nrm(ks[11], (L, NA_HEADS, 2 * NA_WIN_R - 1, 2 * NA_WIN_C - 1), 0.1),
        'g_qnorm': gain(ks[12], (L, HEAD_DIM)),
        'g_knorm': gain(ks[13], (L, HEAD_DIM)),
        'w_out_a': nrm(ks[14], (L, NA_WIDTH, D_MODEL), NA_WIDTH ** -0.5),
        'w_out_b': nrm(ks[15], (L, GQA_WIDTH, D_MODEL), GQA_WIDTH ** -0.5),
        'w_o': nrm(ks[16], (L, D_MODEL, D_MODEL), D_MODEL ** -0.5),
        'w_router': nrm(ks[17], (L, D_MODEL, N_EXPERTS_2), D_MODEL ** -0.5),
        'b_router': nrm(ks[18], (L, N_EXPERTS_2), 0.01),
        'w_gu': nrm(ks[19], (L, N_EXPERTS_2, D_MODEL, 2 * D_FF), D_MODEL ** -0.5),
        'b_gu': nrm(ks[20], (L, N_EXPERTS_2, 2 * D_FF), 0.02),
        'w_dn': nrm(ks[21], (L, N_EXPERTS_2, D_FF, D_MODEL), D_FF ** -0.5),
        'b_dn': nrm(ks[22], (L, N_EXPERTS_2, D_MODEL), 0.02),
    }

def second_block(x, c, ctx, c_ctx, w_mod, b_mod, g_pre_mix, g_post_mix, g_pre_ffn, g_post_ffn,
              w_in, rpb, g_qnorm, g_knorm, w_out_a, w_out_b, w_o,
              w_router, b_router, w_gu, b_gu, w_dn, b_dn):
    B, S, D = x.shape
    C = ctx.shape[1]
    t = jnp.arange(S, dtype=jnp.int32)
    row = t // GRID_W
    col = t % GRID_W
    silu_c = jax.nn.silu(c)
    silu_cc = jax.nn.silu(c_ctx)
    for i in range(DEPTH):
        update_ctx = i < DEPTH - 1
        sh1, sc1, gt1, sh2, sc2, gt2 = jnp.split((silu_c @ w_mod[i] + b_mod[i])[:, None, :], 6, axis=-1)
        n_mod = 6 if update_ctx else 2
        mod_c = jnp.split(silu_cc @ w_mod[i][:, :n_mod * D] + b_mod[i][:n_mod * D], n_mod)

        h = rmsnorm(x, g_pre_mix[i]) * (1 + sc1) + sh1
        h_ctx = rmsnorm(ctx, g_pre_mix[i]) * (1 + mod_c[1]) + mod_c[0]
        y, y_ctx = hybrid_mixer_2(h, h_ctx, w_in[i], rpb[i], g_qnorm[i], g_knorm[i],
                                w_out_a[i], w_out_b[i], w_o[i], row, col, update_ctx)
        x = x + gt1 * rmsnorm(y, g_post_mix[i])

        h2 = rmsnorm(x, g_pre_ffn[i]) * (1 + sc2) + sh2
        tokens = h2.reshape(B * S, D)
        if update_ctx:
            ctx = ctx + mod_c[2] * rmsnorm(y_ctx, g_post_mix[i])
            h2_ctx = rmsnorm(ctx, g_pre_ffn[i]) * (1 + mod_c[4]) + mod_c[3]
            tokens = jnp.concatenate([tokens, h2_ctx.reshape(B * C, D)], axis=0)
        f = moe_ffn(tokens, w_router[i], b_router[i], w_gu[i], b_gu[i], w_dn[i], b_dn[i])
        x = x + gt2 * rmsnorm(f[:B * S].reshape(B, S, D), g_post_ffn[i])
        if update_ctx:
            ctx = ctx + mod_c[5] * rmsnorm(f[B * S:].reshape(B, C, D), g_post_ffn[i])
    return x


def setup_inputs(seed=0):
    out = dict(first_inputs(seed))
    for name, value in second_inputs(seed + 1).items():
        if name != "x":
            out[name + "_2"] = value
    return out


def reference(
    x, c, w_ada, b_ada, w_in, b_f, conv_w, conv_b, w_rg, b_rg, w_ig, b_ig, lru_lambda, g_attn,
    g_lru, w_out, ln1_g, ln1_b, w_grp, b_grp, w_exp, b_exp, w_e_gate, w_e_up, w_e_down, ln2_g,
    ln2_b, c_2, ctx_2, c_ctx_2, w_mod_2, b_mod_2, g_pre_mix_2, g_post_mix_2, g_pre_ffn_2,
    g_post_ffn_2, w_in_2, rpb_2, g_qnorm_2, g_knorm_2, w_out_a_2, w_out_b_2, w_o_2, w_router_2,
    b_router_2, w_gu_2, b_gu_2, w_dn_2, b_dn_2,
):
    x = first_block(
        x, c, w_ada, b_ada, w_in, b_f, conv_w, conv_b, w_rg, b_rg, w_ig, b_ig, lru_lambda,
        g_attn, g_lru, w_out, ln1_g, ln1_b, w_grp, b_grp, w_exp, b_exp, w_e_gate, w_e_up,
        w_e_down, ln2_g, ln2_b,
    )
    return second_block(
        x, c_2, ctx_2, c_ctx_2, w_mod_2, b_mod_2, g_pre_mix_2, g_post_mix_2, g_pre_ffn_2,
        g_post_ffn_2, w_in_2, rpb_2, g_qnorm_2, g_knorm_2, w_out_a_2, w_out_b_2, w_o_2,
        w_router_2, b_router_2, w_gu_2, b_gu_2, w_dn_2, b_dn_2,
    )


_drawn_inputs = setup_inputs


def setup_inputs(seed=0):
    import zlib

    import numpy as np

    out = dict(_drawn_inputs(seed))
    spreads = {}
    factors = {'ctx_2': 6.953,
     'c_ctx_2': 2.818,
     'b_mod_2': 8.0,
     'g_pre_mix_2': 8.0,
     'g_post_mix_2': 8.0,
     'g_pre_ffn_2': 8.0,
     'g_post_ffn_2': 28.038,
     'rpb_2': 51.382,
     'g_qnorm_2': 8.0,
     'g_knorm_2': 8.0,
     'b_router_2': 47.466,
     'b_gu_2': 43.319,
     'b_dn_2': 64.0}
    for name, (base, spread) in spreads.items():
        noise = np.random.default_rng([zlib.crc32(name.encode()), seed]).standard_normal(out[name].shape)
        drawn = base * np.exp(spread * noise) if base else spread * noise
        out[name] = __import__('jax').numpy.asarray(drawn.astype(out[name].dtype))
    for name, factor in factors.items():
        out[name] = (out[name] * factor).astype(out[name].dtype)
    return out
```

```python
from collections import namedtuple
from contextlib import ExitStack, contextmanager

import concourse.bass as bass
from concourse import mybir

F32 = mybir.dt.float32
F32R = mybir.dt.float32r
I32 = mybir.dt.int32
U32 = mybir.dt.uint32
ALU = mybir.AluOpType
ACT = mybir.ActivationFunctionType
AX = mybir.AxisListType

P = 128
D = 1024
KD = D // P
T = 512
TT = T // P
CTX = 256
TC = CTX // P
HD = 64
NH = 8
DA = 512
ALPHA = 2.0 ** 0.25
NEG = -1e30
SLOTS = 6
HI_SLOTS = 3
CHUNK = 2048
ARENA = 24700
ROUTE_AT = 8192


def split3(eng, out, a, b, start, stop):
    eng.matmul(out, a[0], b[0], start=start, stop=False)
    eng.matmul(out, a[0], b[1], start=False, stop=False)
    return eng.matmul(out, a[1], b[0], start=False, stop=stop)


def chain(eng, sem):
    count = [0]

    def link(ins):
        count[0] += 1
        ins.then_inc(sem, 1)
        eng.wait_ge(sem, count[0])
    return link


@contextmanager
def stage(nc):
    before = nc.snapshot_sems()
    with ExitStack() as ctx:
        yield ctx
    nc.clear_and_free_semaphores(nc.allocated_since(before))
    nc.all_engine_barrier()


class Parts:
    pass


def sems(nc, ctx, prefix, *names):
    return namedtuple("Semaphores", names)(*[nc.alloc_semaphore(name=f"{prefix}_{n}") for n in names])


def stream_sems(nc, ctx, prefix, used=None, after=None, offset=0):
    s = Parts()
    s.hi_made = nc.alloc_semaphore(name=f"{prefix}_hi_made")
    s.lo_made = nc.alloc_semaphore(name=f"{prefix}_lo_made")
    s.chunk_used = used if used is not None else nc.alloc_semaphore(name=(f"{prefix}_chunk_used"))
    s.after, s.offset = after, offset
    s.landed = [nc.alloc_semaphore(name=(f"{prefix}_landed{i}")) for i in range(SLOTS)]
    return s



def used_by(s, c, per=0, j=0):
    return s.after[c] if s.after is not None else per * j + (c + 1 + s.offset)


def load_chunk(sp, k, s, src, c, per=0, j=0):
    if per or c >= SLOTS:
        sp.wait_ge(s.chunk_used, used_by(s, c - SLOTS, per, j))
    dst = k.ring[:, c % SLOTS, :]
    if len(src.shape) == 3:
        dst = dst.rearrange("p (a b) -> p a b", a=src.shape[1])
    sp.dma_start(dst, src).then_inc(s.landed[c % SLOTS], 16)


def landed(eng, s, c, per=0, j=0):
    eng.wait_ge(s.landed[c % SLOTS], (per // SLOTS) * 16 * j + 16 * (c // SLOTS + 1))


def make_hi(act, k, s, c, per=0, j=0):
    landed(act, s, c, per, j)
    if per or c >= HI_SLOTS:
        act.wait_ge(s.chunk_used, used_by(s, c - HI_SLOTS, per, j))
    act.activation(k.hi_ring[:, c % HI_SLOTS, :], k.ring[:, c % SLOTS, :], ACT.Copy).then_inc(s.hi_made, 1)


def make_lo(dve, k, s, c, per=0, j=0):
    dve.wait_ge(s.hi_made, per * j + c + 1)
    raw = k.ring[:, c % SLOTS, :]
    dve.tensor_tensor(k.ring_lo[:, c % SLOTS, :], raw, k.hi_ring[:, c % HI_SLOTS, :].bitcast(F32),
                      ALU.subtract).then_inc(s.lo_made, 1)


def chunk_halves(pe, k, s, c, width, per=0, j=0):
    pe.wait_ge(s.lo_made, per * j + c + 1)
    hi = k.hi_ring[:, c % HI_SLOTS, :].rearrange("p (a b) -> p a b", b=width)
    lo = k.ring_lo[:, c % SLOTS, :].rearrange("p (a b) -> p a b", b=width)
    return hi, lo



COLUMNS = {}


def column_rows(a):
    rows = [("conv_w", a["conv_w"].rearrange("o w (j p) -> (o w j) p", p=P)),
            ("conv_b", a["conv_b"].rearrange("o (j p) -> (o j) p", p=P)),
            ("b_rg", a["b_rg"].rearrange("o (j p) -> (o j) p", p=P)),
            ("b_ig", a["b_ig"].rearrange("o (j p) -> (o j) p", p=P)),
            ("lam", a["lru_lambda"].rearrange("o (j p) -> (o j) p", p=P)),
            ("g_lru", a["g_lru"].rearrange("o (j p) -> (o j) p", p=P)),
            ("g_attn", a["g_attn"].rearrange("o (j p) -> (o j) p", p=P)),
            ("g_mix", a["g_pre_mix_2"].rearrange("o (j p) -> (o j) p", p=P)),
            ("g_ffn", a["g_pre_ffn_2"].rearrange("o (j p) -> (o j) p", p=P)),
            ("c1", a["c"].rearrange("o (j p) -> (o j) p", p=P)),
            ("c2", a["c_2"].rearrange("o (j p) -> (o j) p", p=P)),
            ("cc", a["c_ctx_2"].rearrange("(j p) -> j p", p=P))]
    at = 0
    for name, ap in rows:
        COLUMNS[name] = (at, ap.shape[0])
        at += ap.shape[0]
    return rows, at


def col(k, name, j=0, n=1):
    at = COLUMNS[name][0] + j
    return k.cols[:, at:at + n]


def setup(nc, k, a):
    rows, nrows = column_rows(a)
    with stage(nc) as ctx:
        s = sems(nc, ctx, "set", "loaded", "x_loaded", "made", "turned", "copied", "sig", "done", "silu")
        row_tile = k.arena[0:nrows, 0:P]
        turned = k.psum[:, 0, 0:nrows]
        block = ctx.enter_context(nc.Block())

        @block.sync
        def _(sp):
            for name, ap in rows:
                at, n = COLUMNS[name]
                sp.dma_start(row_tile[at:at + n, :], ap).then_inc(s.loaded, 16)
            sp.dma_start(k.x[:], a["x"].rearrange("o (t p) d -> p (o t) d", p=P)).then_inc(s.x_loaded, 16)
            sp.wait_ge(s.x_loaded, 16)

        @block.gpsimd
        def _(pool):
            link = chain(pool, s.done)
            link(pool.memset(k.ident[:], 0.0))
            pool.affine_select(out=k.ident[:], in_=k.ident[:], compare_op=ALU.not_equal, fill=1.0, base=0,
                               pattern=[[-1, P]], channel_multiplier=1).then_inc(s.made, 1)
            link(pool.memset(k.ones[:], 1.0))
            link(pool.affine_select(out=k.before[:], in_=k.ones[:], compare_op=ALU.is_ge, fill=0.0, base=-1,
                               pattern=[[1, P]], channel_multiplier=-1))
            link(pool.memset(k.causal[:], 0.0))
            link(pool.affine_select(out=k.causal[:], in_=k.causal[:], compare_op=ALU.is_ge, fill=NEG, base=0,
                               pattern=[[-1, P]], channel_multiplier=1))
            link(pool.memset(k.neg_sel[:], -1.0))
            link(pool.affine_select(out=k.neg_sel[:], in_=k.neg_sel[:], compare_op=ALU.is_equal, fill=0.0, base=0,
                               pattern=[[-1, NH], [0, P]], channel_multiplier=1))
            link(pool.iota(k.iota[:], pattern=[[1, P]], base=0, channel_multiplier=0,
                      allow_small_or_imprecise_dtypes=True))
            link(pool.iota(k.token[:], pattern=[[P, TT]], base=0, channel_multiplier=1,
                      allow_small_or_imprecise_dtypes=True))
            link(pool.iota(k.half_row[0:32, :], pattern=[[0, 1]], base=0, channel_multiplier=1,
                      allow_small_or_imprecise_dtypes=True))
            link(pool.iota(k.half_row[32:64, :], pattern=[[0, 1]], base=0, channel_multiplier=1,
                      allow_small_or_imprecise_dtypes=True))

        @block.tensor
        def _(pe):
            pe.wait_ge(s.loaded, 16 * len(rows))
            pe.wait_ge(s.made, 1)
            pe.transpose(turned, row_tile, k.ident[0:nrows, 0:nrows]).then_inc(s.turned, 1)

        @block.scalar
        def _(act):
            act.wait_ge(s.copied, 1)
            act.activation(k.silu[:], k.cols[:, COLUMNS["c1"][0]:COLUMNS["c1"][0] + 3 * KD],
                           ACT.Sigmoid).then_inc(s.sig, 1)

        @block.vector
        def _(dve):
            dve.wait_ge(s.turned, 1)
            dve.tensor_copy(k.cols[:], turned).then_inc(s.copied, 1)
            dve.wait_ge(s.copied, 1)
            dve.wait_ge(s.sig, 1)
            dve.tensor_tensor(k.silu[:], k.silu[:], k.cols[:, COLUMNS["c1"][0]:COLUMNS["c1"][0] + 3 * KD],
                              ALU.mult).then_inc(s.silu, 1)



def modulation(nc, k, name, w, b, jobs):
    pieces = sorted({job[0] for job in jobs})
    NQ = 4
    with stage(nc) as ctx:
        s = sems(nc, ctx, name, "bias", "acc", "summed", "put", "row", "chain")
        ss = stream_sems(nc, ctx, name)
        acc = k.arena[:, 0:2 * D].rearrange("p (a n) -> p a n", a=2)
        bias_row = k.arena[0:1, 2 * D:2 * D + 6 * D]
        gate_row = k.arena[0:1, 8 * D:9 * D]
        block = ctx.enter_context(nc.Block())
        by_piece = [[(i, job) for i, job in enumerate(jobs) if job[0] == piece] for piece in pieces]

        @block.sync
        def _(sp):
            sp.dma_start(bias_row, b).then_inc(s.bias, 16)
            for n, (piece, q) in enumerate((piece, q) for piece in pieces for q in range(NQ)):
                src = w[0, q * 256:(q + 1) * 256, piece * D:(piece + 1) * D]
                load_chunk(sp, k, ss, src.rearrange("(k p) n -> p k n", p=P), n)

        @block.vector
        def _(dve):
            link = chain(dve, s.chain)
            for n, group in enumerate(by_piece):
                for q in range(NQ):
                    c = n * NQ + q
                    landed(dve, ss, c)
                    chunk = k.ring[:, c % SLOTS, :].rearrange("p (k n) -> p k n", k=2)
                    for kk in range(2):
                        for i, job in group:
                            scale = k.silu[:, KD * job[1] + 2 * q + kk:KD * job[1] + 2 * q + kk + 1]
                            if q == kk == 0:
                                if i >= 2:
                                    dve.wait_ge(s.summed, i - 1)
                                ins = dve.tensor_scalar(acc[:, i % 2, :], chunk[:, kk, :], scale, None, ALU.mult)
                            else:
                                ins = dve.scalar_tensor_tensor(out=acc[:, i % 2, :], in0=chunk[:, kk, :],
                                                               scalar=scale, in1=acc[:, i % 2, :],
                                                               op0=ALU.mult, op1=ALU.add)
                            if q == NQ - 1 and kk == 1:
                                ins.then_inc(s.acc, 1)
                            else:
                                link(ins)
                    if q < NQ - 1:
                        dve.sem_inc(ss.chunk_used, 1)
                for i, job in group:
                    dve.wait_ge(s.acc, i + 1)
                dve.sem_inc(ss.chunk_used, 1)
                for i, (_, cond, kind, target, gain) in group:
                    dve.wait_ge(s.summed, i + 1)
                    if kind == "shift":
                        dve.tensor_copy(target, k.psum[:, i % 2, 0:KD]).then_inc(s.put, 1)
                    elif kind == "scale":
                        if gain is None:
                            dve.tensor_scalar(target, k.psum[:, i % 2, 0:KD], 1.0, None, ALU.add).then_inc(s.put, 1)
                        else:
                            dve.scalar_tensor_tensor(out=target, in0=k.psum[:, i % 2, 0:KD], scalar=1.0,
                                                     in1=gain, op0=ALU.add, op1=ALU.mult).then_inc(s.put, 1)
                    else:
                        gates = sum(1 for _, job in enumerate(jobs[:i]) if job[2] == "gate")
                        if gates:
                            dve.wait_ge(s.row, 16 * gates)
                        dve.tensor_scalar(gate_row.rearrange("p (a n) -> p a n", a=2), k.psum[0:1, 2:4, :],
                                          1.0 if gain else 0.0, None, ALU.add).then_inc(s.put, 1)

        @block.tensor
        def _(pe):
            pe.wait_ge(s.bias, 16)
            for i, (piece, cond, kind, target, gain) in enumerate(jobs):
                pe.wait_ge(s.acc, i + 1)
                if i >= 1:
                    pe.wait_ge(s.put, i)
                if kind == "gate":
                    for h in range(2):
                        cols = slice(h * 512, (h + 1) * 512)
                        pe.matmul(k.psum[0:1, 2 + h, :], k.ones[:, 0:1], acc[:, i % 2, cols], start=True, stop=False)
                        last = pe.matmul(k.psum[0:1, 2 + h, :], k.ones[0:1, 0:1],
                                         bias_row[:, piece * D + h * 512:piece * D + (h + 1) * 512],
                                         start=False, stop=True)
                else:
                    for kd in range(KD):
                        cols = slice(kd * P, (kd + 1) * P)
                        pe.matmul(k.psum[:, i % 2, kd:kd + 1], acc[:, i % 2, cols], k.ones[:, 0:1],
                                  start=True, stop=False)
                        last = pe.matmul(k.psum[:, i % 2, kd:kd + 1],
                                         bias_row[:, piece * D + kd * P:piece * D + (kd + 1) * P],
                                         k.ones[0:1, 0:1], start=False, stop=True)
                last.then_inc(s.summed, 1)

        @block.gpsimd
        def _(pool):
            rows = 0
            for i, (_, cond, kind, target, gain) in enumerate(jobs):
                if kind == "gate":
                    pool.wait_ge(s.put, i + 1)
                    pool.dma_start(target, gate_row).then_inc(s.row, 16)
                    rows += 1
            if rows:
                pool.wait_ge(s.row, 16 * rows)



def normalise(nc, k, name, src, ntt, width, dst, centre, eps, gain=None, bias=None, store=None):
    halves = width // 512
    with stage(nc) as ctx:
        s = sems(nc, ctx, name, "rows", "chain", "ready", "root", "done", "stored")
        at = k.small
        stats = at[:, 0:ntt * halves * 6].rearrange("p (t h s) -> p t h s", t=ntt, s=6)
        aggr = at[:, 64:64 + 2 * ntt].rearrange("p (t s) -> p t s", s=2)
        inv = at[:, 80:80 + ntt]
        rstd = at[:, 88:88 + ntt]
        gain_t, bias_t = k.rows[:, 0, 0:width], k.rows[:, 1, 0:width]
        block = ctx.enter_context(nc.Block())

        @block.sync
        def _(sp):
            if gain is not None:
                sp.dma_start(gain_t, gain.partition_broadcast(P)).then_inc(s.rows, 16)
            if bias is not None:
                sp.dma_start(bias_t, bias.partition_broadcast(P)).then_inc(s.rows, 16)
            if store is not None:
                for t in range(ntt):
                    sp.wait_ge(s.done, t + 1)
                    sp.dma_start(store[t], dst[:, t, :]).then_inc(s.stored, 16)
                sp.wait_ge(s.stored, 16 * ntt)

        @block.vector
        def _(dve):
            link = chain(dve, s.chain)
            for t in range(ntt):
                for h in range(halves):
                    ins = dve.bn_stats(stats[:, t, h, :], src[:, t, h * 512:(h + 1) * 512])
            link(ins)
            for t in range(ntt):
                ins = dve.bn_aggr(aggr[:, t, :], stats[:, t, :, :])
            link(ins)
            if centre:
                link(dve.tensor_scalar(inv, aggr[:, :, 1], eps, None, ALU.add))
            else:
                link(dve.tensor_tensor(inv, aggr[:, :, 0], aggr[:, :, 0], ALU.mult))
                link(dve.scalar_tensor_tensor(out=inv, in0=inv, scalar=eps, in1=aggr[:, :, 1],
                                              op0=ALU.add, op1=ALU.add))
            dve.reciprocal(inv, inv).then_inc(s.ready, 1)
            dve.wait_ge(s.root, 1)
            if gain is not None:
                dve.wait_ge(s.rows, 16 * (1 + (bias is not None)))
            for t in range(ntt):
                if centre:
                    ins = dve.tensor_scalar(dst[:, t, :], src[:, t, :], aggr[:, t, 0:1], rstd[:, t:t + 1],
                                            ALU.subtract, ALU.mult)
                else:
                    ins = dve.tensor_scalar(dst[:, t, :], src[:, t, :], rstd[:, t:t + 1], None, ALU.mult)
                if gain is not None:
                    link(ins)
                    ins = dve.tensor_tensor(dst[:, t, :], dst[:, t, :], gain_t, ALU.mult)
                if bias is not None:
                    link(ins)
                    ins = dve.tensor_tensor(dst[:, t, :], dst[:, t, :], bias_t, ALU.add)
                ins.then_inc(s.done, 1)

        @block.scalar
        def _(act):
            act.wait_ge(s.ready, 1)
            act.activation(rstd, inv, ACT.Sqrt).then_inc(s.root, 1)


def turn(nc, k, name, src, ntt, nk, scale, shift, hi, lo, plain=None):
    n = ntt * P
    with stage(nc) as ctx:
        s = sems(nc, ctx, name, "turned", "whole", "hi", "lo")
        whole = k.pair[:, :, 0:n]
        block = ctx.enter_context(nc.Block())

        @block.tensor
        def _(pe):
            for i in range(nk):
                if i >= 2:
                    pe.wait_ge(s.whole, i - 1)
                for t in range(ntt):
                    ins = pe.transpose(k.psum[:, i % 2, t * P:(t + 1) * P], src[:, t, i * P:(i + 1) * P], k.ident[:])
                ins.then_inc(s.turned, 1)

        @block.scalar
        def _(act):
            for i in range(nk):
                act.wait_ge(s.turned, i + 1)
                if plain is None and i >= 2:
                    act.wait_ge(s.lo, i - 1)
                out = plain[:, i, :] if plain is not None else whole[:, i % 2, :]
                bias = shift[:, i:i + 1] if shift is not None else 0.0
                if shift is not None:
                    ins = act.activation(out, k.psum[:, i % 2, 0:n], ACT.Identity, bias=bias, scale=scale[:, i:i + 1])
                elif scale is not None:
                    ins = act.activation(out, k.psum[:, i % 2, 0:n], ACT.Identity, scale=scale[:, i:i + 1])
                else:
                    ins = act.activation(out, k.psum[:, i % 2, 0:n], ACT.Copy)
                ins.then_inc(s.whole, 1)
                if plain is None:
                    act.wait_ge(s.whole, i + 1)
                    act.activation(hi[:, i, :], whole[:, i % 2, :], ACT.Copy).then_inc(s.hi, 1)

        @block.vector
        def _(dve):
            if plain is None:
                for i in range(nk):
                    dve.wait_ge(s.hi, i + 1)
                    dve.tensor_tensor(lo[:, i, :], whole[:, i % 2, :], hi[:, i, :].bitcast(F32),
                                      ALU.subtract).then_inc(s.lo, 1)



def project(nc, k, name, chunks, on_dve=False, rows=None, loads=()):
    outs = []
    for n, ch in enumerate(chunks):
        ch["width"] = ch["src"].shape[2]
        for use in ch["uses"]:
            count = use["tokens"] // P if use["kind"] == "T" else ch["width"] // P
            outs += [(n, use, i) for i in range(count)]
    after = [sum(o[0] <= n for o in outs) for n in range(len(chunks))]
    stores = [m for m, (_, use, _) in enumerate(outs) if "store" in use]
    with stage(nc) as ctx:
        s = sems(nc, ctx, name, "multiplied", "emptied", "chain", "rows")
        stored = [nc.alloc_semaphore(name=f"{name}_stored{i}") for i in range(4)] if stores else []
        ss = stream_sems(nc, ctx, name, used=s.multiplied, after=after)
        block = ctx.enter_context(nc.Block())

        @block.sync
        def _(sp):
            for dst, src in loads:
                sp.dma_start(dst, src).then_inc(s.rows, 16)
            if rows is not None:
                sp.dma_start(rows[0], rows[1]).then_inc(s.rows, 16)
            for n, ch in enumerate(chunks):
                load_chunk(sp, k, ss, ch["src"], n)

        def empty(eng, link, n):
            for m, (chunk, use, i) in enumerate(outs):
                if chunk != n:
                    continue
                eng.wait_ge(s.multiplied, m + 1)
                if m in stores and stores.index(m) >= 4:
                    at = stores.index(m)
                    eng.wait_ge(stored[at % 4], 16 * (at // 4))
                use["put"](eng, link, k.psum[:, m % 4, :], i).then_inc(s.emptied, 1)
                if m in stores:
                    at = stores.index(m)
                    eng.wait_ge(s.emptied, m + 1)
                    eng.dma_start(use["store"](i), quarter(k, at)).then_inc(stored[at % 4], 16)

        @block.scalar
        def _(act):
            link = chain(act, s.chain)
            for n in range(min(HI_SLOTS, len(chunks))):
                make_hi(act, k, ss, n)
            for n in range(len(chunks)):
                if not on_dve:
                    empty(act, link, n)
                if n + HI_SLOTS < len(chunks):
                    make_hi(act, k, ss, n + HI_SLOTS)
            for i in range(min(4, len(stores))):
                act.wait_ge(stored[i], 16 * len([x for x in range(len(stores)) if x % 4 == i]))

        @block.vector
        def _(dve):
            link = chain(dve, s.chain)
            if rows is not None or loads:
                dve.wait_ge(s.rows, 16 * (len(loads) + (rows is not None)))
            for n in range(min(HI_SLOTS, len(chunks))):
                make_lo(dve, k, ss, n)
            for n in range(len(chunks)):
                if on_dve:
                    empty(dve, link, n)
                if n + HI_SLOTS < len(chunks):
                    make_lo(dve, k, ss, n + HI_SLOTS)

        @block.tensor
        def _(pe):
            current = None
            for m, (n, use, i) in enumerate(outs):
                ch = chunks[n]
                if n != current:
                    w = chunk_halves(pe, k, ss, n, ch["width"])
                    current = n
                if m >= 4:
                    pe.wait_ge(s.emptied, m - 3)
                nk = ch["src"].shape[1]
                for kk in range(nk):
                    if use["kind"] == "F":
                        a = [x[:, kk, i * P:(i + 1) * P] for x in w]
                        b = [x[:, kk, :] for x in use["u"]]
                        out = k.psum[:, m % 4, 0:use["tokens"]]
                    else:
                        a = [x[:, kk, i * P:(i + 1) * P] for x in use["u"]]
                        b = [x[:, kk, :] for x in w]
                        out = k.psum[:, m % 4, 0:ch["width"]]
                    ins = split3(pe, out, a, b, kk == 0, kk == nk - 1)
                ins.then_inc(s.multiplied, 1)


def quarter(k, i):
    return k.pair[:, (i % 4) // 2, 256 * (i % 2):256 * (i % 2) + 256]


def column_chunk(w, first, width=256):
    return w[:, first:first + width].rearrange("(k p) n -> p k n", p=P)



def log1p_series(dve, link, x, y, y2, acc):
    link(dve.tensor_scalar(y, x, 2.0, None, ALU.add))
    link(dve.reciprocal(y, y))
    link(dve.tensor_tensor(y, y, x, ALU.mult))
    link(dve.tensor_tensor(y2, y, y, ALU.mult))
    terms = [2.0 / (2 * n + 1) for n in range(9)]
    link(dve.tensor_scalar(acc, y2, terms[8], terms[7], ALU.mult, ALU.add))
    for n in range(6, -1, -1):
        link(dve.tensor_tensor(acc, acc, y2, ALU.mult))
        link(dve.tensor_scalar(acc, acc, terms[n], None, ALU.add))
    link(dve.tensor_tensor(acc, acc, y, ALU.mult))


def forget_gates(nc, k, a, u, z, cum, t1, t2, t3, t4):
    first = 3 * DA
    with stage(nc) as ctx:
        s = sems(nc, ctx, "fg", "loaded", "split", "multiplied", "biased", "exp", "chain", "done")
        w = k.small[:, 0:KD * NH].rearrange("p (k h) -> p k h", k=KD)
        w_hi, w_lo = k.small_hi[:], k.small_lo[:]
        b_f = k.small[0:NH, 100:101]
        block = ctx.enter_context(nc.Block())

        @block.sync
        def _(sp):
            sp.dma_start(w, a["w_in"][0, :, first:first + NH].rearrange("(k p) n -> p k n", p=P),
                         allow_slow_non_contiguous=True).then_inc(s.loaded, 16)
            sp.dma_start(b_f, a["b_f"].rearrange("o h -> h o")).then_inc(s.loaded, 16)

        @block.tensor
        def _(pe):
            pe.wait_ge(s.split, 2)
            for kk in range(KD):
                ins = split3(pe, k.psum[0:NH, 0, :], (w_hi[:, kk, :], w_lo[:, kk, :]),
                             [x[:, kk, :] for x in u], kk == 0, kk == KD - 1)
            ins.then_inc(s.multiplied, 1)

        @block.scalar
        def _(act):
            act.wait_ge(s.multiplied, 1)
            act.wait_ge(s.loaded, 32)
            act.activation(z, k.psum[0:NH, 0, :], ACT.Identity, bias=b_f).then_inc(s.biased, 1)
            act.wait_ge(s.biased, 1)
            act.wait_ge(s.biased, 2)
            act.activation(t1, t1, ACT.Exp, scale=-1.0).then_inc(s.exp, 1)

        @block.vector
        def _(dve):
            link = chain(dve, s.chain)
            dve.wait_ge(s.loaded, 32)
            dve.tensor_copy(w_hi, w).then_inc(s.split, 1)
            dve.wait_ge(s.split, 1)
            dve.tensor_tensor(w_lo, w, w_hi.bitcast(F32), ALU.subtract).then_inc(s.split, 1)
            dve.wait_ge(s.biased, 1)
            dve.scalar_tensor_tensor(out=t1, in0=z, scalar=-1.0, in1=z, op0=ALU.mult,
                                     op1=ALU.max).then_inc(s.biased, 1)
            link(dve.tensor_scalar(z, z, 0.0, None, ALU.min))
            dve.wait_ge(s.exp, 1)
            log1p_series(dve, link, t1, t2, t3, t4)
            link(dve.tensor_tensor(z, z, t4, ALU.subtract))
            link(dve.memset(t1, 1.0))
            dve.tensor_tensor_scan(cum, t1, z, 0.0, ALU.mult, ALU.add).then_inc(s.done, 1)


def rg_lru(nc, k, a, xb, gb, xc, r, ig, gl, out):
    NJ = DA // P
    HW = HD
    with stage(nc) as ctx:
        s = sems(nc, ctx, "lru", "zeroed", "loaded", "conv", "gates", "gated", "lam", "lam_exp",
                 "decay", "chain", "tanh_a", "inner", "tanh", "variance", "root", "cubic")
        w_r = k.rows[:, 0, 0:NJ * P].rearrange("p (j n) -> p j n", j=NJ)
        w_i = k.rows[:, 1, 0:NJ * P].rearrange("p (j n) -> p j n", j=NJ)
        rate, e, y, y2 = (k.small[:, 8 * i:8 * i + NJ] for i in range(4))
        flat = lambda t: t.rearrange("p j n -> p (j n)")
        block = ctx.enter_context(nc.Block())

        @block.gpsimd
        def _(pool):
            pool.memset(xb[:, :, 0:3], 0.0)
            pool.memset(w_r, 0.0)
            pool.memset(w_i, 0.0).then_inc(s.zeroed, 1)

        @block.sync
        def _(sp):
            sp.wait_ge(s.zeroed, 1)
            for w, t in (("w_rg", w_r), ("w_ig", w_i)):
                for half in range(2):
                    rows = slice(half * HW, (half + 1) * HW)
                    for j in range(NJ):
                        sp.dma_start(t[rows, j, rows], a[w][0, 2 * j + half]).then_inc(s.loaded, 16)

        @block.vector
        def _(dve):
            link = chain(dve, s.chain)
            dve.wait_ge(s.zeroed, 1)
            for tap in (3, 2, 1, 0):
                for j in range(NJ):
                    wc = col(k, "conv_w", tap * NJ + j)
                    if tap == 3:
                        ins = dve.tensor_scalar(xc[:, j, :], xb[:, j, 3:3 + T], wc, col(k, "conv_b", j),
                                                ALU.mult, ALU.add)
                    else:
                        ins = dve.scalar_tensor_tensor(out=xc[:, j, :], in0=xb[:, j, tap:tap + T], scalar=wc,
                                                       in1=xc[:, j, :], op0=ALU.mult, op1=ALU.add)
                if tap:
                    link(ins)
            ins.then_inc(s.conv, 1)
            lam = col(k, "lam", 0, NJ)
            dve.scalar_tensor_tensor(out=e, in0=lam, scalar=-1.0, in1=lam, op0=ALU.mult,
                                     op1=ALU.max).then_inc(s.lam, 1)
            dve.wait_ge(s.lam_exp, 1)
            log1p_series(dve, link, e, y, y2, rate)
            link(dve.tensor_scalar(e, lam, -1.0, 0.0, ALU.mult, ALU.max))
            link(dve.tensor_tensor(rate, rate, e, ALU.add))
            dve.tensor_scalar(rate, rate, -8.0, None, ALU.mult).then_inc(s.decay, 1)
            link(dve.tensor_tensor(flat(gl), flat(gb), flat(gb), ALU.mult))
            link(dve.tensor_scalar(flat(gl), flat(gl), 0.044715, 1.0, ALU.mult, ALU.add))
            dve.tensor_tensor(flat(gl), flat(gl), flat(gb), ALU.mult).then_inc(s.cubic, 1)
            dve.wait_ge(s.gated, 2 * NJ)
            dve.tensor_tensor(flat(ig), flat(ig), flat(xc), ALU.mult).then_inc(s.inner, 1)
            dve.wait_ge(s.tanh, 1)
            link(dve.scalar_tensor_tensor(out=flat(gl), in0=flat(gl), scalar=1.0, in1=flat(gb),
                                          op0=ALU.add, op1=ALU.mult))
            dve.wait_ge(s.tanh_a, 2 * NJ)
            link(dve.tensor_tensor(flat(gb), flat(r), flat(r), ALU.mult))
            link(dve.scalar_tensor_tensor(out=flat(gb), in0=flat(gb), scalar=1.0, in1=flat(xc),
                                          op0=ALU.add, op1=ALU.mult))
            dve.tensor_scalar(flat(gb), flat(gb), -1.0, None, ALU.mult).then_inc(s.variance, 1)
            dve.wait_ge(s.root, 1)
            dve.wait_ge(s.inner, 1)
            link(dve.tensor_tensor(flat(ig), flat(ig), flat(xc), ALU.mult))
            for j in range(NJ):
                ins = dve.tensor_tensor_scan(gb[:, j, :], r[:, j, :], ig[:, j, :], 0.0, ALU.mult, ALU.add)
            link(ins)
            dve.scalar_tensor_tensor(out=flat(out), in0=flat(gl), scalar=0.5, in1=flat(gb),
                                     op0=ALU.mult, op1=ALU.mult)

        @block.tensor
        def _(pe):
            pe.wait_ge(s.loaded, 16 * 4 * NJ)
            pe.wait_ge(s.conv, 1)
            for i, (w, j) in enumerate((w, j) for w in (w_r, w_i) for j in range(NJ)):
                pe.matmul(k.psum[:, i, :], w[:, j, :], xc[:, j, :], start=True, stop=True).then_inc(s.gates, 1)

        @block.scalar
        def _(act):
            act.wait_ge(s.lam, 1)
            act.activation(e, e, ACT.Exp, scale=-1.0).then_inc(s.lam_exp, 1)
            for i, (t, b, j) in enumerate((t, b, j) for t, b in ((r, "b_rg"), (ig, "b_ig")) for j in range(NJ)):
                act.wait_ge(s.gates, i + 1)
                act.activation(t[:, j, :], k.psum[:, i, :], ACT.Sigmoid, bias=col(k, b, j)).then_inc(s.gated, 1)
            act.wait_ge(s.cubic, 1)
            act.activation(flat(gl), flat(gl), ACT.Tanh, scale=0.7978845608028654).then_inc(s.tanh, 1)
            act.wait_ge(s.decay, 1)
            act.wait_ge(s.gated, 2 * NJ)
            act.wait_ge(s.inner, 1)
            for j in range(NJ):
                act.activation(xc[:, j, :], r[:, j, :], ACT.Tanh, scale=rate[:, j:j + 1]).then_inc(s.tanh_a, 1)
            act.wait_ge(s.tanh_a, NJ)
            for j in range(NJ):
                act.activation(r[:, j, :], r[:, j, :], ACT.Exp, scale=rate[:, j:j + 1]).then_inc(s.tanh_a, 1)
            act.wait_ge(s.variance, 1)
            act.activation(flat(xc), flat(gb), ACT.Sqrt).then_inc(s.root, 1)


def attention(nc, k, name, units, probs, turned, put_scale=1.0):
    groups = [[(g, min(g + 4, u["n"] // P)) for g in range(0, u["n"] // P, 4)] for u in units]
    upto = [sum(len(g) for g in groups[:i + 1]) for i in range(len(units))]
    logits = k.psum[:, 0:4, :].rearrange("p (b a) n -> p b (a n)", b=2)
    with stage(nc) as ctx:
        s = sems(nc, ctx, name, "scored", "chain", "max_ready", "exp_done", "turned", "turned_read", "mixed",
                 "inverted", "put")
        neg_max, total, inverse = k.small[:, 0:2], k.small[:, 8:12], k.small[:, 16:20]
        block = ctx.enter_context(nc.Block())
        last = len(units) - 1

        @block.tensor
        def _(pe):
            def score(u):
                if u >= 2:
                    pe.wait_ge(s.exp_done, u - 1)
                for cols, lhs, rhs, start, stop in units[u]["products"]:
                    ins = pe.matmul(logits[:, u % 2, cols], lhs, rhs, start=start, stop=stop)
                ins.then_inc(s.scored, 1)

            def turn_probs(u):
                pe.wait_ge(s.exp_done, u + 1)
                for i, (g0, g1) in enumerate(groups[u]):
                    m = upto[u] - len(groups[u]) + i
                    if m >= 2:
                        pe.wait_ge(s.turned_read, m - 1)
                    for g in range(g0, g1):
                        ins = pe.transpose(k.psum[:, 4 + m % 2, (g - g0) * P:(g - g0 + 1) * P],
                                           probs[:, u % 2, g * P:(g + 1) * P], k.ident[:])
                    ins.then_inc(s.turned, 1)

            def mix(u):
                pe.wait_ge(s.turned_read, upto[u])
                if u >= 2:
                    pe.wait_ge(s.put, u - 1)
                blocks = units[u]["n"] // P
                for g in range(blocks):
                    ins = pe.matmul(k.psum[:, 6 + u % 2, 0:HD], turned[:, u % 2, g, :], units[u]["v"][g],
                                    start=g == 0, stop=g == blocks - 1)
                ins.then_inc(s.mixed, 1)

            score(0)
            for u in range(len(units)):
                if u < last:
                    score(u + 1)
                if u >= 1:
                    mix(u - 1)
                turn_probs(u)
            mix(last)

        @block.vector
        def _(dve):
            link = chain(dve, s.chain)

            def find_max(u):
                dve.wait_ge(s.scored, u + 1)
                if units[u]["bias"] is not None:
                    bias = units[u]["bias"]
                    part = logits[:, u % 2, 0:bias.shape[1]]
                    link(dve.tensor_tensor(part, part, bias, ALU.add))
                if u >= 2:
                    dve.wait_ge(s.exp_done, u - 1)
                dve.tensor_reduce(neg_max[:, u % 2:u % 2 + 1], logits[:, u % 2, 0:units[u]["n"]], AX.X, ALU.max,
                                  negate=True).then_inc(s.max_ready, 1)

            def put(u):
                dve.wait_ge(s.exp_done, u + 1)
                dve.reciprocal(inverse[:, u % 4:u % 4 + 1], total[:, u % 4:u % 4 + 1]).then_inc(s.inverted, 1)
                dve.wait_ge(s.mixed, u + 1)
                dve.wait_ge(s.inverted, u + 1)
                dve.tensor_scalar(units[u]["out"], k.psum[:, 6 + u % 2, 0:HD], inverse[:, u % 4:u % 4 + 1], None,
                                  ALU.mult).then_inc(s.put, 1)

            for u in range(len(units)):
                find_max(u)
                if u >= 2:
                    put(u - 2)
            for u in range(max(0, last - 1), last + 1):
                put(u)

        @block.scalar
        def _(act):
            def exp(u):
                act.wait_ge(s.max_ready, u + 1)
                if u >= 2:
                    act.wait_ge(s.turned, upto[u - 2])
                if u >= 4:
                    act.wait_ge(s.put, u - 3)
                n = units[u]["n"]
                act.activation(probs[:, u % 2, 0:n], logits[:, u % 2, 0:n], ACT.Exp,
                               bias=neg_max[:, u % 2:u % 2 + 1],
                               accum_out=total[:, u % 4:u % 4 + 1]).then_inc(s.exp_done, 1)

            def read_turned(u):
                if u >= 2:
                    act.wait_ge(s.mixed, u - 1)
                for i, (g0, g1) in enumerate(groups[u]):
                    m = upto[u] - len(groups[u]) + i
                    act.wait_ge(s.turned, m + 1)
                    act.activation(turned[:, u % 2, g0:g1, :].rearrange("p g n -> p (g n)"),
                                   k.psum[:, 4 + m % 2, 0:(g1 - g0) * P], ACT.Copy).then_inc(s.turned_read, 1)

            for u in range(len(units)):
                exp(u)
                if u >= 1:
                    read_turned(u - 1)
            read_turned(last)


def lru_norm(nc, k, lru, squares, hi, lo):
    NJ = DA // P
    with stage(nc) as ctx:
        s = sems(nc, ctx, "lrn", "squared", "summed", "chain", "mean", "root", "whole", "hi", "lo")
        rstd = k.pair[:, 0, :]
        block = ctx.enter_context(nc.Block())

        @block.vector
        def _(dve):
            link = chain(dve, s.chain)
            flat = lambda t: t.rearrange("p j n -> p (j n)")
            dve.tensor_tensor(flat(squares), flat(lru), flat(lru), ALU.mult).then_inc(s.squared, 1)
            dve.wait_ge(s.summed, 1)
            dve.tensor_scalar(rstd, k.psum[:, 0, :], 1.0 / DA, 1e-6, ALU.mult, ALU.add).then_inc(s.mean, 1)
            dve.wait_ge(s.root, 1)
            link(dve.reciprocal(rstd, rstd))
            for j in range(NJ):
                dve.scalar_tensor_tensor(out=lru[:, j, :], in0=lru[:, j, :], scalar=col(k, "g_lru", j),
                                         in1=rstd, op0=ALU.mult, op1=ALU.mult).then_inc(s.whole, 1)
            for j in range(NJ):
                dve.wait_ge(s.hi, j + 1)
                dve.tensor_tensor(lo[:, j, :], lru[:, j, :], hi[:, j, :].bitcast(F32), ALU.subtract)

        @block.tensor
        def _(pe):
            pe.wait_ge(s.squared, 1)
            for j in range(NJ):
                ins = pe.matmul(k.psum[:, 0, :], k.ones[:], squares[:, j, :], start=j == 0, stop=j == NJ - 1)
            ins.then_inc(s.summed, 1)

        @block.scalar
        def _(act):
            act.wait_ge(s.mean, 1)
            act.activation(rstd, rstd, ACT.Sqrt).then_inc(s.root, 1)
            for j in range(NJ):
                act.wait_ge(s.whole, j + 1)
                act.activation(hi[:, j, :], lru[:, j, :], ACT.Copy).then_inc(s.hi, 1)


def block_one_mixer(nc, k, a):
    modulation(nc, k, "mod1", a["w_ada"], a["b_ada"],
               [(0, 0, "shift", k.mod["sh1"], None), (1, 0, "scale", k.mod["sc1"], None),
                (2, 0, "gate", k.gate_rows[0:1, :], True), (3, 0, "shift", k.mod["sh2"], None),
                (4, 0, "scale", k.mod["sc2"], None), (5, 0, "gate", k.gate_rows[1:2, :], True)])

    def area(first, n, cols, dtype=F32):
        t = (k.arena if dtype is F32 else k.arena_r)[:, first:first + n * cols]
        return t.rearrange("p (a b) -> p a b", a=n)

    xn = area(0, TT, D)
    u = (area(4096, KD, T, F32R), area(8192, KD, T, F32R))
    q, kf, v = area(12288, 4, T), area(14336, 4, T), area(16384, TT, DA)
    xb, gb = area(18432, 4, T + 3), area(20492, 4, T)
    cum = k.arena[0:NH, 22540:22540 + T]

    normalise(nc, k, "n1", k.x, TT, D, xn, True, 1e-5)
    turn(nc, k, "t1", xn, TT, KD, k.mod["sc1"], k.mod["sh1"], *u)

    def put_f(dst, j0, offset=0, scale=1.0):
        def put(act, link, psum, i):
            return act.activation(dst[:, j0 + i, offset:offset + T], psum, ACT.Copy, scale=scale)
        return put

    def put_t(dst, c0):
        def put(act, link, psum, i):
            return act.activation(dst[:, i, c0:c0 + 256], psum[:, 0:256], ACT.Copy)
        return put

    w = a["w_in"][0]
    gate0 = 3 * DA + NH
    chunks = []
    for first, kind, put in ((gate0, "F", lambda h: put_f(xb, 2 * h, 3)), (gate0 + DA, "F", lambda h: put_f(gb, 2 * h)),
                             (0, "F", lambda h: put_f(q, 2 * h, scale=HD ** -0.5)), (DA, "F", lambda h: put_f(kf, 2 * h)),
                             (2 * DA, "T", lambda h: put_t(v, 256 * h))):
        for h in range(2):
            chunks.append(dict(src=column_chunk(w, first + 256 * h), uses=[dict(kind=kind, u=u, tokens=T, put=put(h))]))
    project(nc, k, "in1", chunks)

    t = [k.arena[0:NH, 512 * i:512 * (i + 1)] for i in range(5)]
    forget_gates(nc, k, a, u, t[0], cum, *t[1:])
    lru = area(8192, 4, T)
    rg_lru(nc, k, a, xb, gb, area(0, 4, T), area(2048, 4, T), area(4096, 4, T), area(6144, 4, T), lru)

    probs, turned, o = area(0, 2, T), area(1024, 2, T), area(2048, TT, DA)
    units = []
    for h in range(NH):
        rows, j = slice(HD * (h % 2), HD * (h % 2) + HD), h // 2
        for t in range(TT):
            n = (t + 1) * P
            units.append(dict(
                products=[(slice(0, n), q[rows, j, t * P:n], kf[rows, j, 0:n], True, False),
                          (slice(0, n), k.neg_sel[:, h, :], cum[:, 0:n], False, False),
                          (slice(n - P, n), k.ident[:], k.causal[:], False, True)],
                bias=None, n=n, v=[v[:, g, h * HD:(h + 1) * HD] for g in range(t + 1)],
                out=o[:, t, h * HD:(h + 1) * HD]))
    attention(nc, k, "at1", units, probs, turned.rearrange("p b (g n) -> p b g n", n=P))

    mixed = (area(12288, KD, T, F32R), area(16384, KD, T, F32R))
    on = area(4096, TT, DA)
    normalise(nc, k, "n1a", o, TT, DA, on, False, 1e-6)
    turn(nc, k, "t1a", on, TT, 4, col(k, "g_attn", 0, 4), None, mixed[0][:, 0:4, :], mixed[1][:, 0:4, :])
    lru_norm(nc, k, lru, area(4096, 4, T), mixed[0][:, 4:8, :], mixed[1][:, 4:8, :])
    out_projection(nc, k, "out1", a["w_out"][0], mixed, k.gate_rows[0:1, :], k.arena[:, 0:D])
    normalise(nc, k, "n1b", k.x, TT, D, k.x, True, 1e-5, gain=a["ln1_g"][0], bias=a["ln1_b"][0])


def out_projection(nc, k, name, w, mixed, gate_dram, gate):
    def put(h):
        cols = slice(256 * h, 256 * (h + 1))

        def step(dve, link, psum, i):
            tmp = quarter(k, i)
            link(dve.tensor_tensor(tmp, psum[:, 0:256], gate[:, cols], ALU.mult))
            return dve.scalar_tensor_tensor(out=k.x[:, i, cols], in0=k.x[:, i, cols], scalar=ALPHA,
                                            in1=tmp, op0=ALU.mult, op1=ALU.add)
        return step

    chunks = [dict(src=column_chunk(w, 256 * h), uses=[dict(kind="T", u=mixed, tokens=T, put=put(h))])
              for h in range(D // 256)]
    project(nc, k, name, chunks, on_dve=True, rows=(gate, gate_dram[0].partition_broadcast(P)))



def wide(ap, axis, n):
    ap = ap.unsqueeze(axis)
    shape = list(ap.shape)
    shape[axis] = n
    return ap.broadcast_to(shape)


def route(nc, k, name, u, routers, experts, top, groups):
    E, G = experts, groups
    W = E + G
    R = k.route
    NI = R.max_items + 1
    with stage(nc) as ctx:
        s = sems(nc, ctx, name, "loaded", "scored", "chain", "gexp_in", "gexp", "wexp_in", "wexp", "chosen",
                 "ranked", "slots", "listed")
        at = [0]

        def take(*shape):
            n = 1
            for x in shape:
                n *= x
            ap = k.arena[:, ROUTE_AT + at[0]:ROUTE_AT + at[0] + n]
            at[0] += n
            if len(shape) == 1:
                return ap
            letters = "abcd"[:len(shape)]
            return ap.rearrange(f"p ({' '.join(letters)}) -> p {' '.join(letters)}",
                                **{x: y for x, y in zip(letters, shape)})

        w, bias, logits = take(KD, W), take(W), take(TT, W)
        scores, hits, cand = take(TT, E), take(TT, E), take(TT, E)
        best, first, chosen = take(TT, top), take(TT), take(top, TT, E)
        total, shifted, picked = take(TT), take(TT, top), take(TT, E)
        counts, blocks, upto, start = take(E), take(E), take(E), take(E)
        pos, posf, cmp = take(TT, E), take(TT, top), take(NI, E)
        pos_i, slot_i, item_i, slot_f, item_f = (take(TT, top) for _ in range(5))
        place, dest, empty = take(TT, top), take(NI), take(NI)
        slot_hot, item_hot = take(TT * top, P), take(TT * top, NI)
        if G:
            g_hits, g_cand, g_hot, g_best, g_shift, g_total = (
                take(TT, G), take(TT, G), take(TT, G), take(TT), take(TT, G), take(TT))
        block = ctx.enter_context(nc.Block())

        @block.sync
        def _(sp):
            c = 0
            for ws, bs in routers:
                n = ws.shape[1]
                sp.dma_start(w[:, :, c:c + n], ws.rearrange("(k p) n -> p k n", p=P),
                             allow_slow_non_contiguous=True).then_inc(s.loaded, 16)
                sp.dma_start(bias[:, c:c + n], bs.partition_broadcast(P)).then_inc(s.loaded, 16)
                c += n

        @block.tensor
        def _(pe):
            pe.wait_ge(s.loaded, 32 * len(routers))
            for t in range(TT):
                for kk in range(KD):
                    ins = pe.matmul(k.psum[:, 0, t * W:(t + 1) * W], u[:, kk, t * P:(t + 1) * P], w[:, kk, :],
                                    start=kk == 0, stop=kk == KD - 1)
            ins.then_inc(s.scored, 1)
            pe.wait_ge(s.chosen, 1)
            for t in range(TT):
                for t2 in range(t + 1):
                    pe.matmul(k.psum[:, 1, t * E:(t + 1) * E], k.before[:] if t2 == t else k.ones[:],
                              picked[:, t2, :], start=t2 == 0, stop=t2 == t)
            for t in range(TT):
                ins = pe.matmul(k.psum[:, 2, 0:E], k.ones[:], picked[:, t, :], start=t == 0, stop=t == TT - 1)
            ins.then_inc(s.ranked, 1)
            pe.wait_ge(s.slots, 1)
            for m in range(TT * top):
                ins = pe.matmul(k.psum[:, 3, 0:NI], slot_hot[:, m, :], item_hot[:, m, :], start=m == 0,
                                stop=m == TT * top - 1)
            ins.then_inc(s.listed, 1)

        @block.scalar
        def _(act):
            if G:
                act.wait_ge(s.gexp_in, 1)
                act.activation(g_shift, g_shift, ACT.Exp).then_inc(s.gexp, 1)
            act.wait_ge(s.wexp_in, 1)
            act.activation(shifted, shifted, ACT.Exp).then_inc(s.wexp, 1)

        @block.vector
        def _(dve):
            link = chain(dve, s.chain)

            def first_max(src, n, high, hit, cnd, hot):
                link(dve.tensor_reduce(high, src, AX.X, ALU.max))
                link(dve.tensor_tensor(hit, src, wide(high, 2, n), ALU.is_equal))
                link(dve.scalar_tensor_tensor(out=cnd, in0=hit, scalar=-64.0, in1=wide(k.iota[:, 0:n], 1, TT),
                                              op0=ALU.mult, op1=ALU.add))
                link(dve.tensor_reduce(first, cnd, AX.X, ALU.min))
                link(dve.tensor_scalar(first, first, 64.0, None, ALU.add))
                link(dve.tensor_tensor(hot, wide(k.iota[:, 0:n], 1, TT), wide(first, 2, n), ALU.is_equal))

            dve.wait_ge(s.scored, 1)
            psum = k.psum[:, 0, 0:TT * W].rearrange("p (t w) -> p t w", t=TT)
            link(dve.tensor_tensor(logits, psum, wide(bias, 1, TT), ALU.add))
            if G:
                glog = logits[:, :, 0:G]
                first_max(glog, G, g_best, g_hits, g_cand, g_hot)
                dve.tensor_tensor(g_shift, glog, wide(g_best, 2, G), ALU.subtract).then_inc(s.gexp_in, 1)
                sel = wide(g_hot, 3, E // G)
                four = lambda x: x.rearrange("p t (g e) -> p t g e", g=G)
                for t in range(TT):
                    ins = dve.tensor_tensor(four(scores)[:, t], four(logits[:, :, G:])[:, t], sel[:, t], ALU.mult)
                link(ins)
                link(dve.tensor_scalar(g_hot, g_hot, -1.0, -NEG, ALU.add, ALU.mult))
                for t in range(TT):
                    ins = dve.tensor_tensor(four(scores)[:, t], four(scores)[:, t], sel[:, t], ALU.add)
                link(ins)
                dve.wait_ge(s.gexp, 1)
                link(dve.tensor_reduce(g_total, g_shift, AX.X, ALU.add))
            else:
                link(dve.tensor_copy(scores, logits))
            for r in range(top):
                first_max(scores, E, best[:, :, r], hits, cand, chosen[:, r])
                link(dve.scalar_tensor_tensor(out=scores, in0=chosen[:, r], scalar=3 * NEG, in1=scores,
                                              op0=ALU.mult, op1=ALU.add))
                if r == 0:
                    link(dve.tensor_copy(picked, chosen[:, 0]))
                else:
                    link(dve.tensor_tensor(picked, picked, chosen[:, r], ALU.add))
            dve.sem_inc(s.chosen, 1)
            dve.tensor_tensor(shifted, best, wide(best[:, :, 0], 2, top), ALU.subtract).then_inc(s.wexp_in, 1)
            dve.wait_ge(s.wexp, 1)
            link(dve.tensor_reduce(total, shifted, AX.X, ALU.add))
            if G:
                link(dve.tensor_tensor(total, total, g_total, ALU.mult))
            link(dve.reciprocal(total, total))
            link(dve.tensor_tensor(R.weight[:, :, 0:top], shifted, wide(total, 2, top), ALU.mult))

            dve.wait_ge(s.ranked, 1)
            link(dve.tensor_copy(counts, k.psum[:, 2, 0:E]))
            link(dve.tensor_scalar(blocks, counts, 0.0, None, ALU.is_gt))
            for n in range(1, TT):
                link(dve.scalar_tensor_tensor(out=blocks, in0=counts, scalar=float(n * P), in1=blocks,
                                              op0=ALU.is_gt, op1=ALU.add))
            link(dve.tensor_tensor_scan(upto, k.ones[:, 0:E], blocks, 0.0, ALU.mult, ALU.add))
            link(dve.tensor_tensor(start, upto, blocks, ALU.subtract))
            link(dve.tensor_scalar(start, start, float(P), None, ALU.mult))
            rank = k.psum[:, 1, 0:TT * E].rearrange("p (t e) -> p t e", t=TT)
            link(dve.tensor_tensor(pos, rank, wide(start, 1, TT), ALU.add))
            link(dve.tensor_tensor(cmp, wide(upto, 1, NI), wide(k.iota[:, 0:NI], 2, E), ALU.is_le))
            link(dve.tensor_reduce(R.expert_f[:, 0:NI], cmp, AX.X, ALU.add))
            link(dve.tensor_scalar(R.expert_f[:, 0:NI], R.expert_f[:, 0:NI], E - 1.0, None, ALU.min))
            link(dve.tensor_copy(R.expert_i[:, 0:NI], R.expert_f[:, 0:NI]))
            link(dve.tensor_scalar(upto[:, E - 1:E], upto[:, E - 1:E], 1.0, None, ALU.subtract))
            link(dve.tensor_copy(R.last[:], upto[:, E - 1:E]))
            for r in range(top):
                link(dve.tensor_tensor(cand, chosen[:, r], pos, ALU.mult))
                link(dve.tensor_reduce(posf[:, :, r], cand, AX.X, ALU.add))
            link(dve.tensor_copy(pos_i.bitcast(I32), posf))
            link(dve.tensor_scalar(slot_i.bitcast(I32), pos_i.bitcast(I32), P - 1, None, ALU.bitwise_and))
            link(dve.tensor_scalar(item_i.bitcast(I32), pos_i.bitcast(I32), 7, None, ALU.logical_shift_right))
            link(dve.tensor_copy(slot_f, slot_i.bitcast(I32)))
            link(dve.tensor_copy(item_f, item_i.bitcast(I32)))
            for r in range(top):
                ins = dve.tensor_scalar(place[:, :, r], k.token[:], 1.0 + r * T, None, ALU.add)
            link(ins)
            for t in range(TT):
                for r in range(top):
                    m = t * top + r
                    dve.tensor_scalar(slot_hot[:, m, :], k.iota[:], slot_f[:, t, r:r + 1], None, ALU.is_equal)
                    ins = dve.tensor_scalar(item_hot[:, m, :], k.iota[:, 0:NI], item_f[:, t, r:r + 1],
                                            place[:, t, r:r + 1], ALU.is_equal, ALU.mult)
            ins.then_inc(s.slots, 1)
            dve.wait_ge(s.listed, 1)
            listed = k.psum[:, 3, 0:NI]
            link(dve.tensor_scalar(dest, listed, 0.0, None, ALU.is_equal))
            link(dve.tensor_scalar(dest, dest, k.token[:, 0:1], None, ALU.mult))
            link(dve.tensor_tensor(dest, dest, listed, ALU.add))
            link(dve.tensor_scalar(empty, listed, 0.0, float(top * T + 1), ALU.is_equal, ALU.mult))
            link(dve.scalar_tensor_tensor(out=dest, in0=dest, scalar=-1.0, in1=empty, op0=ALU.add, op1=ALU.add))
            link(dve.tensor_copy(R.dest[:, 0:NI], dest))
            link(dve.tensor_scalar(R.ids[:, 0:NI], R.dest[:, 0:NI], T - 1, None, ALU.bitwise_and))



Experts = namedtuple("Experts", "width experts first second down bias down_bias swiglu scale shift x y")


def experts(nc, k, name, m):
    R = k.route
    FK = m.width // P
    A, C = m.first, m.second
    nA, nC, nB = 2 * len(A), 2 * len(C), FK // 2
    PER = nA + nB + nC
    assert PER % SLOTS == 0
    HT_BEFORE = nA - 1
    biased = m.bias is not None

    def area(first, n, cols, dtype=F32):
        t = (k.arena if dtype is F32 else k.arena_r)[:, first:first + n * cols]
        return t.rearrange("p (a b) -> p a b", a=n)

    xg = k.arena[:, 0:D]
    xw = area(1024, KD, P)
    x_hi, x_lo = [area(2048 + 2048 * p, KD, P, F32R) for p in range(2)], [area(3072 + 2048 * p, KD, P, F32R) for p in range(2)]
    h = k.arena[:, 6144:6144 + m.width]
    gate, line, sig, prod = (k.arena[:, 7168 + 512 * i:7680 + 512 * i] for i in range(4))
    h_hi, h_lo = area(9216, FK, P, F32R), area(10240, FK, P, F32R)
    ysb = area(11264, 2, 512)
    bias_hl = k.arena_r[0:64, 12288:15360]
    bias_raw = k.arena[0:64, 15360:18432]
    sel_up = [k.arena_r[0:64, 18432 + P * p:18432 + P * (p + 1)] for p in range(2)]
    sel_down = k.arena_r[0:64, 18432 + 2 * P:18432 + 3 * P]
    idx = k.arena[:, 18432 + 3 * P:18433 + 3 * P].bitcast(I32)
    to_row = k.arena[:, 18433 + 3 * P:18434 + 3 * P].bitcast(I32)
    UP, YB, TB = 0, 4, 6

    with stage(nc) as ctx:
        s = sems(nc, ctx, name, "idx", "to_row", "settled", "gathered", "x_turned", "x_whole", "x_hi", "x_lo", "clipped", "part_read",
                 "line_done", "sig", "h_part", "h_turned", "h_hi", "h_lo", "y_put", "y_stored", "y_free", "bias", "bias_hi",
                 "bias_lo", "sel_up", "sel_down")
        ss = stream_sems(nc, ctx, name, offset=SLOTS)
        block = ctx.enter_context(nc.Block())
        PAIRS = (R.max_items - 1) // 2

        def chunks(j, groups, c0):
            return [(c0 + 2 * g + kh, g, kh) for g in range(len(groups)) for kh in range(2)]


        @block.sync
        def _(sp):
            if biased:
                for half in range(2):
                    c = 0
                    for b in m.bias:
                        sp.dma_start(bias_raw[32 * half:32 * half + b.shape[0], c:c + b.shape[1]], b).then_inc(s.bias, 16)
                        c += b.shape[1]

            def up(e, groups, c0, per, j):
                for c, g, kh in chunks(j, groups, c0):
                    _, w, first, _ = groups[g]
                    src = w[bass.ds(e, 1), kh * 512:(kh + 1) * 512, first:first + 512]
                    load_chunk(sp, k, ss, src.rearrange("a (k p) n -> p (a k) n", p=P), c, per, j)

            def down(e, c0, per, j):
                for q in range(nB):
                    src = m.down[bass.ds(e, 1), q * 256:(q + 1) * 256, :]
                    load_chunk(sp, k, ss, src.rearrange("a (k p) n -> p (a k) n", p=P), c0 + q, per, j)

            def expert(j):
                return sp.value_load(R.expert_i[0:1, bass.ds(j, 1)], min_val=0, max_val=m.experts - 1)

            n = sp.value_load(R.last[0:1, 0:1], min_val=0, max_val=R.max_items - 1) + 1
            e = expert(0)
            up(e, A, 0, 0, 0)
            up(e, C, nA, 0, 0)
            with sp.Fori(0, PAIRS) as i:
                for p in (1, 2):
                    j = 2 * i + p
                    with sp.If(j < n):
                        e = expert(j)
                        up(e, A, -nB, PER, j)
                        down(expert(j - 1), nA - nB, PER, j)
                        up(e, C, nA, PER, j)
            down(expert(n - 1), -nB, PER, n)

        @block.gpsimd
        def _(pool):
            n = pool.value_load(R.last[0:1, 0:1], min_val=0, max_val=R.max_items - 1) + 1

            def gather(j, first=False):
                if not first:
                    pool.wait_ge(s.gathered, 16 * j)
                pool.tensor_copy(idx, R.ids[:, bass.ds(j, 1)]).then_inc(s.idx, 1)
                pool.wait_ge(s.idx, j + 1)
                if not first:
                    pool.wait_ge(s.x_turned, j)
                pool.sem_inc(s.settled, 1)
                pool.indirect_dma_start(xg, None, m.x, bass.IndirectOffsetOnAxis(ap=idx.bitcast(U32), axis=0)
                                        ).then_inc(s.gathered, 16)

            def scatter(j):
                pool.tensor_copy(to_row, R.dest[:, bass.ds(j, 1)]).then_inc(s.to_row, 1)
                pool.wait_ge(s.to_row, j + 1)
                pool.wait_ge(s.y_put, j + 2)
                pool.sem_inc(s.settled, 1)
                pool.indirect_dma_start(m.y, bass.IndirectOffsetOnAxis(ap=to_row.bitcast(U32), axis=0),
                                        ysb.rearrange("p h n -> p (h n)"), None).then_inc(s.y_stored, 16)
                pool.wait_ge(s.y_stored, 16 * j + 16)
                pool.sem_inc(s.y_free, 1)

            pool.sem_inc(s.y_put, 1)
            pool.sem_inc(s.y_free, 1)
            gather(0, True)
            gather(1)
            with pool.Fori(0, PAIRS) as i:
                for p in (1, 2):
                    j = 2 * i + p
                    with pool.If(j < n):
                        gather(j + 1)
                        scatter(j - 1)
            scatter(n - 1)

        @block.tensor
        def _(pe):
            n = pe.value_load(R.last[0:1, 0:1], min_val=0, max_val=R.max_items - 1) + 1

            def turn_x(j, first=False):
                pe.wait_ge(s.gathered, 16 * j + 16)
                if not first:
                    pe.wait_ge(s.h_lo, j - 1)
                    pe.wait_ge(s.x_whole, j)
                for kk in range(KD):
                    ins = pe.transpose(k.psum[:, TB + kk // 4, (kk % 4) * P:(kk % 4 + 1) * P],
                                       xg[:, kk * P:(kk + 1) * P], k.ident[:])
                ins.then_inc(s.x_turned, 1)

            def turn_h(j):
                pe.wait_ge(s.h_part, len(A) * j + len(A))
                pe.wait_ge(s.x_whole, j + 2)
                for kk in range(FK):
                    ins = pe.transpose(k.psum[:, TB + kk // 4, (kk % 4) * P:(kk % 4 + 1) * P],
                                       h[:, kk * P:(kk + 1) * P], k.ident[:])
                ins.then_inc(s.h_turned, 1)

            def up(p, groups, c0, per, j, before=None):
                for c, g, kh in chunks(j, groups, c0):
                    if before is not None and c - c0 == HT_BEFORE:
                        before()
                    bank, _, _, bias_col = groups[g]
                    w = chunk_halves(pe, k, ss, c, 512, per, j)
                    out = k.psum[:, UP + bank, :]
                    if kh == 0 and biased:
                        pe.matmul(out, sel_up[p], bias_hl[:, bias_col:bias_col + 512], start=True, stop=False)
                    for kk in range(4):
                        kd = 4 * kh + kk
                        ins = split3(pe, out, (x_hi[p][:, kd, :], x_lo[p][:, kd, :]), [x[:, kk, :] for x in w],
                                     kd == 0 and not biased, kd == KD - 1)
                    ins.then_inc(ss.chunk_used, 1)

            def down(j, c0, per, jj):
                pe.wait_ge(s.h_lo, jj)
                for q in range(nB):
                    w = chunk_halves(pe, k, ss, c0 + q, D, per, jj)
                    if q == 0:
                        pe.wait_ge(s.y_put, j + 1)
                        if biased:
                            pe.wait_ge(s.sel_down, jj)
                            for hf in range(2):
                                pe.matmul(k.psum[:, YB + hf, :], sel_down,
                                          bias_hl[:, m.down_bias + 512 * hf:m.down_bias + 512 * hf + 512],
                                          start=True, stop=False)
                    for kk in range(2):
                        kf = 2 * q + kk
                        for hf in range(2):
                            ins = split3(pe, k.psum[:, YB + hf, :], (h_hi[:, kf, :], h_lo[:, kf, :]),
                                         [x[:, kk, hf * 512:(hf + 1) * 512] for x in w],
                                         kf == 0 and not biased, kf == FK - 1)
                    ins.then_inc(ss.chunk_used, 1)

            turn_x(0, True)
            pe.wait_ge(s.x_lo, 1)
            if biased:
                pe.wait_ge(s.bias_lo, 1)
                pe.wait_ge(s.sel_up, 1)
            up(0, A, 0, 0, 0)
            pe.wait_ge(s.gathered, 32)
            pe.wait_ge(s.x_whole, 1)
            for kk in range(KD):
                ins = pe.transpose(k.psum[:, TB + kk // 4, (kk % 4) * P:(kk % 4 + 1) * P],
                                   xg[:, kk * P:(kk + 1) * P], k.ident[:])
            ins.then_inc(s.x_turned, 1)
            up(0, C, nA, 0, 0)
            with pe.Fori(0, PAIRS) as i:
                for p in (1, 2):
                    j = 2 * i + p
                    with pe.If(j < n):
                        pe.wait_ge(s.x_lo, j + 1)
                        pe.wait_ge(s.part_read, 2 * j - 1)
                        if biased:
                            pe.wait_ge(s.sel_up, j + 1)
                        up(p % 2, A, -nB, PER, j, before=lambda: turn_h(j - 1))
                        down(j - 1, nA - nB, PER, j)
                        turn_x(j + 1)
                        pe.wait_ge(s.part_read, 2 * j)
                        up(p % 2, C, nA, PER, j)
            turn_h(n - 1)
            down(n - 1, -nB, PER, n)

        @block.scalar
        def _(act):
            n = act.value_load(R.last[0:1, 0:1], min_val=0, max_val=R.max_items - 1) + 1

            def read_x(j, p, free=True):
                act.wait_ge(s.x_turned, j + 1)
                if free:
                    act.wait_ge(s.x_lo, j)
                for kk in range(KD):
                    ins = act.activation(xw[:, kk, :], k.psum[:, TB + kk // 4, (kk % 4) * P:(kk % 4 + 1) * P],
                                         ACT.Identity, bias=m.shift[:, kk:kk + 1], scale=m.scale[:, kk:kk + 1])
                ins.then_inc(s.x_whole, 1)
                act.wait_ge(s.x_whole, j + 1)
                act.activation(x_hi[p].rearrange("p k n -> p (k n)"), xw.rearrange("p k n -> p (k n)"),
                               ACT.Copy).then_inc(s.x_hi, 1)

            def sigmoid(j, half, free=True):
                q = len(A) * j + half
                if m.swiglu:
                    act.wait_ge(s.clipped, q + 1)
                    if free:
                        act.wait_ge(s.h_part, q)
                    act.activation(sig, gate, ACT.Sigmoid, scale=1.702).then_inc(s.sig, 1)
                else:
                    if free:
                        act.wait_ge(s.part_read, 2 * j)
                    act.activation(sig, k.psum[:, UP, :], ACT.Sigmoid).then_inc(s.sig, 1)

            def read_h(j):
                act.wait_ge(s.h_turned, j + 1)
                for hf in range(FK // 4):
                    ins = act.activation(h_hi[:, 4 * hf:4 * hf + 4, :].rearrange("p k n -> p (k n)"),
                                         k.psum[:, TB + hf, :], ACT.Copy)
                ins.then_inc(s.h_hi, 1)

            def put_y(j, free=True):
                if free:
                    act.wait_ge(s.y_free, j + 1)
                for hf in range(2):
                    ins = act.activation(ysb[:, hf, :], k.psum[:, YB + hf, :], ACT.Copy)
                ins.then_inc(s.y_put, 1)

            read_x(0, 0, False)
            for c in range(nA + nC):
                make_hi(act, k, ss, c)
                if c == nA - 1:
                    read_x(1, 1)
                if c == nA + 1 and not m.swiglu:
                    act.wait_ge(ss.chunk_used, SLOTS + nA)
                    sigmoid(0, 0, False)
                if c == nA + 2 and m.swiglu:
                    sigmoid(0, 0, False)
            with act.Fori(0, PAIRS) as i:
                for p in (1, 2):
                    j = 2 * i + p
                    with act.If(j < n):
                        for l in range(PER):
                            c = l - nB
                            make_hi(act, k, ss, c, PER, j)
                            if m.swiglu and l == 1:
                                sigmoid(j - 1, 1)
                            if l == HT_BEFORE + 1:
                                read_h(j - 1)
                            if l == nA + 2:
                                if m.swiglu:
                                    sigmoid(j, 0)
                                else:
                                    act.wait_ge(ss.chunk_used, PER * j + (SLOTS - nB + nA))
                                    sigmoid(j, 0)
                        act.wait_ge(ss.chunk_used, PER * j + (SLOTS + nA))
                        put_y(j - 1)
                        read_x(j + 1, (p + 1) % 2)
            if m.swiglu:
                sigmoid(n - 1, 1)
            make = [make_hi(act, k, ss, -nB + q, PER, n) for q in range(min(nB, HI_SLOTS))]
            read_h(n - 1)
            for q in range(len(make), nB):
                make_hi(act, k, ss, -nB + q, PER, n)
            act.wait_ge(ss.chunk_used, PER * n + SLOTS)
            put_y(n - 1)

        @block.vector
        def _(dve):
            n = dve.value_load(R.last[0:1, 0:1], min_val=0, max_val=R.max_items - 1) + 1

            def select(dst, j, sem):
                dve.tensor_scalar(dst, wide(k.half_row[:, 0], 1, P), R.expert_f[0:64, bass.ds(j, 1)], None,
                                  ALU.is_equal).then_inc(sem, 1)

            def lo_x(j, p):
                dve.wait_ge(s.x_hi, j + 1)
                dve.tensor_tensor(x_lo[p], xw, x_hi[p].bitcast(F32), ALU.subtract).then_inc(s.x_lo, 1)

            def lo_h(j):
                dve.wait_ge(s.h_hi, j + 1)
                for hf in range(FK // 4):
                    part = slice(4 * hf, 4 * hf + 4)
                    ins = dve.tensor_tensor(h_lo[:, part, :].rearrange("p k n -> p (k n)"), k.psum[:, TB + hf, :],
                                            h_hi[:, part, :].rearrange("p k n -> p (k n)").bitcast(F32), ALU.subtract)
                ins.then_inc(s.h_lo, 1)

            def clip(j, half, used):
                dve.wait_ge(ss.chunk_used, used + SLOTS)
                q = 2 * j + half
                dve.tensor_scalar(gate, k.psum[:, UP + 2 * half, :], 7.0, None, ALU.min).then_inc(s.clipped, 1)
                dve.tensor_scalar(line, k.psum[:, UP + 2 * half + 1, :], 7.0, -7.0, ALU.min,
                                  ALU.max).then_inc(s.part_read, 1)
                dve.wait_ge(s.part_read, q + 1)
                dve.scalar_tensor_tensor(out=prod, in0=line, scalar=1.0, in1=gate, op0=ALU.add,
                                         op1=ALU.mult).then_inc(s.line_done, 1)

            def glu(j, half):
                q = 2 * j + half
                dve.wait_ge(s.sig, q + 1)
                dve.wait_ge(s.line_done, q + 1)
                dve.tensor_tensor(h[:, 512 * half:512 * half + 512], prod, sig, ALU.mult).then_inc(s.h_part, 1)

            def silu_gate(j):
                dve.wait_ge(s.sig, j + 1)
                dve.tensor_tensor(prod, k.psum[:, UP, :], sig, ALU.mult).then_inc(s.part_read, 1)

            def silu_up(j, used):
                dve.wait_ge(ss.chunk_used, used + SLOTS)
                dve.wait_ge(s.part_read, 2 * j + 1)
                dve.tensor_tensor(h, prod, k.psum[:, UP + 1, :], ALU.mult).then_inc(s.part_read, 1)
                dve.wait_ge(s.part_read, 2 * j + 2)
                dve.sem_inc(s.h_part, 1)

            dve.sem_inc(ss.chunk_used, SLOTS)
            if biased:
                dve.wait_ge(s.bias, 32 * len(m.bias))
                dve.tensor_copy(bias_hl, bias_raw).then_inc(s.bias_hi, 1)
                dve.wait_ge(s.bias_hi, 1)
                dve.tensor_tensor(bias_hl[32:64, :], bias_raw[32:64, :], bias_hl[32:64, :].bitcast(F32),
                                  ALU.subtract).then_inc(s.bias_lo, 1)
                select(sel_up[0], 0, s.sel_up)
                select(sel_up[1], 1, s.sel_up)
            lo_x(0, 0)
            for c in range(nA + nC):
                make_lo(dve, k, ss, c)
                if c == nA - 1:
                    lo_x(1, 1)
                if c == nA + 1:
                    if m.swiglu:
                        clip(0, 0, nA)
                    else:
                        silu_gate(0)
                if c == nA + 2 and m.swiglu:
                    glu(0, 0)
            with dve.Fori(0, PAIRS) as i:
                for p in (1, 2):
                    j = 2 * i + p
                    with dve.If(j < n):
                        for l in range(PER):
                            c = l - nB
                            make_lo(dve, k, ss, c, PER, j)
                            if l == 1:
                                if m.swiglu:
                                    clip(j - 1, 1, PER * j - nB)
                                    glu(j - 1, 1)
                                else:
                                    silu_up(j - 1, PER * j - nB)
                                if biased:
                                    select(sel_down, j - 1, s.sel_down)
                            if l == HT_BEFORE + 1:
                                lo_h(j - 1)
                            if l == nA + 2:
                                if m.swiglu:
                                    clip(j, 0, PER * j - nB + nA)
                                    glu(j, 0)
                                else:
                                    silu_gate(j)
                        if biased:
                            select(sel_up[(p + 1) % 2], j + 1, s.sel_up)
                        lo_x(j + 1, (p + 1) % 2)
            if m.swiglu:
                clip(n - 1, 1, PER * n - nB)
                glu(n - 1, 1)
            else:
                silu_up(n - 1, PER * n - nB)
            if biased:
                select(sel_down, n - 1, s.sel_down)
            done = min(nB, HI_SLOTS)
            for q in range(done):
                make_lo(dve, k, ss, -nB + q, PER, n)
            lo_h(n - 1)
            for q in range(done, nB):
                make_lo(dve, k, ss, -nB + q, PER, n)


def combine(nc, k, name, top, y, gate_dram=None):
    R = k.route
    NB = 4
    total = k.arena[:, 0:TT * D].rearrange("p (t d) -> p t d", t=TT)
    got = k.arena[:, TT * D:TT * D + NB * D].rearrange("p (b d) -> p b d", b=NB)
    gate = k.rows[:, 0, :]
    with stage(nc) as ctx:
        s = sems(nc, ctx, name, "rows", "added", "chain")
        landed_y = [nc.alloc_semaphore(name=(f"{name}_y{i}")) for i in range(NB)]
        block = ctx.enter_context(nc.Block())

        @block.sync
        def _(sp):
            if gate_dram is not None:
                sp.dma_start(gate, gate_dram[0].partition_broadcast(P)).then_inc(s.rows, 16)
            for m in range(TT * top):
                t, r = m // top, m % top
                if m >= NB:
                    sp.wait_ge(s.added, m - NB + 1)
                sp.dma_start(got[:, m % NB, :], y[r * T + t * P:r * T + (t + 1) * P, :]).then_inc(landed_y[m % NB], 16)

        @block.vector
        def _(dve):
            link = chain(dve, s.chain)
            if gate_dram is not None:
                dve.wait_ge(s.rows, 16)
            for t in range(TT):
                for r in range(top):
                    m = t * top + r
                    dve.wait_ge(landed_y[m % NB], 16 * (m // NB + 1))
                    wt = R.weight[:, t, r:r + 1]
                    if r:
                        dve.wait_ge(s.added, m)
                        dve.scalar_tensor_tensor(out=total[:, t, :], in0=got[:, m % NB, :], scalar=wt,
                                                 in1=total[:, t, :], op0=ALU.mult, op1=ALU.add).then_inc(s.added, 1)
                    else:
                        dve.tensor_scalar(total[:, t, :], got[:, m % NB, :], wt, None, ALU.mult).then_inc(s.added, 1)
                if gate_dram is not None:
                    dve.wait_ge(s.added, (t + 1) * top)
                    link(dve.tensor_tensor(total[:, t, :], total[:, t, :], gate, ALU.mult))
                    dve.scalar_tensor_tensor(out=k.x[:, t, :], in0=k.x[:, t, :], scalar=ALPHA, in1=total[:, t, :],
                                             op0=ALU.mult, op1=ALU.add)


def moe_inputs(nc, k, name, centre, eps):
    xn = k.arena[:, 0:TT * D].rearrange("p (t d) -> p t d", t=TT)
    u = k.arena[:, TT * D:2 * TT * D].rearrange("p (k n) -> p k n", k=KD)
    normalise(nc, k, name + "n", k.x, TT, D, xn, centre, eps,
              store=[k.xn_dram[t * P:(t + 1) * P, :] for t in range(TT)])
    turn(nc, k, name + "t", xn, TT, KD, k.mod["sc2"], k.mod["sh2"], None, None, plain=u)
    return u


def block_one_moe(nc, k, a):
    u = moe_inputs(nc, k, "m1", True, 1e-5)
    k.route.max_items = 23
    route(nc, k, "r1", u, [(a["w_grp"][0], a["b_grp"][0]), (a["w_exp"][0], a["b_exp"][0])], 16, 2, 4)
    m = Experts(width=512, experts=16, first=[(0, a["w_e_gate"][0], 0, 0)],
                        second=[(1, a["w_e_up"][0], 0, 0)], down=a["w_e_down"][0], bias=None, down_bias=None, swiglu=False,
                        scale=k.mod["sc2"], shift=k.mod["sh2"], x=k.xn_dram, y=k.y_dram)
    experts(nc, k, "e1", m)
    combine(nc, k, "c1", 2, k.y_dram, k.gate_rows[1:2, :])
    normalise(nc, k, "n1c", k.x, TT, D, k.x, True, 1e-5, gain=a["ln2_g"][0], bias=a["ln2_b"][0])



GRID_W = 64
GRID_H = T // GRID_W
WIN_R, WIN_C = 8, 16
RPB_R, RPB_C = 2 * WIN_R - 1, 2 * WIN_C - 1
RPB_PAD = 64
RPB_SIZE = NH * RPB_R * RPB_C + 2 * RPB_PAD
NDR = 14
KV = 128
ROT = HD // 4


def constants():
    import numpy as np
    t = np.arange(T)
    freq = np.float32(10000.0) ** (-np.arange(ROT, dtype=np.float32) / np.float32(ROT))
    angle = np.stack([t // GRID_W, t % GRID_W], 1).astype(np.float32)[:, :, None] * freq
    return {"cos_table": np.cos(angle).astype(np.float32), "sin_table": np.sin(angle).astype(np.float32)}


def load_tiles(nc, k, name, loads):
    with stage(nc) as ctx:
        s = sems(nc, ctx, name, "loaded")
        block = ctx.enter_context(nc.Block())

        @block.sync
        def _(sp):
            for dst, src in loads:
                sp.dma_start(dst, src).then_inc(s.loaded, 16)
            sp.wait_ge(s.loaded, 16 * len(loads))


def rotate_heads(nc, k, name, src, heads, ntt, n_rot, gain, scale, outs, scratch, tables):
    n = ntt * heads
    with stage(nc) as ctx:
        s = sems(nc, ctx, name, "loaded", "chain", "mean", "root")
        g = k.small[:, 0:HD]
        mean, rstd = k.small[:, HD:HD + n], scratch[:, 0:n]
        squares = scratch[:, 64:64 + n * HD].rearrange("p (m d) -> p m d", d=HD)
        cos, sin = tables
        flat = src.rearrange("p t h d -> p (t h) d")
        block = ctx.enter_context(nc.Block())

        @block.sync
        def _(sp):
            sp.dma_start(g, gain.partition_broadcast(P)).then_inc(s.loaded, 16)

        @block.scalar
        def _(act):
            act.wait_ge(s.mean, 1)
            act.activation(rstd, mean, ACT.Sqrt).then_inc(s.root, 1)

        @block.vector
        def _(dve):
            link = chain(dve, s.chain)
            link(dve.tensor_tensor(squares, flat, flat, ALU.mult))
            link(dve.tensor_reduce(mean, squares, AX.X, ALU.add))
            link(dve.tensor_scalar(mean, mean, 1.0 / HD, 1e-6, ALU.mult, ALU.add))
            dve.reciprocal(mean, mean).then_inc(s.mean, 1)
            dve.wait_ge(s.root, 1)
            link(dve.tensor_scalar(rstd, rstd, scale, None, ALU.mult))
            link(dve.tensor_tensor(flat, flat, wide(rstd, 2, HD), ALU.mult))
            dve.wait_ge(s.loaded, 16)
            link(dve.tensor_tensor(flat, flat, wide(g, 1, n), ALU.mult))
            q = n * HD // 4
            for t in range(ntt):
                for h0, count, dst in outs:
                    x = src[:, t, h0:h0 + count, :]
                    if t >= n_rot:
                        dve.tensor_copy(dst(t), x)
                        continue
                    v = x.rearrange("p h (a s f) -> p h a s f", a=2, s=2)
                    o = dst(t).rearrange("p h (a s f) -> p h a s f", a=2, s=2)
                    c, sn = wide(cos[:, t], 1, count), wide(sin[:, t], 1, count)
                    w = count * 2 * ROT
                    p1, p2, p3, p4 = (scratch[:, 64 + i * w:64 + (i + 1) * w].rearrange(
                        "p (h a f) -> p h a f", h=count, a=2) for i in range(4))
                    dve.tensor_tensor(p1, v[:, :, :, 0], c, ALU.mult)
                    dve.tensor_tensor(p2, v[:, :, :, 1], sn, ALU.mult)
                    dve.tensor_tensor(p3, v[:, :, :, 1], c, ALU.mult)
                    link(dve.tensor_tensor(p4, v[:, :, :, 0], sn, ALU.mult))
                    dve.tensor_tensor(o[:, :, :, 0], p1, p2, ALU.subtract)
                    link(dve.tensor_tensor(o[:, :, :, 1], p3, p4, ALU.add))


def neighbour_bias(nc, k, a, table, mask):
    size = NH * RPB_R * RPB_C
    zeros = k.small[0:1, 0:RPB_PAD]
    with stage(nc) as ctx:
        s = sems(nc, ctx, "nb", "zero", "padded", "loaded", "chain", "masked", "reversed", "read")
        flip = k.pair[:, 0, 0:P]
        span = NDR * GRID_W // 2
        block = ctx.enter_context(nc.Block())

        @block.gpsimd
        def _(pool):
            link = chain(pool, s.chain)
            pool.memset(zeros, 0.0).then_inc(s.zero, 1)
            link(pool.memset(flip, 0.0))
            link(pool.affine_select(out=flip, in_=flip, compare_op=ALU.not_equal, fill=1.0, base=1 - P,
                                    pattern=[[1, P]], channel_multiplier=1))
            link(pool.memset(mask, 0.0))
            for half in range(2):
                rows = slice(64 * half, 64 * half + 64)
                left = mask[rows, 0:GRID_W - WIN_C]
                link(pool.affine_select(out=left, in_=left, compare_op=ALU.is_ge, fill=NEG, base=WIN_C // 2,
                                        pattern=[[1, GRID_W - WIN_C]], channel_multiplier=-1))
                right = mask[rows, WIN_C:GRID_W]
                ins = pool.affine_select(out=right, in_=right, compare_op=ALU.is_ge, fill=NEG,
                                         base=WIN_C // 2 - 1 - WIN_C, pattern=[[-1, GRID_W - WIN_C]],
                                         channel_multiplier=1)
                if half == 0:
                    link(ins)
            ins.then_inc(s.masked, 1)

        @block.sync
        def _(sp):
            sp.wait_ge(s.zero, 1)
            pad = k.rpb_pad.rearrange("(o n) -> o n", o=1)
            sp.dma_start(pad[:, 0:RPB_PAD], zeros).then_inc(s.padded, 16)
            sp.dma_start(pad[:, RPB_PAD + size:], zeros).then_inc(s.padded, 16)
            sp.dma_start(pad[:, RPB_PAD:RPB_PAD + size], a["rpb_2"].rearrange("o h r c -> o (h r c)")).then_inc(s.padded, 16)
            sp.wait_ge(s.padded, 48)
            for half in range(2):
                for h in range(NH):
                    first = RPB_PAD + (h * RPB_R + 1 - half) * RPB_C + WIN_C - 1 - (GRID_W - 1)
                    src = bass.AP(k.rpb_pad.tensor, first, [[1, GRID_W], [RPB_C, NDR], [1, GRID_W]])
                    sp.dma_start(table[64 * (1 - half):64 * (1 - half) + 64, h], src).then_inc(s.loaded, 16)

        @block.tensor
        def _(pe):
            pe.wait_ge(s.masked, 1)
            pe.wait_ge(s.loaded, 16 * 2 * NH)
            flat = table.rearrange("p h j c -> p (h j c)")
            for m in range(2 * NH):
                if m >= 4:
                    pe.wait_ge(s.read, m - 3)
                pe.matmul(k.psum[:, m % 4, 0:span], flip, flat[:, m * span:(m + 1) * span],
                          start=True, stop=True).then_inc(s.reversed, 1)

        @block.vector
        def _(dve):
            flat = table.rearrange("p h j c -> p (h j) c")
            rows = NDR // 2
            for m in range(2 * NH):
                dve.wait_ge(s.reversed, m + 1)
                dve.tensor_tensor(flat[:, m * rows:(m + 1) * rows, :],
                                  k.psum[:, m % 4, 0:span].rearrange("p (j c) -> p j c", c=GRID_W),
                                  wide(mask, 1, rows), ALU.add).then_inc(s.read, 1)


def add_gated(nc, k, name, y, gate_dram):
    gate = k.rows[:, 0, :]
    with stage(nc) as ctx:
        s = sems(nc, ctx, name, "loaded", "scaled")
        block = ctx.enter_context(nc.Block())

        @block.sync
        def _(sp):
            sp.dma_start(gate, gate_dram[0].partition_broadcast(P)).then_inc(s.loaded, 16)

        @block.vector
        def _(dve):
            dve.wait_ge(s.loaded, 16)
            for t in range(TT):
                dve.tensor_tensor(y[:, t, :], y[:, t, :], gate, ALU.mult).then_inc(s.scaled, 1)
            for t in range(TT):
                dve.wait_ge(s.scaled, t + 1)
                dve.tensor_tensor(k.x[:, t, :], k.x[:, t, :], y[:, t, :], ALU.add)


def block_two_mixer(nc, k, a):
    g_mix, g_ffn = col(k, "g_mix", 0, KD), col(k, "g_ffn", 0, KD)
    modulation(nc, k, "mod2", a["w_mod_2"], a["b_mod_2"],
               [(0, 1, "shift", k.mod["sh1"], None), (0, 2, "shift", k.mod["shc"], None),
                (1, 1, "scale", k.mod["sc1"], g_mix), (1, 2, "scale", k.mod["scc"], g_mix),
                (2, 1, "gate", k.gate_rows[2:3, :], False), (3, 1, "shift", k.mod["sh2"], None),
                (4, 1, "scale", k.mod["sc2"], g_ffn), (5, 1, "gate", k.gate_rows[3:4, :], False)])

    def area(first, n, cols, dtype=F32):
        t = (k.arena if dtype is F32 else k.arena_r)[:, first:first + n * cols]
        return t.rearrange("p (a b) -> p a b", a=n)

    xn = area(0, TT, D)
    u = (area(4096, KD, T, F32R), area(8192, KD, T, F32R))
    normalise(nc, k, "n2", k.x, TT, D, xn, False, 1e-6)
    turn(nc, k, "t2", xn, TT, KD, k.mod["sc1"], k.mod["sh1"], *u)
    ctx_x, ctx_n = area(0, TC, D), area(2048, TC, D)
    uc = (area(12288, KD, CTX, F32R), area(14336, KD, CTX, F32R))
    load_tiles(nc, k, "ctx", [(ctx_x, a["ctx_2"].rearrange("o (t p) d -> p (o t) d", p=P))])
    normalise(nc, k, "n2c", ctx_x, TC, D, ctx_n, False, 1e-6)
    turn(nc, k, "t2c", ctx_n, TC, KD, k.mod["scc"], k.mod["shc"], *uc)

    KEYS = T + CTX
    ka, va, kvb = area(16384, 4, KEYS), area(19456, TT + TC, DA), area(22528, TT + TC, 2 * KV)
    qa, qb = area(0, 4, T), area(2048, TT, DA)

    def use_f(dst, j0, first, uu, tokens, scale=1.0):
        return dict(kind="F", u=uu, tokens=tokens, put=lambda act, link, psum, i: act.activation(
            dst[:, j0 + i, first:first + tokens], psum[:, 0:tokens], ACT.Copy, scale=scale))

    def use_t(dst, t0, c0, uu, tokens):
        return dict(kind="T", u=uu, tokens=tokens, put=lambda act, link, psum, i: act.activation(
            dst[:, t0 + i, c0:c0 + 256], psum[:, 0:256], ACT.Copy))

    staged = [0]

    def use_gate(branch, c0):
        def put(act, link, psum, i):
            staged[0] += 1
            return act.activation(quarter(k, staged[0] - 1), psum[:, 0:256], ACT.Sigmoid)
        return dict(kind="T", u=u, tokens=T, put=put,
                    store=lambda i: k.branch_gates[branch, i * P:(i + 1) * P, c0:c0 + 256])

    w = a["w_in_2"][0]
    at, chunks = 0, []
    for h in range(2):
        chunks.append((at + 256 * h, [use_f(ka, 2 * h, 0, u, T), use_f(ka, 2 * h, T, uc, CTX)]))
    at += DA
    for h in range(2):
        chunks.append((at + 256 * h, [use_t(va, 0, 256 * h, u, T), use_t(va, TT, 256 * h, uc, CTX)]))
    at += DA
    chunks.append((at, [use_t(kvb, 0, 0, u, T), use_t(kvb, TT, 0, uc, CTX)]))
    at += 2 * KV
    for h in range(2):
        chunks.append((at + 256 * h, [use_f(qa, 2 * h, 0, u, T, HD ** -0.5)]))
    at += DA
    for h in range(2):
        chunks.append((at + 256 * h, [use_t(qb, 0, 256 * h, u, T)]))
    at += DA
    for branch in range(2):
        for h in range(4):
            chunks.append((at + branch * D + 256 * h, [use_gate(branch, 256 * h)]))
    project(nc, k, "in2", [dict(src=column_chunk(w, c), uses=uses) for c, uses in chunks])

    tables = [k.arena[:, 4096 + 128 * i:4224 + 128 * i].rearrange("p (t a f) -> p t a f", t=TT, a=2) for i in range(2)]
    load_tiles(nc, k, "rot", [(t, a[n].rearrange("(t p) a f -> p t a f", p=P))
                              for t, n in zip(tables, ("cos_table", "sin_table"))])
    qr, kr = area(4608, TT, DA), area(6656, TT + TC, KV)
    scratch = k.arena[:, 7424:7424 + 4096]
    q_kv = qr.rearrange("p t (m g d) -> p t g m d", m=4, g=2)
    rotate_heads(nc, k, "rq", qb.rearrange("p t (h d) -> p t h d", d=HD), NH, TT, TT, a["g_qnorm_2"][0], HD ** -0.5,
                 [(4 * g, 4, lambda t, g=g: q_kv[:, t, g]) for g in range(2)], scratch, tables)
    kc = area(11520, TT + TC, KV)
    copy_tiles(nc, k, "kc", kc, kvb[:, :, 0:KV])
    rotate_heads(nc, k, "rk", kc.rearrange("p t (h d) -> p t h d", d=HD), 2, TT + TC, TT, a["g_knorm_2"][0], 1.0,
                 [(0, 2, lambda t: kr[:, t, :].rearrange("p (h d) -> p h d", d=HD))], scratch, tables)
    qbt, kbt = area(11520, 4, T), area(13568, 1, KEYS)
    turn(nc, k, "tq", qr, TT, 4, None, None, None, None, plain=qbt)
    turn(nc, k, "tk", kr[:, 0:TT], TT, 1, None, None, None, None, plain=kbt[:, :, 0:T])
    turn(nc, k, "tkc", kr[:, TT:], TC, 1, None, None, None, None, plain=kbt[:, :, T:])

    table = k.arena[:, 4096:4096 + NH * NDR * GRID_W].rearrange("p (h j c) -> p h j c", h=NH, j=NDR)
    neighbour_bias(nc, k, a, table, k.arena[:, 11264:11264 + GRID_W])
    oa, ob = area(14336, TT, DA), area(4096, TT, DA)
    probs = k.rows[:, :, 0:KEYS]
    turned = k.arena[:, 2048:2048 + 2 * KEYS].rearrange("p (b g n) -> p b g n", b=2, n=P)
    units = []
    for h in range(NH):
        rows, j = slice(HD * (h % 2), HD * (h % 2) + HD), h // 2
        for t in range(TT):
            q = qa[rows, j, t * P:(t + 1) * P]
            first = NDR - GRID_H - 2 * t
            units.append(dict(
                products=[(slice(0, T), q, ka[rows, j, 0:T], True, True),
                          (slice(T, KEYS), q, ka[rows, j, T:KEYS], True, True)],
                bias=table[:, h, first:first + GRID_H, :].rearrange("p j c -> p (j c)"), n=KEYS,
                v=[va[:, g, h * HD:(h + 1) * HD] for g in range(TT + TC)], out=oa[:, t, h * HD:(h + 1) * HD]))
    attention(nc, k, "na", units, probs, turned)

    units = []
    for h in range(NH):
        kv = h // 4
        rows = slice(HD * kv, HD * kv + HD)
        for t in range(TT):
            q = qbt[rows, h % 4, t * P:(t + 1) * P]
            units.append(dict(
                products=[(slice(0, T), q, kbt[rows, 0, 0:T], True, True),
                          (slice(T, KEYS), q, kbt[rows, 0, T:KEYS], True, True)],
                bias=None, n=KEYS, v=[kvb[:, g, KV + HD * kv:KV + HD * kv + HD] for g in range(TT + TC)],
                out=ob[:, t, h * HD:(h + 1) * HD]))
    attention(nc, k, "gq", units, probs, turned)

    oat = (area(16384, 4, T, F32R), area(18432, 4, T, F32R))
    obt = (area(20480, 4, T, F32R), area(22528, 4, T, F32R))
    turn(nc, k, "toa", oa, TT, 4, None, None, *oat)
    turn(nc, k, "tob", ob, TT, 4, None, None, *obt)
    z = area(0, TT, D)
    gates = [area(4096, TT, D), area(8192, TT, D)]

    def put_z(branch, c0):
        def put(dve, link, psum, i):
            out = z[:, i, c0:c0 + 512]
            if branch == 0:
                return dve.tensor_tensor(out, psum, gates[0][:, i, c0:c0 + 512], ALU.mult)
            tmp = k.pair[:, i % 2, :]
            link(dve.tensor_tensor(tmp, psum, gates[1][:, i, c0:c0 + 512], ALU.mult))
            return dve.tensor_tensor(out, out, tmp, ALU.add)
        return put

    chunks = [dict(src=column_chunk(a[n][0], c0, 512), uses=[dict(kind="T", u=o, tokens=T, put=put_z(b, c0))])
              for b, (n, o) in enumerate((("w_out_a_2", oat), ("w_out_b_2", obt))) for c0 in (0, 512)]
    project(nc, k, "mg2", chunks, on_dve=True,
            loads=[(gates[b], k.branch_gates[b].rearrange("(t p) d -> p t d", p=P)) for b in range(2)])
    zt = (area(4096, KD, T, F32R), area(8192, KD, T, F32R))
    y = area(12288, TT, D)
    turn(nc, k, "tz", z, TT, KD, None, None, *zt)
    project(nc, k, "out2", [dict(src=column_chunk(a["w_o_2"][0], 256 * h), uses=[use_t(y, 0, 256 * h, zt, T)])
                            for h in range(D // 256)])
    normalise(nc, k, "n2y", y, TT, D, y, False, 1e-6, gain=a["g_post_mix_2"][0])
    add_gated(nc, k, "ag2", y, k.gate_rows[2:3, :])


def copy_tiles(nc, k, name, dst, src):
    with stage(nc) as ctx:
        block = ctx.enter_context(nc.Block())

        @block.vector
        def _(dve):
            dve.tensor_copy(dst, src)


def block_two_moe(nc, k, a):
    u = moe_inputs(nc, k, "m2", False, 1e-6)
    k.route.max_items = 47
    route(nc, k, "r2", u, [(a["w_router_2"][0], a["b_router_2"][0])], 32, 4, 0)
    w_gu = a["w_gu_2"][0]
    m = Experts(width=1024, experts=32, first=[(0, w_gu, 0, 0), (1, w_gu, 1024, 1024)],
                        second=[(2, w_gu, 512, 512), (3, w_gu, 1536, 1536)], down=a["w_dn_2"][0],
                        bias=[a["b_gu_2"][0], a["b_dn_2"][0]], down_bias=2048, swiglu=True,
                        scale=k.mod["sc2"], shift=k.mod["sh2"], x=k.xn_dram, y=k.y_dram)
    experts(nc, k, "e2", m)
    combine(nc, k, "c2", 4, k.y_dram)
    f = k.arena[:, 0:TT * D].rearrange("p (t d) -> p t d", t=TT)
    normalise(nc, k, "n2f", f, TT, D, f, False, 1e-6, gain=a["g_post_ffn_2"][0])
    add_gated(nc, k, "ag3", f, k.gate_rows[3:4, :])


def program(nc, a, out):
    with ExitStack() as ctx:
        def sb(name, shape, dtype=F32):
            return ctx.enter_context(nc.sbuf_tensor("sb_" + name, shape, dtype))

        k = Parts()
        def sb_twice(name, shape):
            at = -(-nc.sbuf_base // 32) * 32
            return sb(name, shape), nc.alloc_sbuf_tensor_at(f"sb_{name}_r", shape, F32R, offset=at)

        k.ring, k.ring_lo = sb_twice("ring", [P, SLOTS, CHUNK])
        k.hi_ring = sb("hi_ring", [P, HI_SLOTS, CHUNK], F32R)
        k.x = sb("x", [P, TT, D])
        k.ident, k.ones, k.before, k.causal = (sb(n, [P, P]) for n in ("ident", "ones", "before", "causal"))
        k.neg_sel = sb("neg_sel", [NH, NH, P])
        k.iota, k.token, k.half_row = sb("iota", [P, P]), sb("token", [P, TT]), sb("half_row", [64, 1])
        k.rows = sb("rows", [P, 2, D])
        k.pair = sb("pair", [P, 2, 512])
        k.small = sb("small", [P, 128])
        k.small_hi, k.small_lo = (sb(n, [P, KD, NH], F32R) for n in ("small_hi", "small_lo"))
        k.cols = sb("cols", [P, column_rows(a)[1]])
        k.silu = sb("silu", [P, 3 * KD])
        mods = sb("mods", [P, 6, KD])
        k.mod = {n: mods[:, i, :] for i, n in enumerate(("sh1", "sc1", "sh2", "sc2", "shc", "scc"))}
        k.arena, k.arena_r = sb_twice("arena", [P, ARENA])
        k.psum = ctx.enter_context(nc.psum_tensor("psum_all", [P, 8, 512], F32))
        k.route = Parts()
        k.route.expert_i, k.route.expert_f = sb("expert_i", [P, 48], I32), sb("expert_f", [P, 48])
        k.route.ids, k.route.dest = sb("ids", [P, 48], I32), sb("dest", [P, 48], I32)
        k.route.last, k.route.weight = sb("last", [P, 1], I32), sb("weight", [P, TT, 4])
        k.branch_gates = nc.dram_tensor("branch_gates", (2, T, D), F32).ap()
        k.rpb_pad = nc.dram_tensor("rpb_pad", (RPB_SIZE,), F32).ap()
        k.xn_dram = nc.dram_tensor("xn_dram", (T, D), F32).ap()
        k.y_dram = nc.dram_tensor("y_dram", (4 * T + P, D), F32).ap()
        k.gate_rows = nc.dram_tensor("gate_rows", (4, D), F32).ap()
        setup(nc, k, a)
        block_one_mixer(nc, k, a)
        block_one_moe(nc, k, a)
        block_two_mixer(nc, k, a)
        block_two_moe(nc, k, a)
        finish(nc, k, out)


def finish(nc, k, out):
    with stage(nc) as ctx:
        stored = nc.alloc_semaphore(name="stored")
        block = ctx.enter_context(nc.Block())

        @block.sync
        def _(sp):
            sp.dma_start(out.rearrange("o (t p) d -> p (o t) d", p=P), k.x[:]).then_inc(stored, 16)
            sp.wait_ge(stored, 16)




_INS = ["x", "c", "w_ada", "b_ada", "w_in", "b_f", "conv_w", "conv_b", "w_rg", "b_rg", "w_ig", "b_ig", "lru_lambda",
        "g_attn", "g_lru", "w_out", "ln1_g", "ln1_b", "w_grp", "b_grp", "w_exp", "b_exp", "w_e_gate", "w_e_up",
        "w_e_down", "ln2_g", "ln2_b", "c_2", "ctx_2", "c_ctx_2", "w_mod_2", "b_mod_2", "g_pre_mix_2",
        "g_post_mix_2", "g_pre_ffn_2", "g_post_ffn_2", "w_in_2", "rpb_2", "g_qnorm_2", "g_knorm_2", "w_out_a_2",
        "w_out_b_2", "w_o_2", "w_router_2", "b_router_2", "w_gu_2", "b_gu_2", "w_dn_2", "b_dn_2"]


def kernel(**inputs):
    import numpy as _np
    import concourse.bacc as _bacc
    from concourse.bass_utils import run_bass_kernel_spmd as _run

    nc = _bacc.Bacc("TRN2", target_bir_lowering=False, num_devices=1)
    values = dict({name: inputs[name] for name in _INS}, **constants())
    arrays, aps = {}, {}
    for name, value in values.items():
        value = _np.ascontiguousarray(value)
        arrays[f"in_{name}_dram"] = value
        aps[name] = nc.dram_tensor(f"in_{name}_dram", value.shape, mybir.dt.from_np(value.dtype),
                                   kind="ExternalInput").ap()
    out = nc.dram_tensor("out_0_dram", (1, T, D), F32, kind="ExternalOutput").ap()
    program(nc, aps, out)
    result = _run(nc, [arrays], core_ids=[0])
    return result.results[0]["out_0_dram"]
```

```python
from collections import namedtuple
from contextlib import ExitStack, contextmanager

import concourse.bass as bass
from concourse import mybir

F32 = mybir.dt.float32
F32R = mybir.dt.float32r
I32 = mybir.dt.int32
U32 = mybir.dt.uint32
ALU = mybir.AluOpType
ACT = mybir.ActivationFunctionType
AX = mybir.AxisListType

P = 128
D = 1024
KD = D // P
T = 512
TT = T // P
CTX = 256
TC = CTX // P
HD = 64
NH = 8
DA = 512
ALPHA = 2.0 ** 0.25
NEG = -1e30
SLOTS = 6
HI_SLOTS = 3
AHEAD = 2
CHUNK = 2048
ARENA = 24700
ROUTE_AT = 8192


def split3(eng, out, a, b, start, stop):
    eng.matmul(out, a[0], b[0], start=start, stop=False)
    eng.matmul(out, a[0], b[1], start=False, stop=False)
    return eng.matmul(out, a[1], b[0], start=False, stop=stop)


def chain(eng, sem):
    count = [0]

    def link(ins):
        count[0] += 1
        ins.then_inc(sem, 1)
        eng.wait_ge(sem, count[0])
    return link


@contextmanager
def stage(nc):
    before = nc.snapshot_sems()
    with ExitStack() as ctx:
        yield ctx
    nc.clear_and_free_semaphores(nc.allocated_since(before))
    nc.all_engine_barrier()


class Parts:
    pass


def sems(nc, ctx, prefix, *names):
    return namedtuple("Semaphores", names)(*[nc.alloc_semaphore(name=f"{prefix}_{n}") for n in names])


def stream_sems(nc, ctx, prefix, k, used=None, after=None, offset=0, more_hi=()):
    s = Parts()
    s.hi_made = nc.alloc_semaphore(name=f"{prefix}_hi_made")
    s.lo_made = nc.alloc_semaphore(name=f"{prefix}_lo_made")
    s.chunk_used = used if used is not None else nc.alloc_semaphore(name=(f"{prefix}_chunk_used"))
    s.after, s.offset, s.ahead = after, offset, 0
    s.raw = [k.ring[:, i, :] for i in range(SLOTS)]
    s.lo = [k.ring_lo[:, i, :] for i in range(SLOTS)]
    s.hi = [k.hi_ring[:, i, :] for i in range(HI_SLOTS)] + list(more_hi)
    s.landed = [nc.alloc_semaphore(name=(f"{prefix}_landed{i}")) for i in range(SLOTS)]
    return s



def used_by(s, c, per=0, j=0):
    return s.after[c] if s.after is not None else per * j + (c + 1 + s.offset)


def load_chunk(sp, k, s, src, c, per=0, j=0):
    if per or c >= SLOTS:
        sp.wait_ge(s.chunk_used, used_by(s, c - SLOTS, per, j))
    dst = s.raw[c % SLOTS]
    if len(src.shape) == 3:
        dst = dst.rearrange("p (a b) -> p a b", a=src.shape[1])
    sp.dma_start(dst, src).then_inc(s.landed[c % SLOTS], 16)


def load_ahead(nc, k, block, name, srcs):
    if not srcs:
        return
    here = nc.alloc_semaphore(name=f"{name}_ahead")

    @block.sync
    def _(sp):
        for i, src in enumerate(srcs):
            sp.dma_start(k.ring[:, i, :].rearrange("p (a b) -> p a b", a=src.shape[1]), src).then_inc(here, 16)
        sp.wait_ge(here, 16 * len(srcs))


def landed(eng, s, c, per=0, j=0):
    if 0 <= c < s.ahead:
        return
    if c % SLOTS < s.ahead:
        c -= SLOTS
    eng.wait_ge(s.landed[c % SLOTS], (per // SLOTS) * 16 * j + 16 * (c // SLOTS + 1))


def make_hi(act, k, s, c, per=0, j=0, whole=False):
    landed(act, s, c, per, j)
    if whole:
        act.wait_ge(s.hi_made, per * j + c)
        act.sem_inc(s.hi_made, 1)
        return
    if per or c >= len(s.hi):
        act.wait_ge(s.chunk_used, used_by(s, c - len(s.hi), per, j))
    act.activation(s.hi[c % len(s.hi)], s.raw[c % SLOTS], ACT.Copy).then_inc(s.hi_made, 1)


def make_lo(dve, k, s, c, per=0, j=0, whole=False):
    dve.wait_ge(s.hi_made, per * j + c + 1)
    if whole:
        dve.wait_ge(s.lo_made, per * j + c)
        dve.sem_inc(s.lo_made, 1)
        return
    dve.tensor_tensor(s.lo[c % SLOTS], s.raw[c % SLOTS], s.hi[c % len(s.hi)].bitcast(F32),
                      ALU.subtract).then_inc(s.lo_made, 1)


def chunk_halves(pe, k, s, c, width, per=0, j=0):
    pe.wait_ge(s.lo_made, per * j + c + 1)
    hi = s.hi[c % len(s.hi)].rearrange("p (a b) -> p a b", b=width)
    lo = s.lo[c % SLOTS].rearrange("p (a b) -> p a b", b=width)
    return hi, lo



NBIAS = 6 * KD
COLUMNS = {}


def column_rows(a):
    rows = [("conv_w", a["conv_w"].rearrange("o w (j p) -> (o w j) p", p=P)),
            ("conv_b", a["conv_b"].rearrange("o (j p) -> (o j) p", p=P)),
            ("b_rg", a["b_rg"].rearrange("o (j p) -> (o j) p", p=P)),
            ("b_ig", a["b_ig"].rearrange("o (j p) -> (o j) p", p=P)),
            ("lam", a["lru_lambda"].rearrange("o (j p) -> (o j) p", p=P)),
            ("g_lru", a["g_lru"].rearrange("o (j p) -> (o j) p", p=P)),
            ("g_attn", a["g_attn"].rearrange("o (j p) -> (o j) p", p=P)),
            ("g_mix", a["g_pre_mix_2"].rearrange("o (j p) -> (o j) p", p=P)),
            ("g_ffn", a["g_pre_ffn_2"].rearrange("o (j p) -> (o j) p", p=P)),
            ("c1", a["c"].rearrange("o (j p) -> (o j) p", p=P)),
            ("c2", a["c_2"].rearrange("o (j p) -> (o j) p", p=P)),
            ("cc", a["c_ctx_2"].rearrange("(j p) -> j p", p=P))]
    at = 0
    for name, ap in rows:
        COLUMNS[name] = (at, ap.shape[0])
        at += ap.shape[0]
    return rows, at


def col(k, name, j=0, n=1):
    at = COLUMNS[name][0] + j
    return k.cols[:, at:at + n]


def setup(nc, k, a):
    rows, nrows = column_rows(a)
    with stage(nc) as ctx:
        s = sems(nc, ctx, "set", "loaded", "x_loaded", "made", "turned", "copied", "sig", "done", "silu")
        row_tile = k.arena[0:nrows, 0:P]
        bias_tile = k.arena[0:2 * NBIAS, P:2 * P]
        turned, bias_turned = k.psum[:, 0, 0:nrows], k.psum[:, 1, 0:2 * NBIAS]
        block = ctx.enter_context(nc.Block())

        @block.sync
        def _(sp):
            for name, ap in rows:
                at, n = COLUMNS[name]
                sp.dma_start(row_tile[at:at + n, :], ap).then_inc(s.loaded, 16)
            for i, b in enumerate(("b_ada", "b_mod_2")):
                sp.dma_start(bias_tile[i * NBIAS:(i + 1) * NBIAS, :],
                             a[b].rearrange("o (j p) -> (o j) p", p=P)).then_inc(s.loaded, 16)
            sp.dma_start(k.x[:], a["x"].rearrange("o (t p) d -> p (o t) d", p=P)).then_inc(s.x_loaded, 16)
            sp.wait_ge(s.x_loaded, 16)

        @block.gpsimd
        def _(pool):
            link = chain(pool, s.done)
            link(pool.memset(k.ident[:], 0.0))
            pool.affine_select(out=k.ident[:], in_=k.ident[:], compare_op=ALU.not_equal, fill=1.0, base=0,
                               pattern=[[-1, P]], channel_multiplier=1).then_inc(s.made, 1)
            link(pool.memset(k.ones[:], 1.0))
            link(pool.affine_select(out=k.before[:], in_=k.ones[:], compare_op=ALU.is_ge, fill=0.0, base=-1,
                               pattern=[[1, P]], channel_multiplier=-1))
            link(pool.memset(k.causal[:], 0.0))
            link(pool.affine_select(out=k.causal[:], in_=k.causal[:], compare_op=ALU.is_ge, fill=NEG, base=0,
                               pattern=[[-1, P]], channel_multiplier=1))
            link(pool.memset(k.neg_sel[:], -1.0))
            link(pool.affine_select(out=k.neg_sel[:], in_=k.neg_sel[:], compare_op=ALU.is_equal, fill=0.0, base=0,
                               pattern=[[-1, NH], [0, P]], channel_multiplier=1))
            link(pool.iota(k.iota[:], pattern=[[1, P]], base=0, channel_multiplier=0,
                      allow_small_or_imprecise_dtypes=True))
            link(pool.iota(k.token[:], pattern=[[P, TT]], base=0, channel_multiplier=1,
                      allow_small_or_imprecise_dtypes=True))
            link(pool.iota(k.half_row[0:32, :], pattern=[[0, 1]], base=0, channel_multiplier=1,
                      allow_small_or_imprecise_dtypes=True))
            link(pool.iota(k.half_row[32:64, :], pattern=[[0, 1]], base=0, channel_multiplier=1,
                      allow_small_or_imprecise_dtypes=True))

        @block.tensor
        def _(pe):
            pe.wait_ge(s.loaded, 16 * (len(rows) + 2))
            pe.wait_ge(s.made, 1)
            pe.transpose(turned, row_tile, k.ident[0:nrows, 0:nrows])
            pe.transpose(bias_turned, bias_tile, k.ident[0:2 * NBIAS, 0:2 * NBIAS]).then_inc(s.turned, 1)

        @block.scalar
        def _(act):
            act.wait_ge(s.copied, 1)
            act.activation(k.silu[:], k.cols[:, COLUMNS["c1"][0]:COLUMNS["c1"][0] + 3 * KD],
                           ACT.Sigmoid).then_inc(s.sig, 1)

        @block.vector
        def _(dve):
            dve.wait_ge(s.turned, 1)
            dve.tensor_copy(k.bias_cols[:], bias_turned)
            dve.tensor_copy(k.cols[:], turned).then_inc(s.copied, 1)
            dve.wait_ge(s.copied, 1)
            dve.wait_ge(s.sig, 1)
            dve.tensor_tensor(k.silu[:], k.silu[:], k.cols[:, COLUMNS["c1"][0]:COLUMNS["c1"][0] + 3 * KD],
                              ALU.mult).then_inc(s.silu, 1)



NQ = 4
NACC = 4


class Modulation:

    def __init__(self, nc, ctx, name, jobs, acc, psum, slots, turns=1):
        self.jobs, self.acc, self.psum, self.slots = jobs, acc, psum, slots
        self.s = sems(nc, ctx, name, "used", "acc", "summed", "put", "stored", "chain")
        self.landed = [nc.alloc_semaphore(name=f"{name}_landed{i}") for i in range(len(slots))]
        self.pieces = []
        for i, job in enumerate(jobs):
            if not self.pieces or self.pieces[-1][0] != job[1:3]:
                self.pieces.append((job[1:3], job[0], []))
            self.pieces[-1][2].append(i)
        self.steps = [(n, q, kk, i) for n, (_, _, group) in enumerate(self.pieces) for q in range(NQ)
                      for kk in range(2) for i in group]
        self.per = -(-len(self.steps) // turns)
        self.rows = sum(job[7] is not None for job in jobs)

    def ready(self, u):
        return [i for n, q, kk, i in self.steps[max(u, 0) * self.per:max(u + 1, 0) * self.per] if q == NQ - 1 and kk == 1]

    def load(self, sp):
        for n, ((_, piece), w, _) in enumerate(self.pieces):
            for q in range(NQ):
                c = n * NQ + q
                if c >= len(self.slots):
                    sp.wait_ge(self.s.used, c - len(self.slots) + 1)
                src = w[0, q * 256:(q + 1) * 256, piece * D:(piece + 1) * D]
                sp.dma_start(self.slots[c % len(self.slots)].rearrange("p (k n) -> p k n", k=2),
                             src.rearrange("(k p) n -> p k n", p=P)).then_inc(self.landed[c % len(self.slots)], 16)

    def accumulate(self, k, dve, u):
        for n, q, kk, i in self.steps[u * self.per:(u + 1) * self.per]:
            c, group, acc = n * NQ + q, self.pieces[n][2], self.acc[i % NACC]
            dve.wait_ge(self.landed[c % len(self.slots)], 16 * (c // len(self.slots) + 1))
            chunk = self.slots[c % len(self.slots)].rearrange("p (k n) -> p k n", k=2)[:, kk, :]
            cond = self.jobs[i][3]
            scale = k.silu[:, KD * cond + 2 * q + kk:KD * cond + 2 * q + kk + 1]
            if q == kk == 0:
                if i >= NACC:
                    dve.wait_ge(self.s.summed, i - NACC + 1)
                ins = dve.tensor_scalar(acc, chunk, scale, None, ALU.mult)
            else:
                dve.wait_ge(self.s.acc, self.done(n, q, kk, i))
                ins = dve.scalar_tensor_tensor(out=acc, in0=chunk, scalar=scale, in1=acc, op0=ALU.mult, op1=ALU.add)
            ins.then_inc(self.s.acc, 1)
            if kk == 1 and i == group[-1]:
                dve.wait_ge(self.s.acc, self.steps.index((n, q, kk, i)) + 1)
                dve.sem_inc(self.s.used, 1)

    def done(self, n, q, kk, i):
        return self.steps.index((n, q, 0, i) if kk else (n, q - 1, 1, i)) + 1

    def sum(self, k, pe, jobs):
        for i in jobs:
            n = [n for n, p in enumerate(self.pieces) if i in p[2]][0]
            pe.wait_ge(self.s.acc, self.steps.index((n, NQ - 1, 1, i)) + 1)
            if i >= 2:
                pe.wait_ge(self.s.put, i - 1)
            for kd in range(KD):
                ins = pe.matmul(self.psum[i % 2][:, kd:kd + 1], self.acc[i % NACC][:, kd * P:(kd + 1) * P],
                                k.ones[:, 0:1], start=True, stop=True)
            ins.then_inc(self.s.summed, 1)

    def put(self, k, dve, jobs):
        for i in jobs:
            _, block, piece, _, kind, target, gain, _ = self.jobs[i]
            at = block * NBIAS + piece * KD
            bias, psum = k.bias_cols[:, at:at + KD], self.psum[i % 2]
            dve.wait_ge(self.s.summed, i + 1)
            if kind == "plain":
                dve.tensor_tensor(target, psum, bias, ALU.add).then_inc(self.s.put, 1)
                continue
            ins = dve.scalar_tensor_tensor(out=target, in0=psum, scalar=1.0, in1=bias, op0=ALU.add, op1=ALU.add)
            if kind == "gain":
                ins.then_inc(self.s.chain, 1)
                dve.wait_ge(self.s.chain, sum(job[4] == "gain" for job in self.jobs[:i + 1]))
                ins = dve.tensor_tensor(target, target, gain, ALU.mult)
            ins.then_inc(self.s.put, 1)

    def store(self, pool):
        for i, job in enumerate(self.jobs):
            if job[7] is not None:
                pool.wait_ge(self.s.put, i + 1)
                pool.dma_start(job[7].rearrange("o (k p) -> p (o k)", p=P), job[5],
                               allow_slow_non_contiguous=True).then_inc(self.s.stored, 16)
        if self.rows:
            pool.wait_ge(self.s.stored, 16 * self.rows)


def modulation(nc, k, name, jobs):
    with stage(nc) as ctx:
        m = Modulation(nc, ctx, name, jobs, [k.arena[:, D * i:D * (i + 1)] for i in range(NACC)],
                       [k.psum[:, b, 0:KD] for b in range(2)], [k.ring[:, i, :] for i in range(SLOTS)])
        block = ctx.enter_context(nc.Block())

        @block.sync
        def _(sp):
            m.load(sp)

        @block.vector
        def _(dve):
            m.accumulate(k, dve, 0)
            m.put(k, dve, range(len(jobs)))

        @block.tensor
        def _(pe):
            m.sum(k, pe, range(len(jobs)))

        @block.gpsimd
        def _(pool):
            m.store(pool)



def normalise(nc, k, name, src, ntt, width, dst, centre, eps, gain=None, bias=None, store=None, gate=None):
    halves = width // 512
    with stage(nc) as ctx:
        s = sems(nc, ctx, name, "rows", "chain", "ready", "root", "done", "stored")
        at = k.small
        stats = at[:, 0:ntt * halves * 6].rearrange("p (t h s) -> p t h s", t=ntt, s=6)
        aggr = at[:, 64:64 + 2 * ntt].rearrange("p (t s) -> p t s", s=2)
        inv = at[:, 80:80 + ntt]
        rstd = at[:, 88:88 + ntt]
        gain_t, bias_t = k.rows[:, 0, 0:width], k.rows[:, 1, 0:width]
        block = ctx.enter_context(nc.Block())

        @block.sync
        def _(sp):
            if gain is not None:
                sp.dma_start(gain_t, gain.partition_broadcast(P)).then_inc(s.rows, 16)
            if bias is not None:
                sp.dma_start(bias_t, bias.partition_broadcast(P)).then_inc(s.rows, 16)
            if gate is not None:
                sp.dma_start(bias_t, gate.partition_broadcast(P)).then_inc(s.rows, 16)
            if store is not None:
                for t in range(ntt):
                    sp.wait_ge(s.done, t + 1)
                    sp.dma_start(store[t], dst[:, t, :]).then_inc(s.stored, 16)
                sp.wait_ge(s.stored, 16 * ntt)

        @block.vector
        def _(dve):
            link = chain(dve, s.chain)
            for t in range(ntt):
                for h in range(halves):
                    ins = dve.bn_stats(stats[:, t, h, :], src[:, t, h * 512:(h + 1) * 512])
            link(ins)
            for t in range(ntt):
                ins = dve.bn_aggr(aggr[:, t, :], stats[:, t, :, :])
            link(ins)
            if centre:
                link(dve.tensor_scalar(inv, aggr[:, :, 1], eps, None, ALU.add))
            else:
                link(dve.tensor_tensor(inv, aggr[:, :, 0], aggr[:, :, 0], ALU.mult))
                link(dve.scalar_tensor_tensor(out=inv, in0=inv, scalar=eps, in1=aggr[:, :, 1],
                                              op0=ALU.add, op1=ALU.add))
            dve.reciprocal(inv, inv).then_inc(s.ready, 1)
            if gain is not None:
                dve.wait_ge(s.rows, 16 * (1 + (bias is not None) + (gate is not None)))
            out = src if gate is not None else dst
            if gate is not None:
                link(dve.tensor_tensor(gain_t, gain_t, bias_t, ALU.mult))
            if centre and gain is not None:
                for t in range(ntt):
                    ins = dve.scalar_tensor_tensor(out=dst[:, t, :], in0=src[:, t, :], scalar=aggr[:, t, 0:1],
                                                   in1=gain_t, op0=ALU.subtract, op1=ALU.mult)
                link(ins)
            dve.wait_ge(s.root, 1)
            for t in range(ntt):
                if centre and gain is not None:
                    ins = dve.scalar_tensor_tensor(out=dst[:, t, :], in0=dst[:, t, :], scalar=rstd[:, t:t + 1],
                                                   in1=bias_t, op0=ALU.mult, op1=ALU.add)
                elif centre:
                    ins = dve.tensor_scalar(dst[:, t, :], src[:, t, :], aggr[:, t, 0:1], rstd[:, t:t + 1],
                                            ALU.subtract, ALU.mult)
                elif gain is not None:
                    ins = dve.scalar_tensor_tensor(out=out[:, t, :], in0=src[:, t, :], scalar=rstd[:, t:t + 1],
                                                   in1=gain_t, op0=ALU.mult, op1=ALU.mult)
                    if bias is not None:
                        link(ins)
                        ins = dve.tensor_tensor(dst[:, t, :], dst[:, t, :], bias_t, ALU.add)
                    if gate is not None:
                        link(ins)
                        ins = dve.tensor_tensor(dst[:, t, :], dst[:, t, :], src[:, t, :], ALU.add)
                else:
                    ins = dve.tensor_scalar(dst[:, t, :], src[:, t, :], rstd[:, t:t + 1], None, ALU.mult)
                ins.then_inc(s.done, 1)

        @block.scalar
        def _(act):
            act.wait_ge(s.ready, 1)
            act.activation(rstd, inv, ACT.Sqrt).then_inc(s.root, 1)


def turn(nc, k, name, src, ntt, nk, scale, shift, hi, lo, plain=None, ahead=()):
    n = ntt * P
    with stage(nc) as ctx:
        s = sems(nc, ctx, name, "turned", "whole", "hi", "lo")
        whole = k.pair[:, :, 0:n]
        block = ctx.enter_context(nc.Block())
        load_ahead(nc, k, block, name, ahead)

        @block.tensor
        def _(pe):
            for i in range(nk):
                if i >= 2:
                    pe.wait_ge(s.whole, i - 1)
                for t in range(ntt):
                    ins = pe.transpose(k.psum[:, i % 2, t * P:(t + 1) * P], src[:, t, i * P:(i + 1) * P], k.ident[:])
                ins.then_inc(s.turned, 1)

        @block.scalar
        def _(act):
            for i in range(nk):
                act.wait_ge(s.turned, i + 1)
                if plain is None and i >= 2:
                    act.wait_ge(s.lo, i - 1)
                out = plain[:, i, :] if plain is not None else whole[:, i % 2, :]
                bias = shift[:, i:i + 1] if shift is not None else 0.0
                if shift is not None:
                    ins = act.activation(out, k.psum[:, i % 2, 0:n], ACT.Identity, bias=bias, scale=scale[:, i:i + 1])
                elif scale is not None:
                    ins = act.activation(out, k.psum[:, i % 2, 0:n], ACT.Identity, scale=scale[:, i:i + 1])
                else:
                    ins = act.activation(out, k.psum[:, i % 2, 0:n], ACT.Copy)
                ins.then_inc(s.whole, 1)
                if plain is None:
                    act.wait_ge(s.whole, i + 1)
                    act.activation(hi[:, i, :], whole[:, i % 2, :], ACT.Copy).then_inc(s.hi, 1)

        @block.vector
        def _(dve):
            if plain is None:
                for i in range(nk):
                    dve.wait_ge(s.hi, i + 1)
                    dve.tensor_tensor(lo[:, i, :], whole[:, i % 2, :], hi[:, i, :].bitcast(F32),
                                      ALU.subtract).then_inc(s.lo, 1)



def project(nc, k, name, chunks, on_dve=False, rows=None, loads=(), beside=None, ahead=0):
    outs = []
    for n, ch in enumerate(chunks):
        ch["width"] = ch["src"].shape[2]
        for use in ch["uses"]:
            count = use["tokens"] // P if use["kind"] == "T" else ch["width"] // P
            outs += [(n, use, i) for i in range(count)]
    after = [sum(o[0] <= n for o in outs) for n in range(len(chunks))]
    stores = [m for m, (_, use, _) in enumerate(outs) if "store" in use]
    with stage(nc) as ctx:
        s = sems(nc, ctx, name, "multiplied", "emptied", "chain", "rows")
        stored = [nc.alloc_semaphore(name=f"{name}_stored{i}") for i in range(4)] if stores else []
        ss = stream_sems(nc, ctx, name, k, used=s.multiplied, after=after)
        ss.ahead = ahead
        mod = beside(nc, ctx, len(chunks)) if beside is not None else None
        block = ctx.enter_context(nc.Block())

        if mod is not None:
            @block.gpsimd
            def _(pool):
                mod.load(pool)
                mod.store(pool)

        @block.sync
        def _(sp):
            for n, ch in enumerate(chunks):
                if n == min(2, len(chunks) - 1):
                    for dst, src in loads:
                        sp.dma_start(dst, src).then_inc(s.rows, 16)
                    if rows is not None:
                        sp.dma_start(rows[0], rows[1]).then_inc(s.rows, 16)
                if n >= ahead:
                    load_chunk(sp, k, ss, ch["src"], n)

        def empty(eng, link, n):
            for m, (chunk, use, i) in enumerate(outs):
                if chunk != n:
                    continue
                eng.wait_ge(s.multiplied, m + 1)
                if m in stores and stores.index(m) >= 4:
                    at = stores.index(m)
                    eng.wait_ge(stored[at % 4], 16 * (at // 4))
                use["put"](eng, link, k.psum[:, m % 4, :], i).then_inc(s.emptied, 1)
                if m in stores:
                    at = stores.index(m)
                    eng.wait_ge(s.emptied, m + 1)
                    eng.dma_start(use["store"](i), quarter(k, at)).then_inc(stored[at % 4], 16)

        @block.scalar
        def _(act):
            link = chain(act, s.chain)
            for n in range(min(HI_SLOTS, len(chunks))):
                make_hi(act, k, ss, n)
            for n in range(len(chunks)):
                if not on_dve:
                    empty(act, link, n)
                if n + HI_SLOTS < len(chunks):
                    make_hi(act, k, ss, n + HI_SLOTS)
            for i in range(min(4, len(stores))):
                act.wait_ge(stored[i], 16 * len([x for x in range(len(stores)) if x % 4 == i]))

        @block.vector
        def _(dve):
            link = chain(dve, s.chain)
            for n in range(min(HI_SLOTS, len(chunks))):
                make_lo(dve, k, ss, n)
            if rows is not None or loads:
                dve.wait_ge(s.rows, 16 * (len(loads) + (rows is not None)))
            for n in range(len(chunks)):
                if on_dve:
                    empty(dve, link, n)
                if n + HI_SLOTS < len(chunks):
                    make_lo(dve, k, ss, n + HI_SLOTS)
                if mod is not None:
                    mod.put(k, dve, mod.ready(n - 3))
                    mod.accumulate(k, dve, n)
            if mod is not None:
                for n in range(len(chunks) - 3, len(chunks)):
                    mod.put(k, dve, mod.ready(n))

        @block.tensor
        def _(pe):
            current = None
            for m, (n, use, i) in enumerate(outs):
                ch = chunks[n]
                if n != current:
                    if mod is not None:
                        mod.sum(k, pe, mod.ready(n - 2))
                    w = chunk_halves(pe, k, ss, n, ch["width"])
                    current = n
                if m >= 4:
                    pe.wait_ge(s.emptied, m - 3)
                nk = ch["src"].shape[1]
                for kk in range(nk):
                    if use["kind"] == "F":
                        a = [x[:, kk, i * P:(i + 1) * P] for x in w]
                        b = [x[:, kk, :] for x in use["u"]]
                        out = k.psum[:, m % 4, 0:use["tokens"]]
                    else:
                        a = [x[:, kk, i * P:(i + 1) * P] for x in use["u"]]
                        b = [x[:, kk, :] for x in w]
                        out = k.psum[:, m % 4, 0:ch["width"]]
                    ins = split3(pe, out, a, b, kk == 0, kk == nk - 1)
                ins.then_inc(s.multiplied, 1)
            if mod is not None:
                for n in range(len(chunks) - 2, len(chunks)):
                    mod.sum(k, pe, mod.ready(n))


def quarter(k, i):
    return k.pair[:, (i % 4) // 2, 256 * (i % 2):256 * (i % 2) + 256]


def column_chunk(w, first, width=256):
    return w[:, first:first + width].rearrange("(k p) n -> p k n", p=P)



def log1p_series(dve, link, x, y, y2, acc):
    link(dve.tensor_scalar(y, x, 2.0, None, ALU.add))
    link(dve.reciprocal(y, y))
    link(dve.tensor_tensor(y, y, x, ALU.mult))
    link(dve.tensor_tensor(y2, y, y, ALU.mult))
    terms = [2.0 / (2 * n + 1) for n in range(9)]
    link(dve.tensor_scalar(acc, y2, terms[8], terms[7], ALU.mult, ALU.add))
    for n in range(6, -1, -1):
        link(dve.tensor_tensor(acc, acc, y2, ALU.mult))
        link(dve.tensor_scalar(acc, acc, terms[n], None, ALU.add))
    link(dve.tensor_tensor(acc, acc, y, ALU.mult))


def gates_and_lru(nc, k, a, u, z, cum, t1, t2, t3, t4, xb, gb, xc, r, ig, gl, out):
    NJ = DA // P
    HW = HD
    with stage(nc) as ctx:
        s = sems(nc, ctx, "lru", "zeroed", "loaded", "conv", "gates", "gated", "lam", "lam_exp",
                 "decay", "chain", "tanh_a", "inner", "tanh", "variance", "root", "cubic",
                 "f_loaded", "split", "multiplied", "biased", "exp")
        w_f = k.rows[:, 0, 512:512 + KD * NH].rearrange("p (k h) -> p k h", k=KD)
        w_hi, w_lo = k.small_hi[:], k.small_lo[:]
        b_f = k.small[0:NH, 100:101]
        w_r = k.rows[:, 0, 0:NJ * P].rearrange("p (j n) -> p j n", j=NJ)
        w_i = k.rows[:, 1, 0:NJ * P].rearrange("p (j n) -> p j n", j=NJ)
        rate, e, y, y2 = (k.small[:, 8 * i:8 * i + NJ] for i in range(4))
        flat = lambda t: t.rearrange("p j n -> p (j n)")
        block = ctx.enter_context(nc.Block())

        @block.gpsimd
        def _(pool):
            pool.memset(xb[:, :, 0:3], 0.0)
            pool.memset(w_r, 0.0)
            pool.memset(w_i, 0.0).then_inc(s.zeroed, 1)

        @block.sync
        def _(sp):
            first = 3 * DA
            sp.dma_start(w_f, a["w_in"][0, :, first:first + NH].rearrange("(k p) n -> p k n", p=P),
                         allow_slow_non_contiguous=True).then_inc(s.f_loaded, 16)
            sp.dma_start(b_f, a["b_f"].rearrange("o h -> h o")).then_inc(s.f_loaded, 16)
            sp.wait_ge(s.zeroed, 1)
            for w, t in (("w_rg", w_r), ("w_ig", w_i)):
                for half in range(2):
                    rows = slice(half * HW, (half + 1) * HW)
                    for j in range(NJ):
                        sp.dma_start(t[rows, j, rows], a[w][0, 2 * j + half]).then_inc(s.loaded, 16)

        @block.vector
        def _(dve):
            link = chain(dve, s.chain)
            dve.wait_ge(s.zeroed, 1)
            for tap in (3, 2, 1, 0):
                for j in range(NJ):
                    wc = col(k, "conv_w", tap * NJ + j)
                    if tap == 3:
                        ins = dve.tensor_scalar(xc[:, j, :], xb[:, j, 3:3 + T], wc, col(k, "conv_b", j),
                                                ALU.mult, ALU.add)
                    else:
                        ins = dve.scalar_tensor_tensor(out=xc[:, j, :], in0=xb[:, j, tap:tap + T], scalar=wc,
                                                       in1=xc[:, j, :], op0=ALU.mult, op1=ALU.add)
                if tap:
                    link(ins)
                if tap == 3:
                    dve.wait_ge(s.f_loaded, 32)
                    dve.tensor_copy(w_hi, w_f).then_inc(s.split, 1)
                    dve.wait_ge(s.split, 1)
                    dve.tensor_tensor(w_lo, w_f, w_hi.bitcast(F32), ALU.subtract).then_inc(s.split, 1)
            ins.then_inc(s.conv, 1)
            dve.wait_ge(s.biased, 1)
            dve.scalar_tensor_tensor(out=t1, in0=z, scalar=-1.0, in1=z, op0=ALU.mult,
                                     op1=ALU.max).then_inc(s.biased, 1)
            lam = col(k, "lam", 0, NJ)
            dve.scalar_tensor_tensor(out=e, in0=lam, scalar=-1.0, in1=lam, op0=ALU.mult,
                                     op1=ALU.max).then_inc(s.lam, 1)
            dve.wait_ge(s.lam_exp, 1)
            log1p_series(dve, link, e, y, y2, rate)
            link(dve.tensor_scalar(e, lam, -1.0, 0.0, ALU.mult, ALU.max))
            link(dve.tensor_tensor(rate, rate, e, ALU.add))
            dve.tensor_scalar(rate, rate, -8.0, None, ALU.mult).then_inc(s.decay, 1)
            link(dve.tensor_tensor(flat(gl), flat(gb), flat(gb), ALU.mult))
            link(dve.tensor_scalar(flat(gl), flat(gl), 0.044715, 1.0, ALU.mult, ALU.add))
            dve.tensor_tensor(flat(gl), flat(gl), flat(gb), ALU.mult).then_inc(s.cubic, 1)
            dve.wait_ge(s.exp, 1)
            link(dve.tensor_scalar(z, z, 0.0, None, ALU.min))
            log1p_series(dve, link, t1, t2, t3, t4)
            link(dve.tensor_tensor(z, z, t4, ALU.subtract))
            link(dve.memset(t1, 1.0))
            dve.tensor_tensor_scan(cum, t1, z, 0.0, ALU.mult, ALU.add)
            dve.wait_ge(s.gated, 2 * NJ)
            dve.tensor_tensor(flat(ig), flat(ig), flat(xc), ALU.mult).then_inc(s.inner, 1)
            dve.wait_ge(s.tanh, 1)
            link(dve.scalar_tensor_tensor(out=flat(gl), in0=flat(gl), scalar=1.0, in1=flat(gb),
                                          op0=ALU.add, op1=ALU.mult))
            dve.wait_ge(s.tanh_a, 2 * NJ)
            link(dve.tensor_tensor(flat(gb), flat(r), flat(r), ALU.mult))
            link(dve.scalar_tensor_tensor(out=flat(gb), in0=flat(gb), scalar=1.0, in1=flat(xc),
                                          op0=ALU.add, op1=ALU.mult))
            dve.tensor_scalar(flat(gb), flat(gb), -1.0, None, ALU.mult).then_inc(s.variance, 1)
            dve.wait_ge(s.root, 1)
            dve.wait_ge(s.inner, 1)
            link(dve.tensor_tensor(flat(ig), flat(ig), flat(xc), ALU.mult))
            for j in range(NJ):
                ins = dve.tensor_tensor_scan(gb[:, j, :], r[:, j, :], ig[:, j, :], 0.0, ALU.mult, ALU.add)
            link(ins)
            dve.scalar_tensor_tensor(out=flat(out), in0=flat(gl), scalar=0.5, in1=flat(gb),
                                     op0=ALU.mult, op1=ALU.mult)

        @block.tensor
        def _(pe):
            pe.wait_ge(s.split, 2)
            for kk in range(KD):
                ins = split3(pe, k.psum[0:NH, 0, :], (w_hi[:, kk, :], w_lo[:, kk, :]),
                             [x[:, kk, :] for x in u], kk == 0, kk == KD - 1)
            ins.then_inc(s.multiplied, 1)
            pe.wait_ge(s.loaded, 16 * 4 * NJ)
            pe.wait_ge(s.conv, 1)
            pe.wait_ge(s.biased, 1)
            for i, (w, j) in enumerate((w, j) for w in (w_r, w_i) for j in range(NJ)):
                pe.matmul(k.psum[:, i, :], w[:, j, :], xc[:, j, :], start=True, stop=True).then_inc(s.gates, 1)

        @block.scalar
        def _(act):
            act.wait_ge(s.multiplied, 1)
            act.wait_ge(s.f_loaded, 32)
            act.activation(z, k.psum[0:NH, 0, :], ACT.Identity, bias=b_f).then_inc(s.biased, 1)
            act.wait_ge(s.biased, 2)
            act.activation(t1, t1, ACT.Exp, scale=-1.0).then_inc(s.exp, 1)
            act.wait_ge(s.lam, 1)
            act.activation(e, e, ACT.Exp, scale=-1.0).then_inc(s.lam_exp, 1)
            for i, (t, b, j) in enumerate((t, b, j) for t, b in ((r, "b_rg"), (ig, "b_ig")) for j in range(NJ)):
                act.wait_ge(s.gates, i + 1)
                act.activation(t[:, j, :], k.psum[:, i, :], ACT.Sigmoid, bias=col(k, b, j)).then_inc(s.gated, 1)
            act.wait_ge(s.cubic, 1)
            act.activation(flat(gl), flat(gl), ACT.Tanh, scale=0.7978845608028654).then_inc(s.tanh, 1)
            act.wait_ge(s.decay, 1)
            act.wait_ge(s.gated, 2 * NJ)
            act.wait_ge(s.inner, 1)
            for j in range(NJ):
                act.activation(xc[:, j, :], r[:, j, :], ACT.Tanh, scale=rate[:, j:j + 1]).then_inc(s.tanh_a, 1)
            act.wait_ge(s.tanh_a, NJ)
            for j in range(NJ):
                act.activation(r[:, j, :], r[:, j, :], ACT.Exp, scale=rate[:, j:j + 1]).then_inc(s.tanh_a, 1)
            act.wait_ge(s.variance, 1)
            act.activation(flat(xc), flat(gb), ACT.Sqrt).then_inc(s.root, 1)


def attention(nc, k, name, units, probs, turned, beside=None):
    groups = [[(g, min(g + 4, u["n"] // P)) for g in range(0, u["n"] // P, 4)] for u in units]
    upto = [sum(len(g) for g in groups[:i + 1]) for i in range(len(units))]
    logits = k.psum[:, 0:4, :].rearrange("p (b a) n -> p b (a n)", b=2)
    with stage(nc) as ctx:
        s = sems(nc, ctx, name, "scored", "chain", "max_ready", "exp_done", "turned", "turned_read", "mixed",
                 "inverted", "scaled", "put")
        neg_max, total, inverse = k.small[:, 0:2], k.small[:, 8:12], k.small[:, 16:20]
        last = len(units) - 1

        def mixed(u):
            rows = units[u]["out"].start_partition()
            return k.psum[rows:rows + HD, 6 + u % 2, 0:P]

        m = beside(nc, ctx, len(units)) if beside is not None else None
        block = ctx.enter_context(nc.Block())

        if m is not None:
            @block.sync
            def _(sp):
                m.load(sp)

            @block.gpsimd
            def _(pool):
                m.store(pool)

        @block.tensor
        def _(pe):
            def score(u):
                if u >= 2:
                    pe.wait_ge(s.exp_done, u - 1)
                for cols, lhs, rhs, start, stop in units[u]["products"]:
                    ins = pe.matmul(logits[:, u % 2, cols], lhs, rhs, start=start, stop=stop)
                ins.then_inc(s.scored, 1)

            def turn_probs(u):
                pe.wait_ge(s.scaled, u + 1)
                for i, (g0, g1) in enumerate(groups[u]):
                    m = upto[u] - len(groups[u]) + i
                    if m >= 2:
                        pe.wait_ge(s.turned_read, m - 1)
                    for g in range(g0, g1):
                        ins = pe.transpose(k.psum[:, 4 + m % 2, (g - g0) * P:(g - g0 + 1) * P],
                                           probs[:, u % 2, g * P:(g + 1) * P], k.ident[:])
                    ins.then_inc(s.turned, 1)

            def mix(u):
                pe.wait_ge(s.turned_read, upto[u])
                if u >= 2:
                    pe.wait_ge(s.put, u - 1)
                blocks = units[u]["n"] // P
                for g in range(blocks):
                    ins = pe.matmul(mixed(u), units[u]["v"][g], turned[:, u % 2, g, :],
                                    start=g == 0, stop=g == blocks - 1)
                ins.then_inc(s.mixed, 1)

            score(0)
            for u in range(last + 3):
                if u < last:
                    score(u + 1)
                if 1 <= u <= last + 1:
                    turn_probs(u - 1)
                if m is not None:
                    m.sum(k, pe, m.ready(u - 2))
                if u >= 2:
                    mix(u - 2)

        @block.vector
        def _(dve):
            link = chain(dve, s.chain)

            def find_max(u):
                dve.wait_ge(s.scored, u + 1)
                if units[u]["bias"] is not None:
                    bias = units[u]["bias"]
                    part = logits[:, u % 2, 0:bias.shape[1]]
                    link(dve.tensor_tensor(part, part, bias, ALU.add))
                if u >= 2:
                    dve.wait_ge(s.exp_done, u - 1)
                dve.tensor_reduce(neg_max[:, u % 2:u % 2 + 1], logits[:, u % 2, 0:units[u]["n"]], AX.X, ALU.max,
                                  negate=True).then_inc(s.max_ready, 1)

            def scale(u):
                dve.wait_ge(s.exp_done, u + 1)
                dve.reciprocal(inverse[:, u % 4:u % 4 + 1], total[:, u % 4:u % 4 + 1]).then_inc(s.inverted, 1)
                dve.wait_ge(s.inverted, u + 1)
                part = probs[:, u % 2, 0:units[u]["n"]]
                dve.tensor_scalar(part, part, inverse[:, u % 4:u % 4 + 1], None, ALU.mult).then_inc(s.scaled, 1)

            def put(u):
                dve.wait_ge(s.mixed, u + 1)
                dve.tensor_copy(units[u]["out"], mixed(u)).then_inc(s.put, 1)

            for u in range(last + 4):
                if 1 <= u <= last + 1:
                    scale(u - 1)
                if u <= last:
                    find_max(u)
                if m is not None:
                    m.put(k, dve, m.ready(u - 3))
                    if u <= last:
                        m.accumulate(k, dve, u)
                if u >= 3:
                    put(u - 3)

        @block.scalar
        def _(act):
            def exp(u):
                act.wait_ge(s.max_ready, u + 1)
                if u >= 2:
                    act.wait_ge(s.turned, upto[u - 2])
                if u >= 4:
                    act.wait_ge(s.inverted, u - 3)
                n = units[u]["n"]
                act.activation(probs[:, u % 2, 0:n], logits[:, u % 2, 0:n], ACT.Exp,
                               bias=neg_max[:, u % 2:u % 2 + 1],
                               accum_out=total[:, u % 4:u % 4 + 1]).then_inc(s.exp_done, 1)

            def read_turned(u):
                if u >= 2:
                    act.wait_ge(s.mixed, u - 1)
                for i, (g0, g1) in enumerate(groups[u]):
                    m = upto[u] - len(groups[u]) + i
                    act.wait_ge(s.turned, m + 1)
                    act.activation(turned[:, u % 2, g0:g1, :].rearrange("p g n -> p (g n)"),
                                   k.psum[:, 4 + m % 2, 0:(g1 - g0) * P], ACT.Copy).then_inc(s.turned_read, 1)

            for u in range(last + 2):
                if u <= last:
                    exp(u)
                if u >= 1:
                    read_turned(u - 1)


def norm_branches(nc, k, name, branches, squares, ahead=()):
    NJ = DA // P
    with stage(nc) as ctx:
        s = sems(nc, ctx, name, "squared", "summed", "chain", "mean", "root", "whole", "hi")
        block = ctx.enter_context(nc.Block())
        load_ahead(nc, k, block, name, ahead)

        @block.vector
        def _(dve):
            link = chain(dve, s.chain)
            flat = lambda t: t.rearrange("p j n -> p (j n)")
            for b, (whole, gain, _, _) in enumerate(branches):
                rstd = k.pair[:, b, :]
                dve.wait_ge(s.summed, b + 1)
                dve.tensor_scalar(rstd, k.psum[:, b, :], 1.0 / DA, 1e-6, ALU.mult, ALU.add).then_inc(s.mean, 1)
            for b, (whole, gain, _, _) in enumerate(branches):
                rstd = k.pair[:, b, :]
                dve.wait_ge(s.root, b + 1)
                link(dve.reciprocal(rstd, rstd))
                for j in range(NJ):
                    dve.scalar_tensor_tensor(out=whole[:, j, :], in0=whole[:, j, :], scalar=col(k, gain, j),
                                             in1=rstd, op0=ALU.mult, op1=ALU.mult).then_inc(s.whole, 1)
            for b, (whole, _, hi, lo) in enumerate(branches):
                dve.wait_ge(s.hi, b + 1)
                dve.tensor_tensor(flat(lo), flat(whole), flat(hi).bitcast(F32), ALU.subtract)

        @block.tensor
        def _(pe):
            for b in range(len(branches)):
                pe.wait_ge(s.squared, b + 1)
                for j in range(NJ):
                    ins = pe.matmul(k.psum[:, b, :], k.ones[:], squares[b][:, j, :], start=j == 0, stop=j == NJ - 1)
                ins.then_inc(s.summed, 1)

        @block.scalar
        def _(act):
            for b, (whole, _, _, _) in enumerate(branches):
                act.activation(squares[b].rearrange("p j n -> p (j n)"), whole.rearrange("p j n -> p (j n)"),
                               ACT.Square).then_inc(s.squared, 1)
            for b in range(len(branches)):
                act.wait_ge(s.mean, b + 1)
                act.activation(k.pair[:, b, :], k.pair[:, b, :], ACT.Sqrt).then_inc(s.root, 1)
            for b, (whole, _, hi, _) in enumerate(branches):
                act.wait_ge(s.whole, NJ * (b + 1))
                act.activation(hi.rearrange("p j n -> p (j n)"), whole.rearrange("p j n -> p (j n)"),
                               ACT.Copy).then_inc(s.hi, 1)


def split_tiles(nc, k, name, tiles, ahead=()):
    with stage(nc) as ctx:
        s = sems(nc, ctx, name, "hi")
        flat = lambda t: t.rearrange("p j n -> p (j n)")
        block = ctx.enter_context(nc.Block())
        load_ahead(nc, k, block, name, ahead)

        @block.scalar
        def _(act):
            for whole, hi, _ in tiles:
                act.activation(flat(hi), flat(whole), ACT.Copy).then_inc(s.hi, 1)

        @block.vector
        def _(dve):
            for i, (whole, hi, lo) in enumerate(tiles):
                dve.wait_ge(s.hi, i + 1)
                dve.tensor_tensor(flat(lo), flat(whole), flat(hi).bitcast(F32), ALU.subtract)


def block_one_mixer(nc, k, a):
    w_1, w_2 = a["w_ada"], a["w_mod_2"]
    g_mix, g_ffn = col(k, "g_mix", 0, KD), col(k, "g_ffn", 0, KD)
    mod, gate = k.mod, k.gate_rows
    modulation(nc, k, "mod1", [(w_1, 0, 0, 0, "plain", mod["sh1"], None, None),
                               (w_1, 0, 1, 0, "plus one", mod["sc1"], None, None)])
    later = [[(w_1, 0, 2, 0, "plus one", mod["gt1"], None, gate[0:1, :]),
             (w_1, 0, 3, 0, "plain", mod["sh2"], None, gate[4:5, :]),
             (w_1, 0, 4, 0, "plus one", mod["sc2"], None, gate[5:6, :]),
             (w_1, 0, 5, 0, "plus one", mod["gt2"], None, gate[1:2, :])],
             [(w_2, 1, 0, 1, "plain", mod["sh1_2"], None, None),
             (w_2, 1, 0, 2, "plain", mod["shc"], None, None),
             (w_2, 1, 1, 1, "gain", mod["sc1_2"], g_mix, None),
             (w_2, 1, 1, 2, "gain", mod["scc"], g_mix, None),
             (w_2, 1, 2, 1, "plain", mod["gt1_2"], None, gate[2:3, :]),
             (w_2, 1, 3, 1, "plain", mod["sh2_2"], None, gate[6:7, :]),
             (w_2, 1, 4, 1, "gain", mod["sc2_2"], g_ffn, gate[7:8, :]),
             (w_2, 1, 5, 1, "plain", mod["gt2_2"], None, gate[3:4, :])]]

    arena = k.arena

    def beside_in(nc, ctx, turns):
        acc = [k.rows[:, 0, :], k.rows[:, 1, :], k.pair[:].rearrange("p a n -> p (a n)"), arena[:, 23060:23060 + D]]
        return Modulation(nc, ctx, "mod1b", later[0], acc, [k.psum[:, b, 0:KD] for b in (4, 5)],
                          [arena[:, CHUNK * i:CHUNK * (i + 1)] for i in range(2)], turns)

    def beside_attention(nc, ctx, turns):
        return Modulation(nc, ctx, "mod2", later[1], [arena[:, 4096 + D * i:4096 + D * (i + 1)] for i in range(NACC)],
                          [k.psum[:, b, 0:KD] for b in (1, 3)], [k.ring[:, i, :] for i in range(SLOTS)], turns)

    def area(first, n, cols, dtype=F32):
        t = (k.arena if dtype is F32 else k.arena_r)[:, first:first + n * cols]
        return t.rearrange("p (a b) -> p a b", a=n)

    xn = area(0, TT, D)
    u = (area(4096, KD, T, F32R), area(8192, KD, T, F32R))
    q, kf, v = area(12288, 4, T), area(14336, 4, T), area(16384, TT, DA)
    xb, gb = area(18432, 4, T + 3), area(20492, 4, T)
    cum = k.arena[0:NH, 22540:22540 + T]

    normalise(nc, k, "n1", k.x, TT, D, xn, True, 1e-5)
    gate0 = 3 * DA + NH
    turn(nc, k, "t1", xn, TT, KD, k.mod["sc1"], k.mod["sh1"], *u,
         ahead=[column_chunk(a["w_in"][0], gate0 + 256 * h) for h in range(AHEAD)])

    def put_f(dst, j0, offset=0, scale=1.0):
        def put(act, link, psum, i):
            return act.activation(dst[:, j0 + i, offset:offset + T], psum, ACT.Copy, scale=scale)
        return put

    def put_t(dst, c0):
        def put(act, link, psum, i):
            return act.activation(dst[:, i, c0:c0 + 256], psum[:, 0:256], ACT.Copy)
        return put

    w = a["w_in"][0]
    chunks = []
    for first, kind, put in ((gate0, "F", lambda h: put_f(xb, 2 * h, 3)), (gate0 + DA, "F", lambda h: put_f(gb, 2 * h)),
                             (0, "F", lambda h: put_f(q, 2 * h, scale=HD ** -0.5)), (DA, "F", lambda h: put_f(kf, 2 * h)),
                             (2 * DA, "T", lambda h: put_t(v, 256 * h))):
        for h in range(2):
            chunks.append(dict(src=column_chunk(w, first + 256 * h), uses=[dict(kind=kind, u=u, tokens=T, put=put(h))]))
    project(nc, k, "in1", chunks, beside=beside_in, ahead=AHEAD)

    t = [k.pair[0:NH, i, :] for i in range(2)] + [k.arena[0:NH, 23060 + 512 * i:23060 + 512 * (i + 1)] for i in range(3)]
    lru = area(8192, 4, T)
    gates_and_lru(nc, k, a, u, t[0], cum, *t[1:], xb, gb, area(0, 4, T), area(2048, 4, T), area(4096, 4, T),
                  area(6144, 4, T), lru)

    probs, turned, o = area(0, 2, T), area(1024, 2, T), area(2048, 4, T)
    units = []
    for h in range(NH):
        rows, j = slice(HD * (h % 2), HD * (h % 2) + HD), h // 2
        for t in range(TT):
            n = (t + 1) * P
            units.append(dict(
                products=[(slice(0, n), q[rows, j, t * P:n], kf[rows, j, 0:n], True, False),
                          (slice(0, n), k.neg_sel[:, h, :], cum[:, 0:n], False, False),
                          (slice(n - P, n), k.ident[:], k.causal[:], False, True)],
                bias=None, n=n, v=[v[:, g, h * HD:(h + 1) * HD] for g in range(t + 1)],
                out=o[rows, j, t * P:(t + 1) * P]))
    attention(nc, k, "at1", units, probs, turned.rearrange("p b (g n) -> p b g n", n=P), beside_attention)

    mixed = (area(12288, KD, T, F32R), area(16384, KD, T, F32R))
    norm_branches(nc, k, "nb1", [(o, "g_attn", mixed[0][:, 0:4, :], mixed[1][:, 0:4, :]),
                                 (lru, "g_lru", mixed[0][:, 4:8, :], mixed[1][:, 4:8, :])],
                  [area(4096, 4, T), area(6144, 4, T)],
                  ahead=[column_chunk(a["w_out"][0], 256 * h) for h in range(AHEAD)])
    out_projection(nc, k, "out1", a["w_out"][0], mixed, k.gate_rows[0:1, :], k.arena[:, 0:D])
    normalise(nc, k, "n1b", k.x, TT, D, k.x, True, 1e-5, gain=a["ln1_g"][0], bias=a["ln1_b"][0])


def out_projection(nc, k, name, w, mixed, gate_dram, gate):
    def put(h):
        cols = slice(256 * h, 256 * (h + 1))

        def step(dve, link, psum, i):
            tmp = quarter(k, i)
            link(dve.tensor_tensor(tmp, psum[:, 0:256], gate[:, cols], ALU.mult))
            return dve.scalar_tensor_tensor(out=k.x[:, i, cols], in0=k.x[:, i, cols], scalar=ALPHA,
                                            in1=tmp, op0=ALU.mult, op1=ALU.add)
        return step

    chunks = [dict(src=column_chunk(w, 256 * h), uses=[dict(kind="T", u=mixed, tokens=T, put=put(h))])
              for h in range(D // 256)]
    project(nc, k, name, chunks, on_dve=True, rows=(gate, gate_dram[0].partition_broadcast(P)),
            ahead=AHEAD)



def wide(ap, axis, n):
    ap = ap.unsqueeze(axis)
    shape = list(ap.shape)
    shape[axis] = n
    return ap.broadcast_to(shape)


def route(nc, k, name, u, routers, experts, top, groups):
    E, G = experts, groups
    W = E + G
    R = k.route
    NI = R.max_items + 1
    with stage(nc) as ctx:
        s = sems(nc, ctx, name, "loaded", "scored", "chain", "gexp_in", "gexp", "wexp_in", "wexp", "chosen",
                 "ranked", "slots", "listed")
        at = [0]

        def take(*shape):
            n = 1
            for x in shape:
                n *= x
            ap = k.arena[:, ROUTE_AT + at[0]:ROUTE_AT + at[0] + n]
            at[0] += n
            if len(shape) == 1:
                return ap
            letters = "abcd"[:len(shape)]
            return ap.rearrange(f"p ({' '.join(letters)}) -> p {' '.join(letters)}",
                                **{x: y for x, y in zip(letters, shape)})

        w, bias, logits = take(KD, W), take(W), take(TT, W)
        scores, hits, cand = take(TT, E), take(TT, E), take(TT, E)
        best, first, chosen = take(TT, top), take(TT), take(top, TT, E)
        total, shifted, picked = take(TT), take(TT, top), take(TT, E)
        counts, blocks, upto, start = take(E), take(E), take(E), take(E)
        pos, posf, cmp = take(TT, E), take(TT, top), take(NI, E)
        pos_i, slot_i, item_i, slot_f, item_f = (take(TT, top) for _ in range(5))
        place, dest, empty = take(TT, top), take(NI), take(NI)
        slot_hot, item_hot = take(TT * top, P), take(TT * top, NI)
        if G:
            g_hits, g_cand, g_hot, g_best, g_shift, g_total = (
                take(TT, G), take(TT, G), take(TT, G), take(TT), take(TT, G), take(TT))
        block = ctx.enter_context(nc.Block())

        @block.sync
        def _(sp):
            c = 0
            for ws, bs in routers:
                n = ws.shape[1]
                sp.dma_start(w[:, :, c:c + n], ws.rearrange("(k p) n -> p k n", p=P),
                             allow_slow_non_contiguous=True).then_inc(s.loaded, 16)
                sp.dma_start(bias[:, c:c + n], bs.partition_broadcast(P)).then_inc(s.loaded, 16)
                c += n

        @block.tensor
        def _(pe):
            pe.wait_ge(s.loaded, 32 * len(routers))
            for t in range(TT):
                for kk in range(KD):
                    ins = pe.matmul(k.psum[:, 0, t * W:(t + 1) * W], u[:, kk, t * P:(t + 1) * P], w[:, kk, :],
                                    start=kk == 0, stop=kk == KD - 1)
            ins.then_inc(s.scored, 1)
            pe.wait_ge(s.chosen, 1)
            for t in range(TT):
                for t2 in range(t + 1):
                    pe.matmul(k.psum[:, 1, t * E:(t + 1) * E], k.before[:] if t2 == t else k.ones[:],
                              picked[:, t2, :], start=t2 == 0, stop=t2 == t)
            for t in range(TT):
                ins = pe.matmul(k.psum[:, 2, 0:E], k.ones[:], picked[:, t, :], start=t == 0, stop=t == TT - 1)
            ins.then_inc(s.ranked, 1)
            pe.wait_ge(s.slots, 1)
            for m in range(TT * top):
                ins = pe.matmul(k.psum[:, 3, 0:NI], slot_hot[:, m, :], item_hot[:, m, :], start=m == 0,
                                stop=m == TT * top - 1)
            ins.then_inc(s.listed, 1)

        @block.scalar
        def _(act):
            if G:
                act.wait_ge(s.gexp_in, 1)
                act.activation(g_shift, g_shift, ACT.Exp).then_inc(s.gexp, 1)
            act.wait_ge(s.wexp_in, 1)
            act.activation(shifted, shifted, ACT.Exp).then_inc(s.wexp, 1)

        @block.vector
        def _(dve):
            link = chain(dve, s.chain)

            def first_max(src, n, high, hit, cnd, hot):
                link(dve.tensor_reduce(high, src, AX.X, ALU.max))
                link(dve.tensor_tensor(hit, src, wide(high, 2, n), ALU.is_equal))
                link(dve.scalar_tensor_tensor(out=cnd, in0=hit, scalar=-64.0, in1=wide(k.iota[:, 0:n], 1, TT),
                                              op0=ALU.mult, op1=ALU.add))
                link(dve.tensor_reduce(first, cnd, AX.X, ALU.min))
                link(dve.tensor_scalar(first, first, 64.0, None, ALU.add))
                link(dve.tensor_tensor(hot, wide(k.iota[:, 0:n], 1, TT), wide(first, 2, n), ALU.is_equal))

            dve.wait_ge(s.scored, 1)
            psum = k.psum[:, 0, 0:TT * W].rearrange("p (t w) -> p t w", t=TT)
            link(dve.tensor_tensor(logits, psum, wide(bias, 1, TT), ALU.add))
            if G:
                glog = logits[:, :, 0:G]
                first_max(glog, G, g_best, g_hits, g_cand, g_hot)
                dve.tensor_tensor(g_shift, glog, wide(g_best, 2, G), ALU.subtract).then_inc(s.gexp_in, 1)
                sel = wide(g_hot, 3, E // G)
                four = lambda x: x.rearrange("p t (g e) -> p t g e", g=G)
                for t in range(TT):
                    ins = dve.tensor_tensor(four(scores)[:, t], four(logits[:, :, G:])[:, t], sel[:, t], ALU.mult)
                link(ins)
                link(dve.tensor_scalar(g_hot, g_hot, -1.0, -NEG, ALU.add, ALU.mult))
                for t in range(TT):
                    ins = dve.tensor_tensor(four(scores)[:, t], four(scores)[:, t], sel[:, t], ALU.add)
                link(ins)
                dve.wait_ge(s.gexp, 1)
                link(dve.tensor_reduce(g_total, g_shift, AX.X, ALU.add))
            else:
                link(dve.tensor_copy(scores, logits))
            for r in range(top):
                first_max(scores, E, best[:, :, r], hits, cand, chosen[:, r])
                link(dve.scalar_tensor_tensor(out=scores, in0=chosen[:, r], scalar=3 * NEG, in1=scores,
                                              op0=ALU.mult, op1=ALU.add))
                if r == 0:
                    link(dve.tensor_copy(picked, chosen[:, 0]))
                else:
                    link(dve.tensor_tensor(picked, picked, chosen[:, r], ALU.add))
            dve.sem_inc(s.chosen, 1)
            dve.tensor_tensor(shifted, best, wide(best[:, :, 0], 2, top), ALU.subtract).then_inc(s.wexp_in, 1)
            dve.wait_ge(s.wexp, 1)
            link(dve.tensor_reduce(total, shifted, AX.X, ALU.add))
            if G:
                link(dve.tensor_tensor(total, total, g_total, ALU.mult))
            link(dve.reciprocal(total, total))
            link(dve.tensor_tensor(R.weight[:, :, 0:top], shifted, wide(total, 2, top), ALU.mult))

            dve.wait_ge(s.ranked, 1)
            link(dve.tensor_copy(counts, k.psum[:, 2, 0:E]))
            link(dve.tensor_scalar(blocks, counts, 0.0, None, ALU.is_gt))
            for n in range(1, TT):
                link(dve.scalar_tensor_tensor(out=blocks, in0=counts, scalar=float(n * P), in1=blocks,
                                              op0=ALU.is_gt, op1=ALU.add))
            link(dve.tensor_tensor_scan(upto, k.ones[:, 0:E], blocks, 0.0, ALU.mult, ALU.add))
            link(dve.tensor_tensor(start, upto, blocks, ALU.subtract))
            link(dve.tensor_scalar(start, start, float(P), None, ALU.mult))
            rank = k.psum[:, 1, 0:TT * E].rearrange("p (t e) -> p t e", t=TT)
            link(dve.tensor_tensor(pos, rank, wide(start, 1, TT), ALU.add))
            link(dve.tensor_tensor(cmp, wide(upto, 1, NI), wide(k.iota[:, 0:NI], 2, E), ALU.is_le))
            link(dve.tensor_reduce(R.expert_f[:, 0:NI], cmp, AX.X, ALU.add))
            link(dve.tensor_scalar(R.expert_f[:, 0:NI], R.expert_f[:, 0:NI], E - 1.0, None, ALU.min))
            link(dve.tensor_copy(R.expert_i[:, 0:NI], R.expert_f[:, 0:NI]))
            link(dve.tensor_scalar(upto[:, E - 1:E], upto[:, E - 1:E], 1.0, None, ALU.subtract))
            link(dve.tensor_copy(R.last[:], upto[:, E - 1:E]))
            for r in range(top):
                link(dve.tensor_tensor(cand, chosen[:, r], pos, ALU.mult))
                link(dve.tensor_reduce(posf[:, :, r], cand, AX.X, ALU.add))
            link(dve.tensor_copy(pos_i.bitcast(I32), posf))
            link(dve.tensor_scalar(slot_i.bitcast(I32), pos_i.bitcast(I32), P - 1, None, ALU.bitwise_and))
            link(dve.tensor_scalar(item_i.bitcast(I32), pos_i.bitcast(I32), 7, None, ALU.logical_shift_right))
            link(dve.tensor_copy(slot_f, slot_i.bitcast(I32)))
            link(dve.tensor_copy(item_f, item_i.bitcast(I32)))
            for r in range(top):
                ins = dve.tensor_scalar(place[:, :, r], k.token[:], 1.0 + r * T, None, ALU.add)
            link(ins)
            for t in range(TT):
                for r in range(top):
                    m = t * top + r
                    dve.tensor_scalar(slot_hot[:, m, :], k.iota[:], slot_f[:, t, r:r + 1], None, ALU.is_equal)
                    ins = dve.tensor_scalar(item_hot[:, m, :], k.iota[:, 0:NI], item_f[:, t, r:r + 1],
                                            place[:, t, r:r + 1], ALU.is_equal, ALU.mult)
            ins.then_inc(s.slots, 1)
            dve.wait_ge(s.listed, 1)
            listed = k.psum[:, 3, 0:NI]
            link(dve.tensor_scalar(dest, listed, 0.0, None, ALU.is_equal))
            link(dve.tensor_scalar(dest, dest, k.token[:, 0:1], None, ALU.mult))
            link(dve.tensor_tensor(dest, dest, listed, ALU.add))
            link(dve.tensor_scalar(empty, listed, 0.0, float(top * T + 1), ALU.is_equal, ALU.mult))
            link(dve.scalar_tensor_tensor(out=dest, in0=dest, scalar=-1.0, in1=empty, op0=ALU.add, op1=ALU.add))
            link(dve.tensor_copy(R.dest[:, 0:NI], dest))
            link(dve.tensor_scalar(R.ids[:, 0:NI], R.dest[:, 0:NI], T - 1, None, ALU.bitwise_and))



Experts = namedtuple("Experts", "width experts first second down bias down_bias swiglu whole x y")


def experts(nc, k, name, m):
    R = k.route
    FK = m.width // P
    A, C = m.first, m.second
    nA, nC, nB = 2 * len(A), 2 * len(C), FK // 2
    PER = nA + nB + nC
    WHOLE = m.whole
    HT_BEFORE = nA - 1
    biased = m.bias is not None

    at = [0]

    def take(n, rounded=False, rows=P):
        at[0] += n
        return (k.arena_r if rounded else k.arena)[0:rows, at[0] - n:at[0]]

    def tiles(n, rounded=False):
        return take(n * P, rounded).rearrange("p (k n) -> p k n", k=n)

    xg = take(D)
    xw = [tiles(KD) for _ in range(2)]
    x_hi, x_lo = [tiles(KD, True) for _ in range(2)], [tiles(KD, True) for _ in range(2)]
    h = take(m.width)
    gate, sig, prod = (take(512) for _ in range(3))
    h_hi, h_lo = tiles(FK, True), tiles(FK, True)
    ysb = take(D).rearrange("p (h n) -> p h n", h=2)
    idx, to_row = take(1).bitcast(I32), take(1).bitcast(I32)
    if biased:
        columns = sum(b.shape[1] for b in m.bias)
        bias_hl = take(columns, True, 64)
        bias_raw = [k.rows[0:64].rearrange("p a d -> p (a d)"), k.pair[0:64].rearrange("p a d -> p (a d)")]
        sel_up, sel_down = [take(P, True, 64) for _ in range(2)], take(P, True, 64)
    more_hi = [take(CHUNK, True) for _ in range(SLOTS - HI_SLOTS)]
    assert at[0] <= ARENA
    FIRST = SLOTS
    UP, YB, TB = 0, 4, 6

    with stage(nc) as ctx:
        s = sems(nc, ctx, name, "idx", "to_row", "settled", "gathered", "x_turned", "x_whole", "x_hi", "x_lo", "clipped", "part_read",
                 "prod_done", "sig", "h_part", "h_turned", "h_hi", "h_lo", "y_put", "y_stored", "y_free", "bias", "bias_hi",
                 "bias_lo", "sel_up", "sel_down")
        ss = stream_sems(nc, ctx, name, k, offset=FIRST, more_hi=more_hi)
        block = ctx.enter_context(nc.Block())
        PAIRS = (R.max_items - 1) // 2

        def chunks(j, groups, c0):
            return [(c0 + 2 * g + kh, g, kh) for g in range(len(groups)) for kh in range(2)]


        @block.sync
        def _(sp):
            if biased:
                for half in range(2):
                    for b, raw in zip(m.bias, bias_raw):
                        sp.dma_start(raw[32 * half:32 * half + b.shape[0], :], b).then_inc(s.bias, 16)

            def up(e, groups, c0, per, j):
                for c, g, kh in chunks(j, groups, c0):
                    _, w, first, _ = groups[g]
                    src = w[bass.ds(e, 1), kh * 512:(kh + 1) * 512, first:first + 512]
                    load_chunk(sp, k, ss, src.rearrange("a (k p) n -> p (a k) n", p=P), c, per, j)

            def down(e, c0, per, j):
                for q in range(nB):
                    src = m.down[bass.ds(e, 1), q * 256:(q + 1) * 256, :]
                    load_chunk(sp, k, ss, src.rearrange("a (k p) n -> p (a k) n", p=P), c0 + q, per, j)

            def expert(j):
                return sp.value_load(R.expert_i[0:1, bass.ds(j, 1)], min_val=0, max_val=m.experts - 1)

            n = sp.value_load(R.last[0:1, 0:1], min_val=0, max_val=R.max_items - 1) + 1
            e = expert(0)
            up(e, A, 0, 0, 0)
            up(e, C, nA, 0, 0)
            with sp.Fori(0, PAIRS) as i:
                for p in (1, 2):
                    j = 2 * i + p
                    with sp.If(j < n):
                        e = expert(j)
                        up(e, A, -nB, PER, j)
                        down(expert(j - 1), nA - nB, PER, j)
                        up(e, C, nA, PER, j)
            down(expert(n - 1), -nB, PER, n)

        @block.gpsimd
        def _(pool):
            n = pool.value_load(R.last[0:1, 0:1], min_val=0, max_val=R.max_items - 1) + 1

            def gather(j, first=False):
                if not first:
                    pool.wait_ge(s.gathered, 16 * j)
                pool.tensor_copy(idx, R.ids[:, bass.ds(j, 1)]).then_inc(s.idx, 1)
                pool.wait_ge(s.idx, j + 1)
                if not first:
                    pool.wait_ge(s.x_turned, j)
                pool.sem_inc(s.settled, 1)
                pool.indirect_dma_start(xg, None, m.x, bass.IndirectOffsetOnAxis(ap=idx.bitcast(U32), axis=0)
                                        ).then_inc(s.gathered, 16)

            def scatter(j):
                pool.tensor_copy(to_row, R.dest[:, bass.ds(j, 1)]).then_inc(s.to_row, 1)
                pool.wait_ge(s.to_row, j + 1)
                pool.wait_ge(s.y_put, j + 2)
                pool.sem_inc(s.settled, 1)
                pool.indirect_dma_start(m.y, bass.IndirectOffsetOnAxis(ap=to_row.bitcast(U32), axis=0),
                                        ysb.rearrange("p h n -> p (h n)"), None).then_inc(s.y_stored, 16)
                pool.wait_ge(s.y_stored, 16 * j + 16)
                pool.sem_inc(s.y_free, 1)

            pool.sem_inc(s.y_put, 1)
            pool.sem_inc(s.y_free, 1)
            gather(0, True)
            gather(1)
            with pool.Fori(0, PAIRS) as i:
                for p in (1, 2):
                    j = 2 * i + p
                    with pool.If(j < n):
                        gather(j + 1)
                        scatter(j - 1)
            scatter(n - 1)

        @block.tensor
        def _(pe):
            n = pe.value_load(R.last[0:1, 0:1], min_val=0, max_val=R.max_items - 1) + 1

            def turn_x(j, first=False):
                pe.wait_ge(s.gathered, 16 * j + 16)
                if not first:
                    pe.wait_ge(s.h_lo, j - 1)
                    pe.wait_ge(s.x_whole, j)
                for kk in range(KD):
                    ins = pe.transpose(k.psum[:, TB + kk // 4, (kk % 4) * P:(kk % 4 + 1) * P],
                                       xg[:, kk * P:(kk + 1) * P], k.ident[:])
                ins.then_inc(s.x_turned, 1)

            def turn_h(j):
                pe.wait_ge(s.h_part, len(A) * j + len(A))
                pe.wait_ge(s.x_whole, j + 2)
                for kk in range(FK):
                    ins = pe.transpose(k.psum[:, TB + kk // 4, (kk % 4) * P:(kk % 4 + 1) * P],
                                       h[:, kk * P:(kk + 1) * P], k.ident[:])
                ins.then_inc(s.h_turned, 1)

            def up(p, groups, c0, per, j, before=None):
                for c, g, kh in chunks(j, groups, c0):
                    if before is not None and c - c0 == HT_BEFORE:
                        before()
                    bank, _, _, bias_col = groups[g]
                    w = chunk_halves(pe, k, ss, c, 512, per, j)
                    out = k.psum[:, UP + bank, :]
                    if kh == 0 and biased:
                        pe.matmul(out, sel_up[p], bias_hl[:, bias_col:bias_col + 512], start=True, stop=False)
                    for kk in range(4):
                        kd = 4 * kh + kk
                        if c in WHOLE:
                            raw = ss.raw[c % SLOTS][:, kk * 512:(kk + 1) * 512]
                            ins = pe.matmul(out, xw[p][:, kd, :], raw, start=kd == 0 and not biased, stop=kd == KD - 1)
                            continue
                        ins = split3(pe, out, (x_hi[p][:, kd, :], x_lo[p][:, kd, :]), [x[:, kk, :] for x in w],
                                     kd == 0 and not biased, kd == KD - 1)
                    ins.then_inc(ss.chunk_used, 1)

            def down(j, c0, per, jj):
                pe.wait_ge(s.h_lo, jj)
                for q in range(nB):
                    w = chunk_halves(pe, k, ss, c0 + q, D, per, jj)
                    if q == 0:
                        pe.wait_ge(s.y_put, j + 1)
                        if biased:
                            pe.wait_ge(s.sel_down, jj)
                            for hf in range(2):
                                pe.matmul(k.psum[:, YB + hf, :], sel_down,
                                          bias_hl[:, m.down_bias + 512 * hf:m.down_bias + 512 * hf + 512],
                                          start=True, stop=False)
                    for kk in range(2):
                        kf = 2 * q + kk
                        for hf in range(2):
                            ins = split3(pe, k.psum[:, YB + hf, :], (h_hi[:, kf, :], h_lo[:, kf, :]),
                                         [x[:, kk, hf * 512:(hf + 1) * 512] for x in w],
                                         kf == 0 and not biased, kf == FK - 1)
                    ins.then_inc(ss.chunk_used, 1)

            turn_x(0, True)
            pe.wait_ge(s.x_lo, 1)
            if biased:
                pe.wait_ge(s.bias_lo, 2)
                pe.wait_ge(s.sel_up, 1)
            up(0, A, 0, 0, 0)
            pe.wait_ge(s.gathered, 32)
            pe.wait_ge(s.x_whole, 1)
            for kk in range(KD):
                ins = pe.transpose(k.psum[:, TB + kk // 4, (kk % 4) * P:(kk % 4 + 1) * P],
                                   xg[:, kk * P:(kk + 1) * P], k.ident[:])
            ins.then_inc(s.x_turned, 1)
            up(0, C, nA, 0, 0)
            with pe.Fori(0, PAIRS) as i:
                for p in (1, 2):
                    j = 2 * i + p
                    with pe.If(j < n):
                        pe.wait_ge(s.x_lo, j + 1)
                        pe.wait_ge(s.part_read, 2 * j - 1)
                        if biased:
                            pe.wait_ge(s.sel_up, j + 1)
                        up(p % 2, A, -nB, PER, j, before=lambda: turn_h(j - 1))
                        down(j - 1, nA - nB, PER, j)
                        turn_x(j + 1)
                        pe.wait_ge(s.part_read, 2 * j)
                        up(p % 2, C, nA, PER, j)
            turn_h(n - 1)
            down(n - 1, -nB, PER, n)

        @block.scalar
        def _(act):
            n = act.value_load(R.last[0:1, 0:1], min_val=0, max_val=R.max_items - 1) + 1

            def read_x(j, p, free=True):
                act.wait_ge(s.x_turned, j + 1)
                if free:
                    act.wait_ge(s.x_lo, j)
                for hf in range(2):
                    ins = act.activation(xw[p][:, 4 * hf:4 * hf + 4, :].rearrange("p k n -> p (k n)"),
                                         k.psum[:, TB + hf, :], ACT.Copy)
                ins.then_inc(s.x_whole, 1)
                act.wait_ge(s.x_whole, j + 1)
                act.activation(x_hi[p].rearrange("p k n -> p (k n)"), xw[p].rearrange("p k n -> p (k n)"),
                               ACT.Copy).then_inc(s.x_hi, 1)

            def sigmoid(j, half, free=True):
                q = len(A) * j + half
                if m.swiglu:
                    act.wait_ge(s.clipped, q + 1)
                    if free:
                        act.wait_ge(s.h_part, q)
                    act.activation(sig, gate, ACT.Sigmoid, scale=1.702).then_inc(s.sig, 1)
                else:
                    if free:
                        act.wait_ge(s.part_read, 2 * j)
                    act.activation(sig, k.psum[:, UP, :], ACT.Sigmoid).then_inc(s.sig, 1)

            def read_h(j):
                act.wait_ge(s.h_turned, j + 1)
                for hf in range(FK // 4):
                    ins = act.activation(h_hi[:, 4 * hf:4 * hf + 4, :].rearrange("p k n -> p (k n)"),
                                         k.psum[:, TB + hf, :], ACT.Copy)
                ins.then_inc(s.h_hi, 1)

            def put_y(j, free=True):
                if free:
                    act.wait_ge(s.y_free, j + 1)
                for hf in range(2):
                    ins = act.activation(ysb[:, hf, :], k.psum[:, YB + hf, :], ACT.Copy)
                ins.then_inc(s.y_put, 1)

            read_x(0, 0, False)
            for c in range(nA + nC):
                make_hi(act, k, ss, c, whole=c in WHOLE)
                if c == nA - 1:
                    read_x(1, 1)
                if c == nA + 1 and not m.swiglu:
                    act.wait_ge(ss.chunk_used, FIRST + nA)
                    sigmoid(0, 0, False)
                if c == nA + 2 and m.swiglu:
                    sigmoid(0, 0, False)
            with act.Fori(0, PAIRS) as i:
                for p in (1, 2):
                    j = 2 * i + p
                    with act.If(j < n):
                        for l in range(PER):
                            c = l - nB
                            make_hi(act, k, ss, c, PER, j, c in WHOLE)
                            if m.swiglu and l == 1:
                                sigmoid(j - 1, 1)
                            if l == HT_BEFORE + 1:
                                read_h(j - 1)
                            if l == nA + 2:
                                if m.swiglu:
                                    sigmoid(j, 0)
                                else:
                                    act.wait_ge(ss.chunk_used, PER * j + (FIRST - nB + nA))
                                    sigmoid(j, 0)
                        act.wait_ge(ss.chunk_used, PER * j + (FIRST + nA))
                        put_y(j - 1)
                        read_x(j + 1, (p + 1) % 2)
            if m.swiglu:
                sigmoid(n - 1, 1)
            make = [make_hi(act, k, ss, -nB + q, PER, n) for q in range(min(nB, HI_SLOTS))]
            read_h(n - 1)
            for q in range(len(make), nB):
                make_hi(act, k, ss, -nB + q, PER, n)
            act.wait_ge(ss.chunk_used, PER * n + FIRST)
            put_y(n - 1)

        @block.vector
        def _(dve):
            n = dve.value_load(R.last[0:1, 0:1], min_val=0, max_val=R.max_items - 1) + 1

            def select(dst, j, sem):
                dve.tensor_scalar(dst, wide(k.half_row[:, 0], 1, P), R.expert_f[0:64, bass.ds(j, 1)], None,
                                  ALU.is_equal).then_inc(sem, 1)

            def lo_x(j, p):
                dve.wait_ge(s.x_hi, j + 1)
                dve.tensor_tensor(x_lo[p], xw[p], x_hi[p].bitcast(F32), ALU.subtract).then_inc(s.x_lo, 1)

            def lo_h(j):
                dve.wait_ge(s.h_hi, j + 1)
                for hf in range(FK // 4):
                    part = slice(4 * hf, 4 * hf + 4)
                    ins = dve.tensor_tensor(h_lo[:, part, :].rearrange("p k n -> p (k n)"), k.psum[:, TB + hf, :],
                                            h_hi[:, part, :].rearrange("p k n -> p (k n)").bitcast(F32), ALU.subtract)
                ins.then_inc(s.h_lo, 1)

            def clip(j, half, used):
                dve.wait_ge(ss.chunk_used, used + FIRST)
                q = 2 * j + half
                dve.tensor_scalar(gate, k.psum[:, UP + 2 * half, :], 7.0, None, ALU.min).then_inc(s.clipped, 1)
                dve.tensor_scalar(prod, k.psum[:, UP + 2 * half + 1, :], 7.0, -7.0, ALU.min,
                                  ALU.max).then_inc(s.part_read, 1)
                dve.wait_ge(s.part_read, q + 1)
                dve.scalar_tensor_tensor(out=prod, in0=prod, scalar=1.0, in1=gate, op0=ALU.add,
                                         op1=ALU.mult).then_inc(s.prod_done, 1)

            def glu(j, half):
                q = 2 * j + half
                dve.wait_ge(s.sig, q + 1)
                dve.wait_ge(s.prod_done, q + 1)
                dve.tensor_tensor(h[:, 512 * half:512 * half + 512], prod, sig, ALU.mult).then_inc(s.h_part, 1)

            def silu_gate(j):
                dve.wait_ge(s.sig, j + 1)
                dve.tensor_tensor(prod, k.psum[:, UP, :], sig, ALU.mult).then_inc(s.part_read, 1)

            def silu_up(j, used):
                dve.wait_ge(ss.chunk_used, used + FIRST)
                dve.wait_ge(s.part_read, 2 * j + 1)
                dve.tensor_tensor(h, prod, k.psum[:, UP + 1, :], ALU.mult).then_inc(s.part_read, 1)
                dve.wait_ge(s.part_read, 2 * j + 2)
                dve.sem_inc(s.h_part, 1)

            dve.sem_inc(ss.chunk_used, FIRST)
            if biased:
                dve.wait_ge(s.bias, 32 * len(m.bias))
                parts, c = [], 0
                for raw in bias_raw:
                    parts.append((bias_hl[:, c:c + raw.shape[1]], raw))
                    c += raw.shape[1]
                for i, (part, raw) in enumerate(parts):
                    dve.tensor_copy(part, raw).then_inc(s.bias_hi, 1)
                    dve.wait_ge(s.bias_hi, i + 1)
                    dve.tensor_tensor(part[32:64, :], raw[32:64, :], part[32:64, :].bitcast(F32),
                                      ALU.subtract).then_inc(s.bias_lo, 1)
                select(sel_up[0], 0, s.sel_up)
                select(sel_up[1], 1, s.sel_up)
            lo_x(0, 0)
            for c in range(nA + nC):
                make_lo(dve, k, ss, c, whole=c in WHOLE)
                if c == nA - 1:
                    lo_x(1, 1)
                if c == nA + 1:
                    if m.swiglu:
                        clip(0, 0, nA)
                    else:
                        silu_gate(0)
                if c == nA + 2 and m.swiglu:
                    glu(0, 0)
            with dve.Fori(0, PAIRS) as i:
                for p in (1, 2):
                    j = 2 * i + p
                    with dve.If(j < n):
                        for l in range(PER):
                            c = l - nB
                            make_lo(dve, k, ss, c, PER, j, c in WHOLE)
                            if l == 1:
                                if m.swiglu:
                                    clip(j - 1, 1, PER * j - nB)
                                    glu(j - 1, 1)
                                else:
                                    silu_up(j - 1, PER * j - nB)
                                if biased:
                                    select(sel_down, j - 1, s.sel_down)
                            if l == HT_BEFORE + 1:
                                lo_h(j - 1)
                            if l == nA + 2:
                                if m.swiglu:
                                    clip(j, 0, PER * j - nB + nA)
                                    glu(j, 0)
                                else:
                                    silu_gate(j)
                        if biased:
                            select(sel_up[(p + 1) % 2], j + 1, s.sel_up)
                        lo_x(j + 1, (p + 1) % 2)
            if m.swiglu:
                clip(n - 1, 1, PER * n - nB)
                glu(n - 1, 1)
            else:
                silu_up(n - 1, PER * n - nB)
            if biased:
                select(sel_down, n - 1, s.sel_down)
            done = min(nB, HI_SLOTS)
            for q in range(done):
                make_lo(dve, k, ss, -nB + q, PER, n)
            lo_h(n - 1)
            for q in range(done, nB):
                make_lo(dve, k, ss, -nB + q, PER, n)


def combine(nc, k, name, top, y, gate_dram=None):
    R = k.route
    NB = 4
    total = k.arena[:, 0:TT * D].rearrange("p (t d) -> p t d", t=TT)
    got = k.arena[:, TT * D:TT * D + NB * D].rearrange("p (b d) -> p b d", b=NB)
    gate = k.rows[:, 0, :]
    with stage(nc) as ctx:
        s = sems(nc, ctx, name, "rows", "added", "chain")
        landed_y = [nc.alloc_semaphore(name=(f"{name}_y{i}")) for i in range(NB)]
        block = ctx.enter_context(nc.Block())

        @block.sync
        def _(sp):
            if gate_dram is not None:
                sp.dma_start(gate, gate_dram[0].partition_broadcast(P)).then_inc(s.rows, 16)
            for m in range(TT * top):
                t, r = m // top, m % top
                if m >= NB:
                    sp.wait_ge(s.added, m - NB + 1)
                sp.dma_start(got[:, m % NB, :], y[r * T + t * P:r * T + (t + 1) * P, :]).then_inc(landed_y[m % NB], 16)

        @block.vector
        def _(dve):
            link = chain(dve, s.chain)
            if gate_dram is not None:
                dve.wait_ge(s.rows, 16)
            for t in range(TT):
                for r in range(top):
                    m = t * top + r
                    dve.wait_ge(landed_y[m % NB], 16 * (m // NB + 1))
                    wt = R.weight[:, t, r:r + 1]
                    if r:
                        dve.wait_ge(s.added, m)
                        dve.scalar_tensor_tensor(out=total[:, t, :], in0=got[:, m % NB, :], scalar=wt,
                                                 in1=total[:, t, :], op0=ALU.mult, op1=ALU.add).then_inc(s.added, 1)
                    else:
                        dve.tensor_scalar(total[:, t, :], got[:, m % NB, :], wt, None, ALU.mult).then_inc(s.added, 1)
                if gate_dram is not None:
                    dve.wait_ge(s.added, (t + 1) * top)
                    link(dve.tensor_tensor(total[:, t, :], total[:, t, :], gate, ALU.mult))
                    dve.scalar_tensor_tensor(out=k.x[:, t, :], in0=k.x[:, t, :], scalar=ALPHA, in1=total[:, t, :],
                                             op0=ALU.mult, op1=ALU.add)


def moe_inputs(nc, k, name, centre, eps, scale, shift):
    xn = k.arena[:, 0:TT * D].rearrange("p (t d) -> p t d", t=TT)
    u = k.arena[:, TT * D:2 * TT * D].rearrange("p (k n) -> p k n", k=KD)
    normalise(nc, k, name + "n", k.x, TT, D, xn, centre, eps, gain=scale, bias=shift,
              store=[k.xn_dram[t * P:(t + 1) * P, :] for t in range(TT)])
    turn(nc, k, name + "t", xn, TT, KD, None, None, None, None, plain=u)
    return u


def block_one_moe(nc, k, a):
    u = moe_inputs(nc, k, "m1", True, 1e-5, k.gate_rows[5], k.gate_rows[4])
    k.route.max_items = 23
    route(nc, k, "r1", u, [(a["w_grp"][0], a["b_grp"][0]), (a["w_exp"][0], a["b_exp"][0])], 16, 2, 4)
    m = Experts(width=512, experts=16, first=[(0, a["w_e_gate"][0], 0, 0)],
                        second=[(1, a["w_e_up"][0], 0, 0)], down=a["w_e_down"][0], bias=None, down_bias=None, swiglu=False, whole=(),
                        x=k.xn_dram, y=k.y_dram)
    experts(nc, k, "e1", m)
    combine(nc, k, "c1", 2, k.y_dram, k.gate_rows[1:2, :])
    normalise(nc, k, "n1c", k.x, TT, D, k.x, True, 1e-5, gain=a["ln2_g"][0], bias=a["ln2_b"][0])



GRID_W = 64
GRID_H = T // GRID_W
WIN_R, WIN_C = 8, 16
RPB_R, RPB_C = 2 * WIN_R - 1, 2 * WIN_C - 1
RPB_PAD = 64
RPB_SIZE = NH * RPB_R * RPB_C + 2 * RPB_PAD
NDR = 14
KV = 128
ROT = HD // 4


def constants():
    import numpy as np
    t = np.arange(T)
    freq = np.float32(10000.0) ** (-np.arange(ROT, dtype=np.float32) / np.float32(ROT))
    angle = np.stack([t // GRID_W, t % GRID_W], 1).astype(np.float32)[:, :, None] * freq
    return {"cos_table": np.cos(angle).astype(np.float32), "sin_table": np.sin(angle).astype(np.float32)}


def load_tiles(nc, k, name, loads):
    with stage(nc) as ctx:
        s = sems(nc, ctx, name, "loaded")
        block = ctx.enter_context(nc.Block())

        @block.sync
        def _(sp):
            for dst, src in loads:
                sp.dma_start(dst, src).then_inc(s.loaded, 16)
            sp.wait_ge(s.loaded, 16 * len(loads))


def rotate_heads(nc, k, name, src, heads, ntt, n_rot, gain, scale, outs, scratch, tables):
    n = ntt * heads
    with stage(nc) as ctx:
        s = sems(nc, ctx, name, "loaded", "chain", "mean", "root")
        g = k.small[:, 0:HD]
        mean, rstd = k.small[:, HD:HD + n], scratch[:, 0:n]
        squares = scratch[:, 64:64 + n * HD].rearrange("p (m d) -> p m d", d=HD)
        cos, sin = tables
        flat = src.rearrange("p t h d -> p (t h) d")
        block = ctx.enter_context(nc.Block())

        @block.sync
        def _(sp):
            sp.dma_start(g, gain.partition_broadcast(P)).then_inc(s.loaded, 16)

        @block.scalar
        def _(act):
            act.wait_ge(s.mean, 1)
            act.activation(rstd, mean, ACT.Sqrt).then_inc(s.root, 1)

        @block.vector
        def _(dve):
            link = chain(dve, s.chain)
            link(dve.tensor_tensor(squares, flat, flat, ALU.mult))
            link(dve.tensor_reduce(mean, squares, AX.X, ALU.add))
            link(dve.tensor_scalar(mean, mean, 1.0 / HD, 1e-6, ALU.mult, ALU.add))
            dve.reciprocal(mean, mean).then_inc(s.mean, 1)
            dve.wait_ge(s.root, 1)
            link(dve.tensor_scalar(rstd, rstd, scale, None, ALU.mult))
            link(dve.tensor_tensor(flat, flat, wide(rstd, 2, HD), ALU.mult))
            dve.wait_ge(s.loaded, 16)
            link(dve.tensor_tensor(flat, flat, wide(g, 1, n), ALU.mult))
            q = n * HD // 4
            for t in range(ntt):
                for h0, count, dst in outs:
                    x = src[:, t, h0:h0 + count, :]
                    if t >= n_rot:
                        dve.tensor_copy(dst(t), x)
                        continue
                    v = x.rearrange("p h (a s f) -> p h a s f", a=2, s=2)
                    o = dst(t).rearrange("p h (a s f) -> p h a s f", a=2, s=2)
                    c, sn = wide(cos[:, t], 1, count), wide(sin[:, t], 1, count)
                    w = count * 2 * ROT
                    p1, p2, p3, p4 = (scratch[:, 64 + i * w:64 + (i + 1) * w].rearrange(
                        "p (h a f) -> p h a f", h=count, a=2) for i in range(4))
                    dve.tensor_tensor(p1, v[:, :, :, 0], c, ALU.mult)
                    dve.tensor_tensor(p2, v[:, :, :, 1], sn, ALU.mult)
                    dve.tensor_tensor(p3, v[:, :, :, 1], c, ALU.mult)
                    link(dve.tensor_tensor(p4, v[:, :, :, 0], sn, ALU.mult))
                    dve.tensor_tensor(o[:, :, :, 0], p1, p2, ALU.subtract)
                    link(dve.tensor_tensor(o[:, :, :, 1], p3, p4, ALU.add))


def neighbour_bias(nc, k, a, table, mask):
    size = NH * RPB_R * RPB_C
    zeros = k.small[0:1, 0:RPB_PAD]
    with stage(nc) as ctx:
        s = sems(nc, ctx, "nb", "zero", "padded", "chain", "masked", "reversed", "read")
        loaded = [nc.alloc_semaphore(name=f"nb_loaded{h}") for h in range(NH)]
        flip = k.pair[:, 0, 0:P]
        span = NDR * GRID_W // 2
        block = ctx.enter_context(nc.Block())

        @block.gpsimd
        def _(pool):
            link = chain(pool, s.chain)
            pool.memset(zeros, 0.0).then_inc(s.zero, 1)
            link(pool.memset(flip, 0.0))
            link(pool.affine_select(out=flip, in_=flip, compare_op=ALU.not_equal, fill=1.0, base=1 - P,
                                    pattern=[[1, P]], channel_multiplier=1))
            link(pool.memset(mask, 0.0))
            for half in range(2):
                rows = slice(64 * half, 64 * half + 64)
                left = mask[rows, 0:GRID_W - WIN_C]
                link(pool.affine_select(out=left, in_=left, compare_op=ALU.is_ge, fill=NEG, base=WIN_C // 2,
                                        pattern=[[1, GRID_W - WIN_C]], channel_multiplier=-1))
                right = mask[rows, WIN_C:GRID_W]
                ins = pool.affine_select(out=right, in_=right, compare_op=ALU.is_ge, fill=NEG,
                                         base=WIN_C // 2 - 1 - WIN_C, pattern=[[-1, GRID_W - WIN_C]],
                                         channel_multiplier=1)
                if half == 0:
                    link(ins)
            ins.then_inc(s.masked, 1)

        @block.sync
        def _(sp):
            sp.wait_ge(s.zero, 1)
            pad = k.rpb_pad.rearrange("(o n) -> o n", o=1)
            sp.dma_start(pad[:, 0:RPB_PAD], zeros).then_inc(s.padded, 16)
            sp.dma_start(pad[:, RPB_PAD + size:], zeros).then_inc(s.padded, 16)
            sp.dma_start(pad[:, RPB_PAD:RPB_PAD + size], a["rpb_2"].rearrange("o h r c -> o (h r c)")).then_inc(s.padded, 16)
            sp.wait_ge(s.padded, 48)
            for h in range(NH):
                for half in range(2):
                    first = RPB_PAD + (h * RPB_R + 1 - half) * RPB_C + WIN_C - 1 - (GRID_W - 1)
                    src = bass.AP(k.rpb_pad.tensor, first, [[1, GRID_W], [RPB_C, NDR], [1, GRID_W]])
                    sp.dma_start(table[64 * (1 - half):64 * (1 - half) + 64, h], src).then_inc(loaded[h], 16)

        @block.tensor
        def _(pe):
            pe.wait_ge(s.masked, 1)
            flat = table.rearrange("p h j c -> p (h j c)")
            for m in range(2 * NH):
                if m % 2 == 0:
                    pe.wait_ge(loaded[m // 2], 32)
                if m >= 4:
                    pe.wait_ge(s.read, m - 3)
                pe.matmul(k.psum[:, m % 4, 0:span], flip, flat[:, m * span:(m + 1) * span],
                          start=True, stop=True).then_inc(s.reversed, 1)

        @block.vector
        def _(dve):
            flat = table.rearrange("p h j c -> p (h j) c")
            rows = NDR // 2
            for m in range(2 * NH):
                dve.wait_ge(s.reversed, m + 1)
                dve.tensor_tensor(flat[:, m * rows:(m + 1) * rows, :],
                                  k.psum[:, m % 4, 0:span].rearrange("p (j c) -> p j c", c=GRID_W),
                                  wide(mask, 1, rows), ALU.add).then_inc(s.read, 1)


def block_two_mixer(nc, k, a):
    def area(first, n, cols, dtype=F32):
        t = (k.arena if dtype is F32 else k.arena_r)[:, first:first + n * cols]
        return t.rearrange("p (a b) -> p a b", a=n)

    xn = area(0, TT, D)
    u = (area(4096, KD, T, F32R), area(8192, KD, T, F32R))
    normalise(nc, k, "n2", k.x, TT, D, xn, False, 1e-6)
    turn(nc, k, "t2", xn, TT, KD, k.mod["sc1_2"], k.mod["sh1_2"], *u)
    ctx_x, ctx_n = area(0, TC, D), area(2048, TC, D)
    uc = (area(12288, KD, CTX, F32R), area(14336, KD, CTX, F32R))
    load_tiles(nc, k, "ctx", [(ctx_x, a["ctx_2"].rearrange("o (t p) d -> p (o t) d", p=P))])
    normalise(nc, k, "n2c", ctx_x, TC, D, ctx_n, False, 1e-6)
    turn(nc, k, "t2c", ctx_n, TC, KD, k.mod["scc"], k.mod["shc"], *uc,
         ahead=[column_chunk(a["w_in_2"][0], 256 * h) for h in range(AHEAD)])

    KEYS = T + CTX
    ka, va, kvb = area(16384, 4, KEYS), area(19456, TT + TC, DA), area(22528, TT + TC, 2 * KV)
    qa, qb = area(0, 4, T), area(2048, TT, DA)

    def use_f(dst, j0, first, uu, tokens, scale=1.0):
        return dict(kind="F", u=uu, tokens=tokens, put=lambda act, link, psum, i: act.activation(
            dst[:, j0 + i, first:first + tokens], psum[:, 0:tokens], ACT.Copy, scale=scale))

    def use_t(dst, t0, c0, uu, tokens):
        return dict(kind="T", u=uu, tokens=tokens, put=lambda act, link, psum, i: act.activation(
            dst[:, t0 + i, c0:c0 + 256], psum[:, 0:256], ACT.Copy))

    staged = [0]

    def use_gate(branch, c0):
        def put(act, link, psum, i):
            staged[0] += 1
            return act.activation(quarter(k, staged[0] - 1), psum[:, 0:256], ACT.Sigmoid)
        return dict(kind="T", u=u, tokens=T, put=put,
                    store=lambda i: k.branch_gates[branch, i * P:(i + 1) * P, c0:c0 + 256])

    w = a["w_in_2"][0]
    at, chunks = 0, []
    for h in range(2):
        chunks.append((at + 256 * h, [use_f(ka, 2 * h, 0, u, T), use_f(ka, 2 * h, T, uc, CTX)]))
    at += DA
    for h in range(2):
        chunks.append((at + 256 * h, [use_t(va, 0, 256 * h, u, T), use_t(va, TT, 256 * h, uc, CTX)]))
    at += DA
    chunks.append((at, [use_t(kvb, 0, 0, u, T), use_t(kvb, TT, 0, uc, CTX)]))
    at += 2 * KV
    for h in range(2):
        chunks.append((at + 256 * h, [use_f(qa, 2 * h, 0, u, T, HD ** -0.5)]))
    at += DA
    for h in range(2):
        chunks.append((at + 256 * h, [use_t(qb, 0, 256 * h, u, T)]))
    at += DA
    for branch in range(2):
        for h in range(4):
            chunks.append((at + branch * D + 256 * h, [use_gate(branch, 256 * h)]))
    project(nc, k, "in2", [dict(src=column_chunk(w, c), uses=uses) for c, uses in chunks], ahead=AHEAD)

    tables = [k.arena[:, 4096 + 128 * i:4224 + 128 * i].rearrange("p (t a f) -> p t a f", t=TT, a=2) for i in range(2)]
    load_tiles(nc, k, "rot", [(t, a[n].rearrange("(t p) a f -> p t a f", p=P))
                              for t, n in zip(tables, ("cos_table", "sin_table"))])
    qr, kr = area(4608, TT, DA), area(6656, TT + TC, KV)
    scratch = k.arena[:, 7424:7424 + 4096]
    q_kv = qr.rearrange("p t (m g d) -> p t g m d", m=4, g=2)
    rotate_heads(nc, k, "rq", qb.rearrange("p t (h d) -> p t h d", d=HD), NH, TT, TT, a["g_qnorm_2"][0], HD ** -0.5,
                 [(4 * g, 4, lambda t, g=g: q_kv[:, t, g]) for g in range(2)], scratch, tables)
    kc = area(11520, TT + TC, KV)
    copy_tiles(nc, k, "kc", kc, kvb[:, :, 0:KV])
    rotate_heads(nc, k, "rk", kc.rearrange("p t (h d) -> p t h d", d=HD), 2, TT + TC, TT, a["g_knorm_2"][0], 1.0,
                 [(0, 2, lambda t: kr[:, t, :].rearrange("p (h d) -> p h d", d=HD))], scratch, tables)
    qbt, kbt = area(11520, 4, T), area(13568, 1, KEYS)
    turn(nc, k, "tq", qr, TT, 4, None, None, None, None, plain=qbt)
    turn(nc, k, "tk", kr[:, 0:TT], TT, 1, None, None, None, None, plain=kbt[:, :, 0:T])
    turn(nc, k, "tkc", kr[:, TT:], TC, 1, None, None, None, None, plain=kbt[:, :, T:])

    table = k.arena[:, 4096:4096 + NH * NDR * GRID_W].rearrange("p (h j c) -> p h j c", h=NH, j=NDR)
    neighbour_bias(nc, k, a, table, k.arena[:, 11264:11264 + GRID_W])
    oa, ob = area(14336, 4, T), area(4096, 4, T)
    probs = k.rows[:, :, 0:KEYS]
    turned = k.arena[:, 2048:2048 + 2 * KEYS].rearrange("p (b g n) -> p b g n", b=2, n=P)
    units = []
    for h in range(NH):
        rows, j = slice(HD * (h % 2), HD * (h % 2) + HD), h // 2
        for t in range(TT):
            q = qa[rows, j, t * P:(t + 1) * P]
            first = NDR - GRID_H - 2 * t
            units.append(dict(
                products=[(slice(0, T), q, ka[rows, j, 0:T], True, True),
                          (slice(T, KEYS), q, ka[rows, j, T:KEYS], True, True)],
                bias=table[:, h, first:first + GRID_H, :].rearrange("p j c -> p (j c)"), n=KEYS,
                v=[va[:, g, h * HD:(h + 1) * HD] for g in range(TT + TC)], out=oa[rows, j, t * P:(t + 1) * P]))
    attention(nc, k, "na", units, probs, turned)

    units = []
    for h in range(NH):
        kv = h // 4
        rows = slice(HD * kv, HD * kv + HD)
        for t in range(TT):
            q = qbt[rows, h % 4, t * P:(t + 1) * P]
            units.append(dict(
                products=[(slice(0, T), q, kbt[rows, 0, 0:T], True, True),
                          (slice(T, KEYS), q, kbt[rows, 0, T:KEYS], True, True)],
                bias=None, n=KEYS, v=[kvb[:, g, KV + HD * kv:KV + HD * kv + HD] for g in range(TT + TC)],
                out=ob[HD * (h % 2):HD * (h % 2) + HD, h // 2, t * P:(t + 1) * P]))
    attention(nc, k, "gq", units, probs, turned)

    oat = (area(16384, 4, T, F32R), area(18432, 4, T, F32R))
    obt = (area(20480, 4, T, F32R), area(22528, 4, T, F32R))
    split_tiles(nc, k, "so", [(oa, *oat), (ob, *obt)],
                ahead=[column_chunk(a["w_out_a_2"][0], 512 * h, 512) for h in range(AHEAD)])
    z = area(0, TT, D)
    gates = [area(4096, TT, D), area(8192, TT, D)]

    def put_z(branch, c0):
        def put(dve, link, psum, i):
            out = z[:, i, c0:c0 + 512]
            if branch == 0:
                return dve.tensor_tensor(out, psum, gates[0][:, i, c0:c0 + 512], ALU.mult)
            tmp = k.pair[:, i % 2, :]
            link(dve.tensor_tensor(tmp, psum, gates[1][:, i, c0:c0 + 512], ALU.mult))
            return dve.tensor_tensor(out, out, tmp, ALU.add)
        return put

    chunks = [dict(src=column_chunk(a[n][0], c0, 512), uses=[dict(kind="T", u=o, tokens=T, put=put_z(b, c0))])
              for b, (n, o) in enumerate((("w_out_a_2", oat), ("w_out_b_2", obt))) for c0 in (0, 512)]
    project(nc, k, "mg2", chunks, on_dve=True, ahead=AHEAD,
            loads=[(gates[b], k.branch_gates[b].rearrange("(t p) d -> p t d", p=P)) for b in range(2)])
    zt = (area(4096, KD, T, F32R), area(8192, KD, T, F32R))
    y = area(12288, TT, D)
    turn(nc, k, "tz", z, TT, KD, None, None, *zt,
         ahead=[column_chunk(a["w_o_2"][0], 256 * h) for h in range(AHEAD)])
    project(nc, k, "out2", [dict(src=column_chunk(a["w_o_2"][0], 256 * h), uses=[use_t(y, 0, 256 * h, zt, T)])
                            for h in range(D // 256)], ahead=AHEAD)
    normalise(nc, k, "n2y", y, TT, D, k.x, False, 1e-6, gain=a["g_post_mix_2"][0], gate=k.gate_rows[2])


def copy_tiles(nc, k, name, dst, src):
    with stage(nc) as ctx:
        block = ctx.enter_context(nc.Block())

        @block.vector
        def _(dve):
            dve.tensor_copy(dst, src)


def block_two_moe(nc, k, a, out):
    u = moe_inputs(nc, k, "m2", False, 1e-6, k.gate_rows[7], k.gate_rows[6])
    k.route.max_items = 47
    route(nc, k, "r2", u, [(a["w_router_2"][0], a["b_router_2"][0])], 32, 4, 0)
    w_gu = a["w_gu_2"][0]
    m = Experts(width=1024, experts=32, first=[(0, w_gu, 0, 0), (1, w_gu, 1024, 1024)],
                        second=[(2, w_gu, 512, 512), (3, w_gu, 1536, 1536)], down=a["w_dn_2"][0],
                        bias=[a["b_gu_2"][0], a["b_dn_2"][0]], down_bias=2048, swiglu=True, whole=(5,),
                        x=k.xn_dram, y=k.y_dram)
    experts(nc, k, "e2", m)
    combine(nc, k, "c2", 4, k.y_dram)
    f = k.arena[:, 0:TT * D].rearrange("p (t d) -> p t d", t=TT)
    normalise(nc, k, "n2f", f, TT, D, k.x, False, 1e-6, gain=a["g_post_ffn_2"][0], gate=k.gate_rows[3],
              store=[out[0, t * P:(t + 1) * P, :] for t in range(TT)])


def program(nc, a, out):
    with ExitStack() as ctx:
        def sb(name, shape, dtype=F32):
            return ctx.enter_context(nc.sbuf_tensor("sb_" + name, shape, dtype))

        k = Parts()
        def sb_twice(name, shape):
            at = -(-nc.sbuf_base // 32) * 32
            return sb(name, shape), nc.alloc_sbuf_tensor_at(f"sb_{name}_r", shape, F32R, offset=at)

        k.ring, k.ring_lo = sb_twice("ring", [P, SLOTS, CHUNK])
        k.hi_ring = sb("hi_ring", [P, HI_SLOTS, CHUNK], F32R)
        k.x = sb("x", [P, TT, D])
        k.ident, k.ones, k.before, k.causal = (sb(n, [P, P]) for n in ("ident", "ones", "before", "causal"))
        k.neg_sel = sb("neg_sel", [NH, NH, P])
        k.iota, k.token, k.half_row = sb("iota", [P, P]), sb("token", [P, TT]), sb("half_row", [64, 1])
        k.rows = sb("rows", [P, 2, D])
        k.pair = sb("pair", [P, 2, 512])
        k.small = sb("small", [P, 128])
        k.small_hi, k.small_lo = (sb(n, [P, KD, NH], F32R) for n in ("small_hi", "small_lo"))
        k.cols = sb("cols", [P, column_rows(a)[1]])
        k.bias_cols = sb("bias_cols", [P, 2 * NBIAS])
        k.silu = sb("silu", [P, 3 * KD])
        names = ("sh1", "sc1", "gt1", "sh2", "sc2", "gt2", "shc", "scc", "sh1_2", "sc1_2", "gt1_2", "sh2_2", "sc2_2",
                 "gt2_2")
        mods = sb("mods", [P, len(names), KD])
        k.mod = {n: mods[:, i, :] for i, n in enumerate(names)}
        k.arena, k.arena_r = sb_twice("arena", [P, ARENA])
        k.psum = ctx.enter_context(nc.psum_tensor("psum_all", [P, 8, 512], F32))
        k.route = Parts()
        k.route.expert_i, k.route.expert_f = sb("expert_i", [P, 48], I32), sb("expert_f", [P, 48])
        k.route.ids, k.route.dest = sb("ids", [P, 48], I32), sb("dest", [P, 48], I32)
        k.route.last, k.route.weight = sb("last", [P, 1], I32), sb("weight", [P, TT, 4])
        k.branch_gates = nc.dram_tensor("branch_gates", (2, T, D), F32).ap()
        k.rpb_pad = nc.dram_tensor("rpb_pad", (RPB_SIZE,), F32).ap()
        k.xn_dram = nc.dram_tensor("xn_dram", (T, D), F32).ap()
        k.y_dram = nc.dram_tensor("y_dram", (4 * T + P, D), F32).ap()
        k.gate_rows = nc.dram_tensor("gate_rows", (8, D), F32).ap()
        setup(nc, k, a)
        block_one_mixer(nc, k, a)
        block_one_moe(nc, k, a)
        block_two_mixer(nc, k, a)
        block_two_moe(nc, k, a, out)


_INS = ["x", "c", "w_ada", "b_ada", "w_in", "b_f", "conv_w", "conv_b", "w_rg", "b_rg", "w_ig", "b_ig", "lru_lambda",
        "g_attn", "g_lru", "w_out", "ln1_g", "ln1_b", "w_grp", "b_grp", "w_exp", "b_exp", "w_e_gate", "w_e_up",
        "w_e_down", "ln2_g", "ln2_b", "c_2", "ctx_2", "c_ctx_2", "w_mod_2", "b_mod_2", "g_pre_mix_2",
        "g_post_mix_2", "g_pre_ffn_2", "g_post_ffn_2", "w_in_2", "rpb_2", "g_qnorm_2", "g_knorm_2", "w_out_a_2",
        "w_out_b_2", "w_o_2", "w_router_2", "b_router_2", "w_gu_2", "b_gu_2", "w_dn_2", "b_dn_2"]


def kernel(**inputs):
    import numpy as _np
    import concourse.bacc as _bacc
    from concourse.bass_utils import run_bass_kernel_spmd as _run

    nc = _bacc.Bacc("TRN2", target_bir_lowering=False, num_devices=1)
    values = dict({name: inputs[name] for name in _INS}, **constants())
    arrays, aps = {}, {}
    for name, value in values.items():
        value = _np.ascontiguousarray(value)
        arrays[f"in_{name}_dram"] = value
        aps[name] = nc.dram_tensor(f"in_{name}_dram", value.shape, mybir.dt.from_np(value.dtype),
                                   kind="ExternalInput").ap()
    out = nc.dram_tensor("out_0_dram", (1, T, D), F32, kind="ExternalOutput").ap()
    program(nc, aps, out)
    result = _run(nc, [arrays], core_ids=[0])
    return result.results[0]["out_0_dram"]
```
